# Optimizing a Trainium2 kernel written in Bass

```python
import math
import jax
import jax.numpy as jnp
from jax import lax
import numpy as np

D_MODEL = 1024
BATCH = 1
SEQ = 1024
DEPTH = 1

GRID_W = 64
CTX_LEN = 256
RMS_EPS = 1e-6

SSD_HEADS = 6
SSD_HEAD_DIM = 64
SSD_WIDTH = SSD_HEADS * SSD_HEAD_DIM
SSD_GROUPS = 2
SSD_STATE = 128
SSD_CONV = 5
SSD_CHUNK = 128
SSD_XBC = SSD_WIDTH + 2 * SSD_GROUPS * SSD_STATE

NA_HEADS = 6
NA_HEAD_DIM = 64
NA_WIDTH = NA_HEADS * NA_HEAD_DIM
NA_ROWS = 8
NA_COLS = 16

HY_WIDTH = 256
HY_SHORT = 3
HY_EMB = 33
HY_BANDS = (HY_EMB - 1) // 2
HY_HIDDEN = 64
HY_FAST_DECAY = 0.3
HY_SLOW_DECAY = 1.5
HY_DECAY_TARGET = 1e-2

D_MIX = SSD_WIDTH + NA_WIDTH + HY_WIDTH

OFF_Z = 0
OFF_XBC = OFF_Z + SSD_WIDTH
OFF_DT = OFF_XBC + SSD_XBC
OFF_Q = OFF_DT + 2 * SSD_HEADS
OFF_K = OFF_Q + NA_WIDTH
OFF_V = OFF_K + NA_WIDTH
OFF_HY = OFF_V + NA_WIDTH
IN_COLS = OFF_HY + 3 * HY_WIDTH

N_EXPERTS = 32
TOP_K = 4
D_EXPERT = 1024
SWIGLU_LIMIT = 7.0
SWIGLU_ALPHA = 1.702
MOE_BLOCK = 128

kernel_name = "hybrid_ssd_natten_hyena_moe_dit"

F32 = jnp.float32

def rms_norm(x, g):
    xf = x.astype(F32)
    y = xf * lax.rsqrt(jnp.mean(xf * xf, axis=-1, keepdims=True) + RMS_EPS)
    return (y * g.astype(F32)).astype(x.dtype)

def dw_conv(u, w, b):
    k = w.shape[0]
    out = lax.conv_general_dilated(
        u, w[:, None, :].astype(u.dtype), window_strides=(1,), padding=[(k // 2, k // 2)],
        dimension_numbers=("NWC", "WIO", "NWC"), feature_group_count=u.shape[-1])
    return out + b.astype(u.dtype)

def ssd_scan(xs, dt, a, bm, cm, init, with_output):
    b, l, h, p = xs.shape
    g, n = bm.shape[2], bm.shape[3]
    q = SSD_CHUNK
    nc = l // q
    rep = h // g
    bh = jnp.repeat(bm.astype(F32), rep, axis=2).reshape(b, nc, q, h, n)
    xdt = (xs.astype(F32) * dt[..., None]).reshape(b, nc, q, h, p)
    a_cs = jnp.cumsum((dt * a).reshape(b, nc, q, h), axis=2)
    a_last = a_cs[:, :, -1]
    states = jnp.einsum("bcjhn,bcjh,bcjhp->bchpn", bh, jnp.exp(a_last[:, :, None] - a_cs), xdt)

    def carry_chunk(s, inp):
        st, dec = inp
        return s * dec[..., None, None] + st, s

    final, s_start = lax.scan(carry_chunk, init,
                              (jnp.moveaxis(states, 1, 0), jnp.moveaxis(jnp.exp(a_last), 1, 0)))
    if not with_output:
        return None, final
    ch = jnp.repeat(cm.astype(F32), rep, axis=2).reshape(b, nc, q, h, n)
    tri = jnp.tril(jnp.ones((q, q), dtype=bool))[:, :, None]
    seg = a_cs[:, :, :, None, :] - a_cs[:, :, None, :, :]
    decay = jnp.exp(jnp.where(tri, seg, -jnp.inf))
    scores = jnp.einsum("bcihn,bcjhn->bcijh", ch, bh) * decay
    y = (jnp.einsum("bcijh,bcjhp->bcihp", scores, xdt)
         + jnp.einsum("bcihn,bchpn,bcih->bcihp", ch, jnp.moveaxis(s_start, 0, 1), jnp.exp(a_cs)))
    return y.reshape(b, l, h, p), final

def ssd_prepare(p, conv_w, conv_b):
    b, l, _ = p.shape
    z = p[..., OFF_Z:OFF_XBC]
    xbc = jax.nn.silu(dw_conv(p[..., OFF_XBC:OFF_DT], conv_w, conv_b))
    gn = SSD_GROUPS * SSD_STATE
    xs = xbc[..., :SSD_WIDTH].reshape(b, l, SSD_HEADS, SSD_HEAD_DIM)
    bm = xbc[..., SSD_WIDTH:SSD_WIDTH + gn].reshape(b, l, SSD_GROUPS, SSD_STATE)
    cm = xbc[..., SSD_WIDTH + gn:].reshape(b, l, SSD_GROUPS, SSD_STATE)
    dt_raw = p[..., OFF_DT:OFF_Q].astype(F32).reshape(b, l, 2, SSD_HEADS)
    return z, xs, bm, cm, dt_raw

def ssd_direction(xs, bm, cm, dt_raw, a_log, dt_bias, direction, init, with_output):
    dt = jax.nn.softplus(dt_raw[:, :, direction] + dt_bias[direction].astype(F32))
    a = -jnp.exp(a_log[direction].astype(F32))
    if direction == 1:
        xs, bm, cm, dt = xs[:, ::-1], bm[:, ::-1], cm[:, ::-1], dt[:, ::-1]
    y, final = ssd_scan(xs, dt, a, bm, cm, init, with_output)
    if direction == 1 and y is not None:
        y = y[:, ::-1]
    return y, final

def ssd_output(y_sum, xs, z, d_skip, norm_g):
    b, l = xs.shape[:2]
    gsz = SSD_WIDTH // SSD_GROUPS
    y = (y_sum + d_skip.astype(F32)[:, None] * xs.astype(F32)).reshape(b, l, SSD_GROUPS, gsz)
    gated = y * jax.nn.silu(z.astype(F32)).reshape(b, l, SSD_GROUPS, gsz)
    gated = gated * lax.rsqrt(jnp.mean(gated * gated, axis=-1, keepdims=True) + RMS_EPS)
    return (gated.reshape(b, l, SSD_WIDTH) * norm_g.astype(F32)).astype(z.dtype)

def ssd_mixer(p_lat, p_ctx, conv_w, conv_b, a_log, dt_bias, d_skip, norm_g, ctx_out):
    z_c, x_c, b_c, c_c, dt_c = ssd_prepare(p_ctx, conv_w, conv_b)
    z_l, x_l, b_l, c_l, dt_l = ssd_prepare(p_lat, conv_w, conv_b)
    init = jnp.zeros((p_ctx.shape[0], SSD_HEADS, SSD_HEAD_DIM, SSD_STATE), F32)
    y_lat, y_ctx = [], []
    for direction in (0, 1):
        yc, s_ctx = ssd_direction(x_c, b_c, c_c, dt_c, a_log, dt_bias, direction, init, ctx_out)
        yl, _ = ssd_direction(x_l, b_l, c_l, dt_l, a_log, dt_bias, direction, s_ctx, True)
        y_lat.append(yl)
        y_ctx.append(yc)
    out_lat = ssd_output(y_lat[0] + y_lat[1], x_l, z_l, d_skip, norm_g)
    out_ctx = ssd_output(y_ctx[0] + y_ctx[1], x_c, z_c, d_skip, norm_g) if ctx_out else None
    return out_lat, out_ctx

def na_mixer(p_lat, p_ctx, rpb, ctx_out):
    b, l, _ = p_lat.shape
    rows = l // GRID_W
    kh = min(NA_ROWS, rows)
    scale = NA_HEAD_DIM ** -0.5

    def heads(p, off):
        return p[..., off:off + NA_WIDTH].reshape(p.shape[0], p.shape[1], NA_HEADS, NA_HEAD_DIM)

    q_grid = heads(p_lat, OFF_Q).reshape(b, rows, GRID_W, NA_HEADS, NA_HEAD_DIM)
    k_grid = heads(p_lat, OFF_K).reshape(b, rows, GRID_W, NA_HEADS, NA_HEAD_DIM)
    v_grid = heads(p_lat, OFF_V).reshape(b, rows, GRID_W, NA_HEADS, NA_HEAD_DIM)
    k_ctx, v_ctx = heads(p_ctx, OFF_K), heads(p_ctx, OFF_V)

    col = jnp.arange(GRID_W)
    col_start = jnp.clip(col - NA_COLS // 2, 0, GRID_W - NA_COLS)
    col_ok = (col[None, :] >= col_start[:, None]) & (col[None, :] < col_start[:, None] + NA_COLS)
    dc = jnp.clip(col[None, :] - col[:, None] + NA_COLS - 1, 0, 2 * NA_COLS - 2)
    bias_tab = rpb.astype(F32)

    def query_row(args):
        q_row, r = args
        r0 = jnp.clip(r - kh // 2, 0, rows - kh)
        k_blk = lax.dynamic_slice_in_dim(k_grid, r0, kh, axis=1)
        v_blk = lax.dynamic_slice_in_dim(v_grid, r0, kh, axis=1)
        dr = r0 + jnp.arange(kh) - r + NA_ROWS - 1
        bias = bias_tab[dr[None, :, None], dc[:, None, :]]
        s_loc = jnp.einsum("bqhd,bkwhd->bqkwh", q_row, k_blk, preferred_element_type=F32) * scale + bias
        s_loc = jnp.where(col_ok[None, :, None, :, None], s_loc, -jnp.inf)
        s_loc = s_loc.reshape(b, GRID_W, kh * GRID_W, NA_HEADS)
        s_ctx = jnp.einsum("bqhd,bchd->bqch", q_row, k_ctx, preferred_element_type=F32) * scale
        prob = jax.nn.softmax(jnp.concatenate([s_loc, s_ctx], axis=2), axis=2).astype(v_grid.dtype)
        p_loc = prob[:, :, :kh * GRID_W].reshape(b, GRID_W, kh, GRID_W, NA_HEADS)
        return (jnp.einsum("bqkwh,bkwhd->bqhd", p_loc, v_blk)
                + jnp.einsum("bqch,bchd->bqhd", prob[:, :, kh * GRID_W:], v_ctx))

    o = lax.map(query_row, (jnp.moveaxis(q_grid, 1, 0), jnp.arange(rows)))
    y_lat = jnp.moveaxis(o, 0, 1).reshape(b, l, NA_WIDTH)
    if not ctx_out:
        return y_lat, None
    q_ctx = heads(p_ctx, OFF_Q)
    s = jnp.einsum("bqhd,bkhd->bhqk", q_ctx, k_ctx, preferred_element_type=F32) * scale
    o_ctx = jnp.einsum("bhqk,bkhd->bqhd", jax.nn.softmax(s, axis=-1).astype(v_ctx.dtype), v_ctx)
    return y_lat, o_ctx.reshape(b, p_ctx.shape[1], NA_WIDTH)

def hyena_filters(length, w1, b1, w2, b2, w3, freq):
    t = jnp.linspace(0.0, 1.0, length, dtype=F32)[:, None]
    w = 2.0 * math.pi * jnp.arange(length, dtype=F32)[:, None] / length
    f = jnp.linspace(1e-4, HY_BANDS - 1, HY_BANDS, dtype=F32)[None, :]
    z = jnp.concatenate([t, jnp.cos(f * w), -jnp.sin(f * w)], axis=1)
    freq = freq.astype(F32)
    h = jnp.sin(freq[0] * (z @ w1.astype(F32) + b1.astype(F32)))
    h = jnp.sin(freq[1] * (h @ w2.astype(F32) + b2.astype(F32)))
    h = (h @ w3.astype(F32)).reshape(length, 2, HY_WIDTH)
    max_decay = math.log(HY_DECAY_TARGET) / HY_FAST_DECAY
    min_decay = math.log(HY_DECAY_TARGET) / HY_SLOW_DECAY
    deltas = jnp.abs(jnp.linspace(min_decay, max_decay, HY_WIDTH, dtype=F32))
    h = h * jnp.exp(-t[:, :, None] * deltas)
    h = h / jnp.sum(jnp.abs(h), axis=(0, 1), keepdims=True)
    return h[:, 0], h[:, 1]

def long_conv(u, h_fwd, h_bwd, d_bias):
    b, l, ch = u.shape
    k = jnp.concatenate([h_fwd, jnp.zeros((1, ch), F32), h_bwd[:0:-1]], axis=0)
    uf = u.astype(F32)
    y = jnp.fft.irfft(jnp.fft.rfft(uf, n=2 * l, axis=1) * jnp.fft.rfft(k, axis=0)[None], n=2 * l, axis=1)[:, :l]
    return (y + uf * d_bias.astype(F32)).astype(u.dtype)

def hyena_mixer(p, conv_w, conv_b, f_w1, f_b1, f_w2, f_b2, f_w3, freq, d_bias):
    uc = dw_conv(p[..., OFF_HY:IN_COLS], conv_w, conv_b)
    x0, x1, v = jnp.split(uc, 3, axis=-1)
    h_fwd, h_bwd = hyena_filters(p.shape[1], f_w1, f_b1, f_w2, f_b2, f_w3, freq)
    return x0 * long_conv(v * x1, h_fwd, h_bwd, d_bias)

def moe_ffn(h, w_router, b_router, w_gate_up, b_gate_up, w_down, b_down):
    t, d = h.shape
    logits = (h @ w_router + b_router).astype(F32)
    top_logit, top_idx = lax.top_k(logits, TOP_K)
    gate_w = jax.nn.softmax(top_logit, axis=-1)
    n = t * TOP_K
    flat_e = top_idx.reshape(n)
    order = jnp.argsort(flat_e)
    sorted_e = flat_e[order]
    counts = jnp.bincount(flat_e, length=N_EXPERTS)
    padded = (counts + MOE_BLOCK - 1) // MOE_BLOCK * MOE_BLOCK
    pad_end = jnp.cumsum(padded)
    pad_start = pad_end - padded
    start = jnp.cumsum(counts) - counts
    dest = pad_start[sorted_e] + jnp.arange(n) - start[sorted_e]
    n_blocks = (n + N_EXPERTS * (MOE_BLOCK - 1) + MOE_BLOCK - 1) // MOE_BLOCK
    n_rows = n_blocks * MOE_BLOCK
    row_tok = jnp.full((n_rows,), t, jnp.int32).at[dest].set((order // TOP_K).astype(jnp.int32))
    row_w = jnp.zeros((n_rows,), F32).at[dest].set(gate_w.reshape(n)[order])
    block_e = jnp.minimum(jnp.searchsorted(pad_end, jnp.arange(n_blocks) * MOE_BLOCK, side="right"),
                          N_EXPERTS - 1)
    h_pad = jnp.concatenate([h, jnp.zeros((1, d), h.dtype)], axis=0)
    xb = h_pad[row_tok].reshape(n_blocks, MOE_BLOCK, d)

    def expert_block(args):
        xblk, e = args
        gu = xblk @ w_gate_up[e] + b_gate_up[e]
        gate, up = jnp.split(gu, 2, axis=-1)
        gate = jnp.minimum(gate, SWIGLU_LIMIT)
        up = jnp.clip(up, -SWIGLU_LIMIT, SWIGLU_LIMIT)
        act = gate * jax.nn.sigmoid(SWIGLU_ALPHA * gate) * (up + 1.0)
        return act @ w_down[e] + b_down[e]

    yb = lax.map(expert_block, (xb, block_e)).reshape(n_rows, d)
    y = jax.ops.segment_sum(yb * row_w[:, None].astype(yb.dtype), row_tok, num_segments=t + 1)
    return y[:t]

def trunk_layer(x, ctx, c, c_ctx, lp, last):
    b, l, d = x.shape
    mod = jax.nn.silu(c) @ lp["w_mod"] + lp["b_mod"]
    mod_c = jax.nn.silu(c_ctx) @ lp["w_mod"] + lp["b_mod"]
    sh1, sc1, g1, sh2, sc2, g2 = jnp.split(mod[:, None, :], 6, axis=-1)
    sh1c, sc1c, g1c, sh2c, sc2c, g2c = jnp.split(mod_c, 6)
    gains = lp["norm_g"]

    h = rms_norm(x, gains[0]) * (1.0 + sc1) + sh1
    hc = rms_norm(ctx, gains[0]) * (1.0 + sc1c) + sh1c
    p = h @ lp["w_in"]
    pc = hc @ lp["w_in"]
    ctx_out = not last
    y_ssd, y_ssd_c = ssd_mixer(p, pc, lp["ssd_conv_w"], lp["ssd_conv_b"], lp["ssd_a_log"],
                               lp["ssd_dt_bias"], lp["ssd_d"], lp["ssd_norm_g"], ctx_out)
    y_na, y_na_c = na_mixer(p, pc, lp["na_rpb"], ctx_out)
    hy_args = (lp["hy_conv_w"], lp["hy_conv_b"], lp["hy_f_w1"], lp["hy_f_b1"], lp["hy_f_w2"],
               lp["hy_f_b2"], lp["hy_f_w3"], lp["hy_freq"], lp["hy_d"])
    y_hy = hyena_mixer(p, *hy_args)
    mix = jnp.concatenate([y_ssd, y_na, y_hy], axis=-1) @ lp["w_out"]
    x = x + g1 * rms_norm(mix, gains[1])
    h2 = rms_norm(x, gains[2]) * (1.0 + sc2) + sh2
    moe_args = (lp["w_router"], lp["b_router"], lp["w_gate_up"], lp["b_gate_up"], lp["w_down"], lp["b_down"])

    if last:
        f = moe_ffn(h2.reshape(b * l, d), *moe_args).reshape(b, l, d)
        return x + g2 * rms_norm(f, gains[3]), None

    y_hy_c = hyena_mixer(pc, *hy_args)
    mix_c = jnp.concatenate([y_ssd_c, y_na_c, y_hy_c], axis=-1) @ lp["w_out"]
    ctx = ctx + g1c * rms_norm(mix_c, gains[1])
    h2c = rms_norm(ctx, gains[2]) * (1.0 + sc2c) + sh2c
    lc = ctx.shape[1]
    f = moe_ffn(jnp.concatenate([h2.reshape(b * l, d), h2c.reshape(b * lc, d)], axis=0), *moe_args)
    x = x + g2 * rms_norm(f[:b * l].reshape(b, l, d), gains[3])
    ctx = ctx + g2c * rms_norm(f[b * l:].reshape(b, lc, d), gains[3])
    return x, ctx

def setup_inputs(seed: int = 0) -> dict:
    key = jax.random.key(seed)
    ks = jax.random.split(key, 32)

    def nrm(i, shape, scale):
        return jax.random.normal(ks[i], shape, F32) * scale

    x = nrm(0, (BATCH, SEQ, D_MODEL), 1.0)
    c = nrm(1, (BATCH, D_MODEL), 1.0)
    ctx = nrm(2, (BATCH, CTX_LEN, D_MODEL), 1.0)
    c_ctx = nrm(3, (D_MODEL,), 1.0)
    w_mod = nrm(4, (DEPTH, D_MODEL, 6 * D_MODEL), 0.5 * D_MODEL ** -0.5)
    b_mod = nrm(5, (DEPTH, 6 * D_MODEL), 0.02)
    norm_g = 1.0 + nrm(6, (DEPTH, 4, D_MODEL), 0.05)
    w_in = nrm(7, (DEPTH, D_MODEL, IN_COLS), D_MODEL ** -0.5)
    ssd_conv_w = nrm(8, (DEPTH, SSD_CONV, SSD_XBC), SSD_CONV ** -0.5)
    ssd_conv_b = nrm(9, (DEPTH, SSD_XBC), 0.01)
    ssd_a_log = jnp.log(jax.random.uniform(ks[10], (DEPTH, 2, SSD_HEADS), F32, 1.0, 16.0))
    dt0 = jnp.exp(jax.random.uniform(ks[11], (DEPTH, 2, SSD_HEADS), F32, math.log(1e-3), math.log(1e-1)))
    ssd_dt_bias = dt0 + jnp.log(-jnp.expm1(-dt0))
    ssd_d = 1.0 + nrm(12, (DEPTH, SSD_HEADS), 0.1)
    ssd_norm_g = 1.0 + nrm(13, (DEPTH, SSD_WIDTH), 0.05)
    na_rpb = nrm(14, (DEPTH, 2 * NA_ROWS - 1, 2 * NA_COLS - 1, NA_HEADS), 0.1)
    hy_conv_w = nrm(15, (DEPTH, HY_SHORT, 3 * HY_WIDTH), HY_SHORT ** -0.5)
    hy_conv_b = nrm(16, (DEPTH, 3 * HY_WIDTH), 0.01)
    hy_f_w1 = nrm(17, (DEPTH, HY_EMB, HY_HIDDEN), HY_EMB ** -0.5)
    hy_f_b1 = nrm(18, (DEPTH, HY_HIDDEN), 0.1)
    hy_f_w2 = nrm(19, (DEPTH, HY_HIDDEN, HY_HIDDEN), HY_HIDDEN ** -0.5)
    hy_f_b2 = nrm(20, (DEPTH, HY_HIDDEN), 0.1)
    hy_f_w3 = nrm(21, (DEPTH, HY_HIDDEN, 2 * HY_WIDTH), HY_HIDDEN ** -0.5)
    hy_freq = 1.0 + nrm(22, (DEPTH, 2, HY_HIDDEN), 0.1)
    hy_d = nrm(23, (DEPTH, HY_WIDTH), 0.5)
    w_out = nrm(24, (DEPTH, D_MIX, D_MODEL), D_MIX ** -0.5)
    w_router = nrm(25, (DEPTH, D_MODEL, N_EXPERTS), D_MODEL ** -0.5)
    b_router = nrm(26, (DEPTH, N_EXPERTS), 0.01)
    w_gate_up = nrm(27, (DEPTH, N_EXPERTS, D_MODEL, 2 * D_EXPERT), D_MODEL ** -0.5)
    b_gate_up = nrm(28, (DEPTH, N_EXPERTS, 2 * D_EXPERT), 0.01)
    w_down = nrm(29, (DEPTH, N_EXPERTS, D_EXPERT, D_MODEL), D_EXPERT ** -0.5)
    b_down = nrm(30, (DEPTH, N_EXPERTS, D_MODEL), 0.01)
    return {"x": x, "c": c, "ctx": ctx, "c_ctx": c_ctx, "w_mod": w_mod, "b_mod": b_mod,
            "norm_g": norm_g, "w_in": w_in, "ssd_conv_w": ssd_conv_w, "ssd_conv_b": ssd_conv_b,
            "ssd_a_log": ssd_a_log, "ssd_dt_bias": ssd_dt_bias, "ssd_d": ssd_d, "ssd_norm_g": ssd_norm_g,
            "na_rpb": na_rpb, "hy_conv_w": hy_conv_w, "hy_conv_b": hy_conv_b, "hy_f_w1": hy_f_w1,
            "hy_f_b1": hy_f_b1, "hy_f_w2": hy_f_w2, "hy_f_b2": hy_f_b2, "hy_f_w3": hy_f_w3,
            "hy_freq": hy_freq, "hy_d": hy_d, "w_out": w_out, "w_router": w_router, "b_router": b_router,
            "w_gate_up": w_gate_up, "b_gate_up": b_gate_up, "w_down": w_down, "b_down": b_down}

def reference(x, c, ctx, c_ctx, w_mod, b_mod, norm_g, w_in, ssd_conv_w, ssd_conv_b, ssd_a_log,
              ssd_dt_bias, ssd_d, ssd_norm_g, na_rpb, hy_conv_w, hy_conv_b, hy_f_w1, hy_f_b1,
              hy_f_w2, hy_f_b2, hy_f_w3, hy_freq, hy_d, w_out, w_router, b_router, w_gate_up,
              b_gate_up, w_down, b_down):
    for i in range(DEPTH):
        lp = {"w_mod": w_mod[i], "b_mod": b_mod[i], "norm_g": norm_g[i], "w_in": w_in[i],
              "ssd_conv_w": ssd_conv_w[i], "ssd_conv_b": ssd_conv_b[i], "ssd_a_log": ssd_a_log[i],
              "ssd_dt_bias": ssd_dt_bias[i], "ssd_d": ssd_d[i], "ssd_norm_g": ssd_norm_g[i],
              "na_rpb": na_rpb[i], "hy_conv_w": hy_conv_w[i], "hy_conv_b": hy_conv_b[i],
              "hy_f_w1": hy_f_w1[i], "hy_f_b1": hy_f_b1[i], "hy_f_w2": hy_f_w2[i], "hy_f_b2": hy_f_b2[i],
              "hy_f_w3": hy_f_w3[i], "hy_freq": hy_freq[i], "hy_d": hy_d[i], "w_out": w_out[i],
              "w_router": w_router[i], "b_router": b_router[i], "w_gate_up": w_gate_up[i],
              "b_gate_up": b_gate_up[i], "w_down": w_down[i], "b_down": b_down[i]}
        x, ctx = trunk_layer(x, ctx, c, c_ctx, lp, i == DEPTH - 1)
    return x


_drawn_inputs = setup_inputs


def setup_inputs(seed=0):
    import zlib

    import numpy as np

    out = dict(_drawn_inputs(seed))
    spreads = {}
    factors = {'ssd_conv_b': 4.756,
     'ssd_d': 2.856,
     'na_rpb': 7.797,
     'hy_conv_b': 6.364,
     'hy_f_b1': 4.302,
     'hy_f_b2': 4.088,
     'hy_freq': 7.5,
     'b_router': 2.901,
     'b_gate_up': 8.0,
     'b_down': 8.0}
    for name, (base, spread) in spreads.items():
        noise = np.random.default_rng([zlib.crc32(name.encode()), seed]).standard_normal(out[name].shape)
        drawn = base * np.exp(spread * noise) if base else spread * noise
        out[name] = jnp.asarray(drawn.astype(out[name].dtype))
    for name, factor in factors.items():
        out[name] = (out[name] * factor).astype(out[name].dtype)
    return out
```

```python
import numpy as np
import concourse.bass as bass
from concourse import mybir
from contextlib import ExitStack


F32 = mybir.dt.float32
I32 = mybir.dt.int32
U32 = mybir.dt.uint32
ALU = mybir.AluOpType
ACT = mybir.ActivationFunctionType
AXX = mybir.AxisListType.X

P = 128
D = 1024
T = 1024
TC = 256
TA = T + TC
KD = D // P
NT, NTC = T // P, TC // P
EPS = 1e-6
SSD_H, HD, NGRP, NST, SSD_W = 6, 64, 2, 128, 384
GW = SSD_W // NGRP
XBC = SSD_W + 2 * NGRP * NST
NA_W, HY_W = 384, 256
OFF_XBC = SSD_W
OFF_DT = OFF_XBC + XBC
OFF_Q = OFF_DT + 2 * SSD_H
OFF_K, OFF_V = OFF_Q + NA_W, OFF_Q + 2 * NA_W
OFF_HY = OFF_V + NA_W
NXT, NQT, NHT = XBC // P, NA_W // P, 3 * HY_W // P
NXT_CTX = (SSD_W + NGRP * NST) // P
SSD_K, HY_K = 5, 3
NE, TOPK, DE = 32, 4, 1024
LIMIT, ALPHA = 7.0, 1.702


class Kit:

    def __init__(self, nc, top):
        self.nc, self.top, self.sems = nc, top, []

    def sem(self, name):
        self.sems.append(self.nc.alloc_semaphore(name=name))
        return self.sems[-1]

    def recycle(self):
        self.nc.clear_and_free_semaphores(self.sems)
        self.nc.all_engine_barrier()
        self.sems = []

    def sb(self, scope, name, shape, dt=F32):
        return scope.enter_context(self.nc.sbuf_tensor("sb_" + name, shape, dt))

    def ps(self, scope, name, shape):
        return scope.enter_context(self.nc.psum_tensor(name, shape, F32))


def linked(eng, sem):
    n = [0]

    def link(ins):
        n[0] += 1
        ins.then_inc(sem, 1)
        eng.wait_ge(sem, n[0])

    return link


def phase_project(nc, kit, keep, io):
    scope = ExitStack()
    with scope:
        hT = keep["hT"]
        ring = kit.sb(scope, "w_ring", [P, 4, KD, 2 * P])
        wtok = kit.sb(scope, "w_tok", [P, KD, NA_W + 2 * SSD_H])
        rstd = kit.sb(scope, "rstd", [P, TA])
        ccol = kit.sb(scope, "c_col", [P, KD, 2])
        scol = kit.sb(scope, "silu_c_col", [P, KD, 2])
        bmod = kit.sb(scope, "b_mod_col", [P, 6 * KD])
        gcol = kit.sb(scope, "gain0_col", [P, KD])
        amul = kit.sb(scope, "norm_scale_col", [P, KD, 2])
        cw = kit.sb(scope, "ssd_conv_col", [P, NXT, SSD_K + 1])
        hw = kit.sb(scope, "hy_conv_col", [P, NHT, HY_K + 1])
        ones = kit.sb(scope, "ones_a", [P, P])
        eps = kit.sb(scope, "eps_a", [P, 1])
        modT, xbcT, qT, kT, hyT = keep["modT"], keep["xbcT"], keep["qT"], keep["kT"], keep["hyT"]
        v, z, dt = keep["v"], keep["z"], keep["dt"]
        acc = [kit.ps(scope, f"acc{i}", [P, 1536]) for i in range(2)]
        pmod = kit.ps(scope, "pmod", [P, 512])

        small_in = kit.sem("a_small_in")
        x_in = [kit.sem(f"a_x_in{k}") for k in range(KD)]
        ring_in = [kit.sem(f"a_ring_in{i}") for i in range(4)]
        ring_used = kit.sem("a_ring_used")
        wtok_in = kit.sem("a_wtok_in")
        consts = kit.sem("a_consts")
        silu_done = kit.sem("a_silu_done")
        sq_done = kit.sem("a_sq_done")
        sq_used = kit.sem("a_sq_used")
        ssq_done = kit.sem("a_ssq_done")
        std_done = kit.sem("a_std_done")
        h_done = kit.sem("a_h_done")
        tile_done = kit.sem("a_tile_done")
        tile_convolved = kit.sem("a_tile_convolved")
        tile_copied = kit.sem("a_tile_copied")
        conv_done = kit.sem("a_conv_done")
        silu_x = kit.sem("a_silu_x")
        vec = kit.sem("a_vec")

        n_mod1 = 2 * KD // 2
        n_mod = 6 * KD // 2
        chan = [("x", m, OFF_XBC + m * P) for m in range(NXT)]
        chan += [("h", m, OFF_HY + m * P) for m in range(NHT)]
        chan += [("q", m, OFF_Q + m * P) for m in range(NQT)] + [("k", m, OFF_K + m * P) for m in range(NQT)]
        loads = [("mod", m) for m in range(n_mod1)] + [("in", c) for c in range(len(chan))]
        loads += [("mod", m) for m in range(n_mod1, n_mod)]
        tok = [("v", t) for t in range(NT + NTC)] + [("z", t) for t in range(NT + NTC)]
        wmod = io["w_mod"].rearrange("(k p) n -> p k n", p=P)
        win = io["w_in"].rearrange("(k p) n -> p k n", p=P)

        n_conv = NXT + NHT

        def accumulator_free(pe, n):
            if n - 2 >= n_conv:
                pe.wait_ge(tile_copied, n - 2 - n_conv + 1)
            elif n >= 2:
                pe.wait_ge(tile_convolved, n - 1)

        def has_ctx(c):
            kind, m, _ = chan[c]
            return kind == "k" or (kind == "x" and m < NXT_CTX)

        block = scope.enter_context(nc.Block())

        @block.sync
        def _(sp):
            sp.dma_start(ccol[:, :, :], io["c_col"]).then_inc(small_in, 16)
            sp.dma_start(bmod[:, :], io["b_mod_col"]).then_inc(small_in, 16)
            sp.dma_start(gcol[:, :], io["gain0_col"]).then_inc(small_in, 16)
            sp.dma_start(cw[:, :, :], io["ssd_conv_col"]).then_inc(small_in, 16)
            sp.dma_start(hw[:, :, :], io["hy_conv_col"]).then_inc(small_in, 16)
            for n, (kind, m) in enumerate(loads):
                if n >= 4:
                    sp.wait_ge(ring_used, n - 3)
                if kind == "mod":
                    sp.dma_start(ring[:, n % 4, :, :], wmod[:, :, 2 * P * m:2 * P * (m + 1)]).then_inc(ring_in[n % 4], 16)
                else:
                    off = chan[m][2]
                    sp.dma_start(ring[:, n % 4, :, 0:P], win[:, :, off:off + P]).then_inc(ring_in[n % 4], 16)
                if n == 3:
                    for k in range(KD):
                        sp.dma_start(hT[:, k, 0:T], io["x_t"][k * P:(k + 1) * P, :]).then_inc(x_in[k], 16)
                        sp.dma_start(hT[:, k, T:TA], io["ctx_t"][k * P:(k + 1) * P, :]).then_inc(x_in[k], 16)
                    sp.dma_start(wtok[:, :, 0:NA_W], win[:, :, OFF_V:OFF_V + NA_W]).then_inc(wtok_in, 16)
            sp.wait_ge(tile_done, NT + NTC)
            sp.dma_start(wtok[:, :, 0:SSD_W], win[:, :, 0:SSD_W]).then_inc(wtok_in, 16)
            sp.dma_start(wtok[:, :, SSD_W:], win[:, :, OFF_DT:OFF_Q]).then_inc(wtok_in, 16)

        @block.gpsimd
        def _(pool):
            nc.gpsimd.memset(ones[:, :], 1.0).then_inc(consts, 1)
            nc.gpsimd.memset(eps[:, :], EPS).then_inc(consts, 1)

        @block.tensor
        def _(pe):
            n = 0

            def mod_tiles(n, m):
                for h in range(2):
                    for k in range(KD):
                        last = nc.tensor.matmul(pmod[:, 2 * (2 * m + h):2 * (2 * m + h) + 2], ring[:, n % 4, k, h * P:(h + 1) * P],
                                                scol[:, k, :], start=(k == 0), stop=(k == KD - 1))
                last.then_inc(ring_used, 1)
                return last

            pe.wait_ge(silu_done, 1)
            used = [0, 0, 0, 0]
            tiles = 0
            for n, (kind, m) in enumerate(loads):
                used[n % 4] += 16
                pe.wait_ge(ring_in[n % 4], used[n % 4])
                if kind == "mod":
                    mod_tiles(n, m)
                    if m == n_mod1 - 1:
                        pe.wait_ge(consts, 2)
                        for k in range(KD):
                            pe.wait_ge(sq_done, k + 1)
                            for a, b in ((0, 512), (512, 1024), (1024, TA)):
                                last = nc.tensor.matmul(acc[0][:, a:b], ones[:, :], xbcT[:, k % 4, a:b],
                                                        start=(k == 0), stop=(k == KD - 1), skip_group_check=True)
                            last.then_inc(sq_used, 1)
                else:
                    if tiles == 0:
                        pe.wait_ge(h_done, 2 * KD)
                    accumulator_free(pe, tiles)
                    a = acc[tiles % 2]
                    for k in range(KD):
                        lhs = ring[:, n % 4, k, 0:P]
                        for lo, hi in ((0, 512), (512, 1024)) + (((1024, TA),) if has_ctx(m) else ()):
                            last = nc.tensor.matmul(a[:, lo:hi], lhs, hT[:, k, lo:hi], start=(k == 0), stop=(k == KD - 1),
                                                    skip_group_check=True)
                    last.then_inc(ring_used, 1)
                    tiles += 1
            for i, (kind, t) in enumerate(tok):
                if i == 0:
                    pe.wait_ge(wtok_in, 16)
                if kind == "z" and t == 0:
                    pe.wait_ge(wtok_in, 48)
                accumulator_free(pe, tiles)
                a = acc[tiles % 2]
                lo, hi = (0, NA_W) if kind == "v" else (0 if t < NT else SSD_W, NA_W + 2 * SSD_H)
                for k in range(KD):
                    last = nc.tensor.matmul(a[:, lo:hi], hT[:, k, t * P:(t + 1) * P], wtok[:, k, lo:hi],
                                            start=(k == 0), stop=(k == KD - 1))
                last.then_inc(tile_done, 1)
                tiles += 1

        n_before = n_mod1

        @block.scalar
        def _(act):
            act.wait_ge(small_in, 80)
            nc.scalar.activation(scol[:, :, :], ccol[:, :, :], ACT.Silu).then_inc(silu_done, 1)
            for k in range(KD):
                act.wait_ge(x_in[k], 32)
                if k >= 4:
                    act.wait_ge(sq_used, k - 3)
                nc.scalar.activation(xbcT[:, k % 4, :], hT[:, k, :], ACT.Square).then_inc(sq_done, 1)
            act.wait_ge(sq_used, KD)
            act.wait_ge(consts, 2)
            nc.scalar.activation(rstd[:, :], acc[0][:, 0:TA], ACT.Sqrt, bias=eps[:, 0:1], scale=1.0 / D).then_inc(std_done, 1)
            for c, (kind, m, _) in enumerate(chan):
                if kind == "x":
                    act.wait_ge(conv_done, m + 1)
                    hi = TA if has_ctx(c) else T
                    nc.scalar.activation(xbcT[:, m, 0:hi], xbcT[:, m, 0:hi], ACT.Silu).then_inc(silu_x, 1)
                elif kind in "qk":
                    act.wait_ge(ring_used, n_before + c + 1)
                    dst = qT[:, m, :] if kind == "q" else kT[:, m, :]
                    nc.scalar.copy(dst, acc[c % 2][:, 0:(T if kind == "q" else TA)]).then_inc(tile_copied, 1)
            for i, (kind, t) in enumerate(tok):
                a = acc[(len(chan) + i) % 2]
                act.wait_ge(tile_done, i + 1)
                if kind == "v":
                    nc.scalar.copy(v[:, t, :], a[:, 0:NA_W]).then_inc(tile_copied, 1)
                else:
                    if t < NT:
                        nc.scalar.copy(z[:, t, :], a[:, 0:SSD_W]).then_inc(silu_x, 1)
                    nc.scalar.copy(dt[:, t, :], a[:, SSD_W:SSD_W + 2 * SSD_H]).then_inc(tile_copied, 1)

        @block.vector
        def _(dve):
            link = linked(dve, vec)
            dve.wait_ge(small_in, 80)

            def add_mod_bias(lo, hi):
                pm = pmod[:, 2 * lo:2 * hi].rearrange("p (m s) -> p m s", s=2)
                for s in range(2):
                    link(nc.vector.tensor_tensor(modT[:, lo:hi, s], pm[:, :, s], bmod[:, lo:hi], ALU.add))

            dve.wait_ge(ring_used, n_mod1)
            add_mod_bias(0, 2 * KD)
            for s in range(2):
                link(nc.vector.tensor_scalar(amul[:, :, s], modT[:, KD:2 * KD, s], 1.0, None, ALU.add))
                link(nc.vector.tensor_tensor(amul[:, :, s], amul[:, :, s], gcol[:, :], ALU.mult))
            dve.wait_ge(std_done, 1)
            link(nc.vector.reciprocal(rstd[:, :], rstd[:, :]))
            for s, (lo, hi) in enumerate(((0, T), (T, TA))):
                for k in range(KD):
                    h = hT[:, k, lo:hi]
                    link(nc.vector.scalar_tensor_tensor(h, h, amul[:, k, s:s + 1], rstd[:, lo:hi], ALU.mult, ALU.mult))
                    nc.vector.tensor_scalar(h, h, modT[:, k, s:s + 1], None, ALU.add).then_inc(h_done, 1)

            def conv(dst, src, w, taps):
                mid, width = taps // 2, src.shape[-1]
                link(nc.vector.tensor_scalar(dst, src, w[:, mid:mid + 1], w[:, taps:taps + 1], ALU.mult, ALU.add))
                for j in [j for j in range(taps) if j != mid]:
                    s = j - mid
                    o, i = (dst[:, 0:width - s], src[:, s:width]) if s > 0 else (dst[:, -s:width], src[:, 0:width + s])
                    last = nc.vector.scalar_tensor_tensor(o, i, w[:, j:j + 1], o, ALU.mult, ALU.add)
                    link(last)

            for c, (kind, m, _) in enumerate(chan):
                if kind == "x" or kind == "h":
                    dve.wait_ge(ring_used, n_before + c + 1)
                    a = acc[c % 2]
                    if kind == "x":
                        if has_ctx(c):
                            conv(xbcT[:, m, T:TA], a[:, T:TA], cw[:, m, :], SSD_K)
                        conv(xbcT[:, m, 0:T], a[:, 0:T], cw[:, m, :], SSD_K)
                        dve.sem_inc(conv_done, 1)
                    else:
                        conv(hyT[:, m, :], a[:, 0:T], hw[:, m, :], HY_K)
                    dve.sem_inc(tile_convolved, 1)
            dve.wait_ge(ring_used, len(loads))
            add_mod_bias(2 * KD, 6 * KD)


GRID_W, ROWS, NA_ROWS, NA_COLS, NA_H = 64, T // 64, 8, 16, 6
MASKED = -1e30


def identity(nc, pool, tile, sem):
    nc.gpsimd.memset(tile[:, :], 0.0).then_inc(sem, 1)
    pool.wait_ge(sem, 1)
    nc.gpsimd.affine_select(out=tile[:, :], in_=tile[:, :], compare_op=ALU.not_equal, fill=1.0, base=0,
                            pattern=[[-1, P]], channel_multiplier=1).then_inc(sem, 1)


def phase_attention(nc, kit, keep, io):
    scope = ExitStack()
    with scope:
        qT, kT, v, mixT = keep["qT"], keep["kT"], keep["v"], keep["mixT"]
        NS = 2 * NA_ROWS
        bias = kit.sb(scope, "na_bias", [P, NA_H, NS, GRID_W])
        cmask = kit.sb(scope, "na_col_mask", [P, GRID_W])
        ident = kit.sb(scope, "ident_na", [P, P])
        probs = kit.sb(scope, "na_probs", [P, 2, 832])
        pT = kit.sb(scope, "na_probs_t", [P, 2, 7, P])
        y = kit.sb(scope, "na_y", [P, NT, NA_W])
        items = [(m, h) for m in range(NT) for h in range(NA_H)]
        NI = len(items)
        mx = kit.sb(scope, "na_max", [P, NI, 4])
        sm = kit.sb(scope, "na_sum", [P, NI, 4])
        score = [kit.ps(scope, f"na_score{i}", [P, 1024]) for i in range(2)]
        trA = kit.ps(scope, "na_trA", [P, 512])
        trB = kit.ps(scope, "na_trB", [P, 512])
        out = [kit.ps(scope, f"na_out{i}", [P, 512]) for i in range(2)]
        S = {n: kit.sem("n_" + n) for n in ("bias_in", "mask_in", "ident", "bias_ready", "scored", "max_ready", "exped", "trA_done",
                                            "trB_done", "evA", "evB", "pv", "y_ready", "vec", "mtA", "mtB", "mcA", "mcB")}
        CTX0 = 576

        def key_rows(m):
            first = max(0, min(2 * m - NA_ROWS // 2, ROWS - NA_ROWS))
            return first, (9 if 2 * m - 4 >= 0 and 2 * m - 3 <= ROWS - NA_ROWS else 8)

        block = scope.enter_context(nc.Block())

        @block.sync
        def _(sp):
            sp.dma_start(cmask[:, :], io["na_col_mask"]).then_inc(S["mask_in"], 16)
            for h in range(NA_H):
                sp.dma_start(bias[:, h, :, :], io["rpb_skewed"][:, h, :, :]).then_inc(S["bias_in"], 16)

        @block.gpsimd
        def _(pool):
            identity(nc, pool, ident, S["ident"])
            pool.wait_ge(S["mask_in"], 16)
            pool.wait_ge(S["bias_in"], 16 * NA_H)
            for h in range(NA_H):
                m = bass.AP(cmask[:, :].tensor, cmask[:, :].offset, [cmask[:, :].ap[0], [0, NS], [1, GRID_W]])
                nc.gpsimd.tensor_tensor(bias[:, h, :, :], bias[:, h, :, :], m, ALU.add).then_inc(S["bias_ready"], 1)

        @block.tensor
        def _(pe):
            pe.wait_ge(S["ident"], 2)

            def scores(i):
                m, h = items[i]
                r0, nr = key_rows(m)
                lo = (h % 2) * HD
                if i >= 2:
                    pe.wait_ge(S["exped"], i - 1)
                q = qT[lo:lo + HD, h // 2, m * P:(m + 1) * P]
                ps = score[i % 2]
                k0 = r0 * GRID_W
                nc.tensor.matmul(ps[:, 0:512], q, kT[lo:lo + HD, h // 2, k0:k0 + 512], start=True, stop=True)
                if nr == 9:
                    nc.tensor.matmul(ps[:, 512:576], q, kT[lo:lo + HD, h // 2, k0 + 512:k0 + 576], start=True, stop=True)
                nc.tensor.matmul(ps[:, 768:1024], q, kT[lo:lo + HD, h // 2, T:TA], start=True, stop=True).then_inc(S["scored"], 1)

            def transposes(i):
                m, h = items[i]
                pe.wait_ge(S["exped"], i + 1)
                if i >= 1:
                    pe.wait_ge(S["evA"], i)
                    pe.wait_ge(S["evB"], i)
                pr = probs[:, i % 2, :]
                for b in range(4):
                    last = nc.tensor.transpose(trA[:, b * P:(b + 1) * P], pr[:, b * P:(b + 1) * P], ident[:, :])
                last.then_inc(S["trA_done"], 1)
                if key_rows(m)[1] == 9:
                    nc.tensor.transpose(trB[0:64, 0:P], pr[:, 512:576], ident[:, :])
                for b in range(2):
                    last = nc.tensor.transpose(trB[:, (b + 1) * P:(b + 2) * P], pr[:, CTX0 + b * P:CTX0 + (b + 1) * P], ident[:, :])
                last.then_inc(S["trB_done"], 1)

            def values(i):
                m, h = items[i]
                r0, nr = key_rows(m)
                pe.wait_ge(S["evA"], i + 1)
                pe.wait_ge(S["evB"], i + 1)
                if i >= 2:
                    pe.wait_ge(S["y_ready"], i - 1)
                o = out[i % 2][:, 0:HD]
                hc = slice(h * HD, (h + 1) * HD)
                t0 = r0 // 2
                for b in range(4):
                    nc.tensor.matmul(o, pT[:, i % 2, b, :], v[:, t0 + b, hc], start=(b == 0), stop=False)
                if nr == 9:
                    nc.tensor.matmul(o, pT[0:64, i % 2, 4, :], v[0:64, t0 + 4, hc], start=False, stop=False)
                for b in range(2):
                    last = nc.tensor.matmul(o, pT[:, i % 2, 5 + b, :], v[:, NT + b, hc], start=False, stop=(b == 1))
                last.then_inc(S["pv"], 1)

            for i in range(NI + 2):
                if i < NI:
                    scores(i)
                if 1 <= i <= NI:
                    transposes(i - 1)
                if i >= 2:
                    values(i - 2)
            for g in range(6):
                c, half = g // 2, g % 2
                pe.wait_ge(S["y_ready"], NI)
                if g >= 2:
                    pe.wait_ge(S["mcA" if half == 0 else "mcB"], g // 2)
                ps = trA if half == 0 else trB
                for b in range(4):
                    last = nc.tensor.transpose(ps[:, b * P:(b + 1) * P], y[:, 4 * half + b, c * P:(c + 1) * P], ident[:, :])
                last.then_inc(S["mtA" if half == 0 else "mtB"], 1)

        @block.scalar
        def _(act):
            for i in range(NI + 1):
                if i >= 1:
                    j = i - 1
                    act.wait_ge(S["trB_done"], j + 1)
                    if j >= 2:
                        act.wait_ge(S["pv"], j - 1)
                    if key_rows(items[j][0])[1] == 9:
                        nc.scalar.copy(pT[0:64, j % 2, 4, :], trB[0:64, 0:P])
                    nc.scalar.copy(pT[:, j % 2, 5:7, :], trB[:, P:3 * P]).then_inc(S["evB"], 1)
                if i < NI:
                    m, h = items[i]
                    w = key_rows(m)[1] * GRID_W
                    act.wait_ge(S["max_ready"], i + 1)
                    pr = probs[:, i % 2, :]
                    nc.scalar.activation(pr[:, 0:w], pr[:, 0:w], ACT.Exp, bias=mx[:, i, 3:4], accum_out=sm[:, i, 0:1])
                    nc.scalar.activation(pr[:, CTX0:832], score[i % 2][:, 768:1024], ACT.Exp, bias=mx[:, i, 3:4],
                                         scale=HD ** -0.5, accum_out=sm[:, i, 1:2]).then_inc(S["exped"], 1)
            for g in range(1, 6, 2):
                act.wait_ge(S["mtB"], g // 2 + 1)
                nc.scalar.copy(mixT[:, 3 + g // 2, T // 2:T], trB[:, :]).then_inc(S["mcB"], 1)

        @block.vector
        def _(dve):
            link = linked(dve, S["vec"])
            dve.wait_ge(S["bias_ready"], NA_H)
            for i in range(NI + 2):
                if i < NI:
                    m, h = items[i]
                    r0, nr = key_rows(m)
                    w = nr * GRID_W
                    s0 = r0 - 2 * m + NA_ROWS - 1
                    dve.wait_ge(S["scored"], i + 1)
                    if i >= 2:
                        dve.wait_ge(S["trB_done"], i - 1)
                    pr, ps = probs[:, i % 2, :], score[i % 2]
                    b = bias[:, h, s0:s0 + nr, :].rearrange("p r c -> p (r c)")
                    link(nc.vector.scalar_tensor_tensor(pr[:, 0:w], ps[:, 0:w], HD ** -0.5, b, ALU.mult, ALU.add))
                    if nr == 9:
                        nc.vector.memset(pr[64:128, 0:64], MASKED)
                        link(nc.vector.memset(pr[0:64, 512:576], MASKED))
                    nc.vector.tensor_reduce(mx[:, i, 0:1], pr[:, 0:w], AXX, ALU.max)
                    link(nc.vector.tensor_reduce(mx[:, i, 1:2], ps[:, 768:1024], AXX, ALU.max))
                    link(nc.vector.tensor_scalar(mx[:, i, 2:3], mx[:, i, 1:2], HD ** -0.5, mx[:, i, 0:1], ALU.mult, ALU.max))
                    nc.vector.tensor_scalar(mx[:, i, 3:4], mx[:, i, 2:3], -1.0, None, ALU.mult).then_inc(S["max_ready"], 1)
                if 1 <= i <= NI:
                    j = i - 1
                    dve.wait_ge(S["trA_done"], j + 1)
                    if j >= 2:
                        dve.wait_ge(S["pv"], j - 1)
                    nc.vector.tensor_copy(pT[:, j % 2, 0:4, :].rearrange("p a b -> p (a b)"), trA[:, :]).then_inc(S["evA"], 1)
                if i >= 2:
                    j = i - 2
                    m, h = items[j]
                    dve.wait_ge(S["exped"], j + 1)
                    link(nc.vector.tensor_tensor(sm[:, j, 2:3], sm[:, j, 0:1], sm[:, j, 1:2], ALU.add))
                    link(nc.vector.reciprocal(sm[:, j, 3:4], sm[:, j, 2:3]))
                    dve.wait_ge(S["pv"], j + 1)
                    nc.vector.tensor_scalar(y[:, m, h * HD:(h + 1) * HD], out[j % 2][:, 0:HD], sm[:, j, 3:4], None,
                                            ALU.mult).then_inc(S["y_ready"], 1)
            for g in range(0, 6, 2):
                dve.wait_ge(S["mtA"], g // 2 + 1)
                nc.vector.tensor_copy(mixT[:, 3 + g // 2, 0:T // 2], trA[:, :]).then_inc(S["mcA"], 1)


BF16 = mybir.dt.bfloat16


def phase_ssd(nc, kit, keep, io):
    scope = ExitStack()
    with scope:
        xbcT, z, dt, mixT = keep["xbcT"], keep["z"], keep["dt"], keep["mixT"]
        NC = NT + NTC
        H2 = 2 * SSD_H
        brow = kit.sb(scope, "dt_bias_row", [P, H2])
        arow = kit.sb(scope, "a_row", [P, H2])
        drow = kit.sb(scope, "d_skip_row", [P, SSD_H])
        ncol = kit.sb(scope, "ssd_norm_col", [P, 3])
        one = kit.sb(scope, "one_c", [P, 1])
        eps = kit.sb(scope, "eps_c", [P, 1])
        ones = kit.sb(scope, "ones_c", [P, P])
        tri = kit.sb(scope, "tri", [P, 2, P])
        ident = kit.sb(scope, "ident_c", [P, P])
        identb = kit.sb(scope, "ident_bf", [P, P], BF16)
        outside = kit.sb(scope, "outside_bf", [P, 2, P], BF16)
        sp_a = kit.sb(scope, "softplus_a", [P, NC, H2])
        sp_b = kit.sb(scope, "softplus_b", [P, NC, H2])
        dta = kit.sb(scope, "dta", [P, NC, H2])
        acs = kit.sb(scope, "acs", [P, NC, H2])
        nacs = kit.sb(scope, "neg_acs", [P, NC, H2])
        eacs = kit.sb(scope, "exp_acs", [P, NC, H2])
        wdec = kit.sb(scope, "state_weight", [P, NC, H2])
        dec = kit.sb(scope, "chunk_decay", [P, NC, H2])
        xs = kit.sb(scope, "xs_tok", [P, NC, SSD_W])
        btok = kit.sb(scope, "b_tok", [P, 2, NGRP * NST])
        xdec = kit.sb(scope, "x_decayed", [P, 2, 2, SSD_W])
        st = kit.sb(scope, "chunk_state", [P, NC, 2, SSD_W])
        run = kit.sb(scope, "run_state", [P, 2, SSD_W])
        start = kit.sb(scope, "start_state", [P, NT, NGRP, 2, GW])
        trirhs = kit.sb(scope, "tri_dta", [P, 2, SSD_H, P])
        E = xdec[:, :, :, :].rearrange("p a b c -> p (a b c)").rearrange("p (d h i) -> p d h i", d=2, h=SSD_H)
        W = E
        xdt = run
        t1 = kit.sb(scope, "ssd_t1", [P, SSD_W])
        t2 = btok[:, :, :].rearrange("p a b -> p (a b)")[:, 0:SSD_W]
        ssq = kit.sb(scope, "ssd_ssq", [P, NT, NGRP])
        squares = st
        y = z
        psG = kit.ps(scope, "psG", [P, 512])
        psY = kit.ps(scope, "psY", [P, 512])
        psI = kit.ps(scope, "psI", [P, 2, 512])
        psA = [kit.ps(scope, f"psA{d}", [P, 2, 512]) for d in range(2)]
        S = {n: kit.sem("s_" + n) for n in ("small_in", "pool", "vec", "actv", "dta_ready", "cum", "acs_ready", "exps", "tr", "ev", "xdec",
                                            "st", "st_ev", "scan", "tri_ready", "G", "A", "E", "W", "intra", "inter", "y_used", "gated",
                                            "ssq", "std", "scaled", "ytr", "mixed", "i_used")}

        def head_cols(ap):
            return bass.AP(ap.tensor, ap.offset, [ap.ap[0], [1, SSD_H], [0, HD]])

        def by_head(ap):
            return ap.rearrange("p (h d) -> p h d", d=HD)

        def g_bcast(g):
            a = psG[:, g * P:(g + 1) * P]
            return bass.AP(a.tensor, a.offset, [a.ap[0], [0, 3], [1, P]])

        def group_squares(act, c):
            act.wait_ge(S["gated"], c + 1)
            for g in range(NGRP):
                last = nc.scalar.activation(squares[:, c, 0, g * GW:(g + 1) * GW], y[:, c, g * GW:(g + 1) * GW], ACT.Square, accum_out=ssq[:, c, g:g + 1])
            last.then_inc(S["ssq"], 1)

        block = scope.enter_context(nc.Block())

        @block.sync
        def _(sp):
            for dst, src in ((brow, "dt_bias"), (arow, "a_log"), (drow, "ssd_d")):
                a = io[src]
                sp.dma_start(dst[:, :], bass.AP(a.tensor, a.offset, [[0, P], [1, a.shape[0]]])).then_inc(S["small_in"], 16)
            sp.dma_start(ncol[:, :], io["ssd_norm_col"]).then_inc(S["small_in"], 16)

        @block.gpsimd
        def _(pool):
            link = linked(pool, S["pool"])
            nc.gpsimd.memset(one[:, :], 1.0)
            nc.gpsimd.memset(eps[:, :], EPS)
            nc.gpsimd.memset(ones[:, :], 1.0)
            nc.gpsimd.memset(outside[:, :, :], 0.0)
            nc.gpsimd.memset(ident[:, :], 0.0)
            nc.gpsimd.memset(identb[:, :], 0.0)
            link(nc.gpsimd.memset(tri[:, :, :], 1.0))
            for m in (ident, identb):
                nc.gpsimd.affine_select(out=m[:, :], in_=m[:, :], compare_op=ALU.not_equal, fill=1.0, base=0,
                                        pattern=[[-1, P]], channel_multiplier=1)
            for m, fill in ((tri, 0.0), (outside, MASKED)):
                nc.gpsimd.affine_select(out=m[:, 0, :], in_=m[:, 0, :], compare_op=ALU.is_ge, fill=fill, base=0,
                                        pattern=[[1, P]], channel_multiplier=-1)
                last = nc.gpsimd.affine_select(out=m[:, 1, :], in_=m[:, 1, :], compare_op=ALU.is_ge, fill=fill, base=0,
                                               pattern=[[-1, P]], channel_multiplier=1)
            link(last)
            pool.wait_ge(S["dta_ready"], 1)
            for c in range(NT):
                if c >= 1:
                    pool.wait_ge(S["A"], c)
                for d in range(2):
                    a = dta[:, c, d * SSD_H:(d + 1) * SSD_H]
                    tr = tri[:, d, :]
                    nc.gpsimd.tensor_tensor(trirhs[:, d, :, :], bass.AP(tr.tensor, tr.offset, [tr.ap[0], [0, SSD_H], [1, P]]),
                                            bass.AP(a.tensor, a.offset, [a.ap[0], [1, SSD_H], [0, P]]),
                                            ALU.mult).then_inc(S["tri_ready"], 1)

        @block.tensor
        def _(pe):
            pe.wait_ge(S["pool"], 2)
            pe.wait_ge(S["dta_ready"], 1)
            for d in range(2):
                hs = slice(d * SSD_H, (d + 1) * SSD_H)
                nc.tensor.matmul(psA[0][:, d, 0:NC * SSD_H].rearrange("p (c h) -> p c h", h=SSD_H), tri[:, d, :], dta[:, :, hs],
                                 start=True, stop=True)
            nc.tensor.matmul(psA[1][:, 0, 0:NC * H2], ones[:, :], dta[:, :, :].rearrange("p c h -> p (c h)"), start=True,
                             stop=True).then_inc(S["cum"], 1)

            def turn(c):
                if c >= 1:
                    pe.wait_ge(S["ev"], c)
                for j in range(3):
                    nc.tensor.transpose(psY[:, j * P:(j + 1) * P], xbcT[:, j, c * P:(c + 1) * P], ident[:, :])
                for g in range(NGRP):
                    last = nc.tensor.transpose(psG[:, g * P:(g + 1) * P], xbcT[:, 3 + g, c * P:(c + 1) * P], ident[:, :])
                last.then_inc(S["tr"], 1)

            def states(c):
                pe.wait_ge(S["xdec"], c + 1)
                if c >= 1:
                    pe.wait_ge(S["st_ev"], c)
                for g in range(NGRP):
                    for d in range(2):
                        last = nc.tensor.matmul(psI[:, d, g * GW:(g + 1) * GW], btok[:, c % 2, g * P:(g + 1) * P],
                                                xdec[:, c % 2, d, g * GW:(g + 1) * GW], start=True, stop=True)
                last.then_inc(S["st"], 1)

            for c in range(NC + 1):
                if c < NC:
                    turn(c)
                if c >= 1:
                    states(c - 1)

            def decays(c):
                if c >= 1:
                    pe.wait_ge(S["W"], 4 * c)
                for g in range(NGRP):
                    last = nc.tensor.matmul(psG[:, g * P:(g + 1) * P], xbcT[:, 3 + g, c * P:(c + 1) * P],
                                            xbcT[:, 5 + g, c * P:(c + 1) * P], start=True, stop=True)
                last.then_inc(S["G"], 1)
                pe.wait_ge(S["exps"], 1)
                if c >= 1:
                    pe.wait_ge(S["E"], 2 * c)
                for d in range(2):
                    pe.wait_ge(S["tri_ready"], 2 * c + d + 1)
                    for h in range(2):
                        nc.tensor.matmul(psA[d][:, h, 0:3 * P], ones[:, :], trirhs[:, d, 3 * h:3 * h + 3, :], start=True, stop=False)
                    for h in range(2):
                        o = outside[:, d, :]
                        last = nc.tensor.matmul(psA[d][:, h, 0:3 * P].rearrange("p (a b) -> p a b", a=3), identb[:, :],
                                                bass.AP(o.tensor, o.offset, [o.ap[0], [0, 3], [1, P]]), start=False, stop=True)
                last.then_inc(S["A"], 1)

            def outputs(c):
                pe.wait_ge(S["scan"], 1)
                if c >= 1:
                    pe.wait_ge(S["i_used"], c)
                for g in range(NGRP):
                    last = nc.tensor.matmul(psI[:, g, 0:2 * GW], xbcT[:, 5 + g, c * P:(c + 1) * P],
                                            start_flat(c, g), start=True, stop=True)
                last.then_inc(S["inter"], 1)
                pe.wait_ge(S["W"], 4 * c + 4)
                if c >= 1:
                    pe.wait_ge(S["y_used"], c)
                for h in range(SSD_H):
                    for d in range(2):
                        last = nc.tensor.matmul(psY[:, h * HD:(h + 1) * HD], W[:, d, h, :], xdt[:, d, h * HD:(h + 1) * HD],
                                                start=(d == 0), stop=(d == 1))
                last.then_inc(S["intra"], 1)

            def start_flat(c, g):
                return start[:, c, g, :, :].rearrange("p d w -> p (d w)")

            for c in range(NT):
                decays(c)
                outputs(c)
            pe.wait_ge(S["scaled"], 1)
            for n in range(6):
                j, half = n // 2, n % 2
                ps = psY if half == 0 else psG
                if n >= 2:
                    pe.wait_ge(S["mixed"], n - 1)
                for b in range(4):
                    last = nc.tensor.transpose(ps[:, b * P:(b + 1) * P], y[:, 4 * half + b, j * P:(j + 1) * P], ident[:, :])
                last.then_inc(S["ytr"], 1)

        @block.scalar
        def _(act):
            link = linked(act, S["actv"])
            act.wait_ge(S["pool"], 2)
            act.wait_ge(S["small_in"], 64)
            nc.scalar.activation(z[:, :, :], z[:, :, :], ACT.Silu)
            act.wait_ge(S["vec"], 2)
            link(nc.scalar.activation(sp_b[:, :, :], sp_b[:, :, :], ACT.Exp, scale=-1.0))
            link(nc.scalar.activation(arow[:, :], arow[:, :], ACT.Exp))
            link(nc.scalar.activation(acs[:, :, :], sp_b[:, :, :], ACT.Ln, bias=one[:, 0:1]))
            for c in range(NC):
                act.wait_ge(S["tr"], c + 1)
                if c >= 2:
                    act.wait_ge(S["st"], c - 1)
                nc.scalar.copy(xs[:, c, :], psY[:, 0:SSD_W])
                nc.scalar.copy(btok[:, c % 2, :], psG[:, 0:2 * P]).then_inc(S["ev"], 1)
                if c == 0:
                    act.wait_ge(S["acs_ready"], 1)
                    nc.scalar.activation(eacs[:, :, :], acs[:, :, :], ACT.Exp)
                    nc.scalar.activation(wdec[:, :, :], wdec[:, :, :], ACT.Exp)
                    nc.scalar.activation(dec[:, :, :], dec[:, :, :], ACT.Exp).then_inc(S["exps"], 1)
                if c >= 1:
                    act.wait_ge(S["st"], c)
                    nc.scalar.copy(st[:, c - 1, :, :], psI[:, :, 0:SSD_W]).then_inc(S["st_ev"], 1)
            act.wait_ge(S["st"], NC)
            nc.scalar.copy(st[:, NC - 1, :, :], psI[:, :, 0:SSD_W]).then_inc(S["st_ev"], 1)
            for c in range(NT):
                act.wait_ge(S["A"], c + 1)
                if c >= 1:
                    act.wait_ge(S["intra"], c)
                for d in range(2):
                    for h in range(SSD_H):
                        last = nc.scalar.activation(E[:, d, h, :], psA[d][:, h // 3, (h % 3) * P:(h % 3 + 1) * P], ACT.Exp,
                                                    bias=nacs[:, c, d * SSD_H + h:d * SSD_H + h + 1])
                    last.then_inc(S["E"], 1)
                if c >= 1:
                    group_squares(act, c - 1)
            group_squares(act, NT - 1)
            act.wait_ge(S["ssq"], NT)
            nc.scalar.activation(ssq[:, :, :], ssq[:, :, :], ACT.Sqrt, bias=eps[:, 0:1], scale=1.0 / GW).then_inc(S["std"], 1)
            for n in range(6):
                act.wait_ge(S["ytr"], n + 1)
                j, half = n // 2, n % 2
                nc.scalar.activation(mixT[:, j, half * 512:(half + 1) * 512], (psY if half == 0 else psG)[:, :], ACT.Copy,
                                     scale=ncol[:, j:j + 1]).then_inc(S["mixed"], 1)

        @block.vector
        def _(dve):
            link = linked(dve, S["vec"])
            dve.wait_ge(S["small_in"], 64)
            b = bass.AP(brow[:, :].tensor, brow[:, :].offset, [brow[:, :].ap[0], [0, NC], [1, H2]])
            link(nc.vector.tensor_tensor(sp_a[:, :, :], dt[:, :, :], b, ALU.add))
            link(nc.vector.scalar_tensor_tensor(sp_b[:, :, :], sp_a[:, :, :], -1.0, sp_a[:, :, :], ALU.mult, ALU.max))
            dve.wait_ge(S["actv"], 3)
            link(nc.vector.tensor_scalar(nacs[:, :, :], sp_b[:, :, :], 1.0, None, ALU.add))
            link(nc.vector.tensor_scalar(eacs[:, :, :], nacs[:, :, :], -1.0, None, ALU.add))
            link(nc.vector.tensor_tensor(sp_b[:, :, :], sp_b[:, :, :], eacs[:, :, :], ALU.subtract))
            link(nc.vector.reciprocal(nacs[:, :, :], nacs[:, :, :]))
            link(nc.vector.tensor_tensor(sp_b[:, :, :], sp_b[:, :, :], nacs[:, :, :], ALU.mult))
            link(nc.vector.tensor_tensor(sp_b[:, :, :], sp_b[:, :, :], acs[:, :, :], ALU.add))
            link(nc.vector.scalar_tensor_tensor(dt[:, :, :], sp_a[:, :, :], 0.0, sp_b[:, :, :], ALU.max, ALU.add))
            a = bass.AP(arow[:, :].tensor, arow[:, :].offset, [arow[:, :].ap[0], [0, NC], [1, H2]])
            nc.vector.scalar_tensor_tensor(dta[:, :, :], dt[:, :, :], -1.0, a, ALU.mult, ALU.mult).then_inc(S["dta_ready"], 1)
            dve.wait_ge(S["cum"], 1)
            for d in range(2):
                hs = slice(d * SSD_H, (d + 1) * SSD_H)
                link(nc.vector.tensor_copy(acs[:, :, hs], psA[0][:, d, 0:NC * SSD_H].rearrange("p (c h) -> p c h", h=SSD_H)))
            link(nc.vector.tensor_copy(dec[:, :, :].rearrange("p c h -> p (c h)"), psA[1][:, 0, 0:NC * H2]))
            link(nc.vector.tensor_scalar(nacs[:, :, :], acs[:, :, :], -1.0, None, ALU.mult))
            nc.vector.tensor_tensor(wdec[:, :, :], dec[:, :, :], nacs[:, :, :], ALU.add).then_inc(S["acs_ready"], 1)
            dve.wait_ge(S["exps"], 1)
            link(nc.vector.tensor_tensor(wdec[:, :, :], wdec[:, :, :], dt[:, :, :], ALU.mult))
            for c in range(NC):
                dve.wait_ge(S["ev"], c + 1)
                if c >= 2:
                    dve.wait_ge(S["st"], c - 1)
                for d in range(2):
                    last = nc.vector.tensor_tensor(by_head(xdec[:, c % 2, d, :]), by_head(xs[:, c, :]),
                                                   head_cols(wdec[:, c, d * SSD_H:(d + 1) * SSD_H]), ALU.mult)
                last.then_inc(S["xdec"], 1)
            link(nc.vector.memset(run[:, :, :], 0.0))
            dve.wait_ge(S["st_ev"], NC)
            for n in range(NC):
                for d in range(2):
                    c = (NT + n if n < NTC else n - NTC) if d == 0 else (NT + NTC - 1 - n if n < NTC else NT - 1 - (n - NTC))
                    if n >= NTC:
                        nc.vector.tensor_copy(start[:, c, :, d, :], run[:, d, :].rearrange("p (g w) -> p g w", g=NGRP))
                    if n < NC - 1:
                        link(nc.vector.tensor_tensor(by_head(run[:, d, :]), by_head(run[:, d, :]),
                                                     head_cols(dec[:, c, d * SSD_H:(d + 1) * SSD_H]), ALU.mult))
                        link(nc.vector.tensor_tensor(run[:, d, :], run[:, d, :], st[:, c, d, :], ALU.add))
            link(nc.vector.memset(t1[:, :], 0.0))
            dve.sem_inc(S["scan"], 1)
            for c in range(NT):
                if c >= 1:
                    dve.wait_ge(S["intra"], c)
                for d in range(2):
                    nc.vector.tensor_tensor(by_head(xdt[:, d, :]), by_head(xs[:, c, :]),
                                            head_cols(dt[:, c, d * SSD_H:(d + 1) * SSD_H]), ALU.mult)
                dve.wait_ge(S["G"], c + 1)
                for d in range(2):
                    dve.wait_ge(S["E"], 2 * c + d + 1)
                    for g in range(NGRP):
                        nc.vector.tensor_tensor(W[:, d, 3 * g:3 * g + 3, :], E[:, d, 3 * g:3 * g + 3, :], g_bcast(g),
                                                ALU.mult).then_inc(S["W"], 1)
                dve.wait_ge(S["inter"], c + 1)
                for d, t in ((0, t1[:, :]), (1, t2)):
                    src = psI[:, :, d * GW:(d + 1) * GW].rearrange("p g (h e) -> p g h e", e=HD)
                    e = eacs[:, c, d * SSD_H:(d + 1) * SSD_H]
                    e = bass.AP(e.tensor, e.offset, [e.ap[0], [3, NGRP], [1, 3], [0, HD]])
                    link(nc.vector.tensor_tensor(t.rearrange("p (g h e) -> p g h e", g=NGRP, e=HD), src, e, ALU.mult))
                dve.sem_inc(S["i_used"], 1)
                link(nc.vector.tensor_tensor(t1[:, :], t1[:, :], t2, ALU.add))
                link(nc.vector.tensor_tensor(by_head(t2), by_head(xs[:, c, :]), head_cols(drow[:, :]), ALU.mult))
                link(nc.vector.tensor_tensor(t1[:, :], t1[:, :], t2, ALU.add))
                dve.wait_ge(S["intra"], c + 1)
                link(nc.vector.tensor_tensor(t1[:, :], t1[:, :], psY[:, 0:SSD_W], ALU.add))
                dve.sem_inc(S["y_used"], 1)
                link(nc.vector.tensor_tensor(y[:, c, :], t1[:, :], z[:, c, :], ALU.mult))
                dve.sem_inc(S["gated"], 1)
            dve.wait_ge(S["std"], 1)
            link(nc.vector.reciprocal(ssq[:, :, :], ssq[:, :, :]))
            for c in range(NT):
                for g in range(NGRP):
                    last = nc.vector.tensor_scalar(y[:, c, g * GW:(g + 1) * GW], y[:, c, g * GW:(g + 1) * GW], ssq[:, c, g:g + 1], None,
                                                   ALU.mult)
            last.then_inc(S["scaled"], 1)


HY_EMB, HY_HID = 33, 64
TWO_PI_HI = 6.28125
TWO_PI_LO = 2 * np.pi - 6.28125
PI_BELOW = float(np.nextafter(np.float32(np.pi), np.float32(0)))
ROUND = 1.5 * 2.0 ** 23


def phase_hyena(nc, kit, keep, io):
    scope = ExitStack()
    with scope:
        hyT, mixT = keep["hyT"], keep["mixT"]
        cos = kit.sb(scope, "dft_cos", [P, NT, T])
        sin = kit.sb(scope, "dft_sin", [P, NT, T])
        X = kit.sb(scope, "hy_x", [P, NT, 3, HY_W])
        Z = kit.sb(scope, "hy_z", [P, NT, 2, HY_W])
        decay = kit.sb(scope, "hy_decay", [P, NT, HY_W])
        w1 = kit.sb(scope, "hy_w1", [HY_EMB, HY_HID])
        w2 = kit.sb(scope, "hy_w2", [HY_HID, HY_HID])
        w3 = kit.sb(scope, "hy_w3", [HY_HID, 2 * HY_W])
        zt = kit.sb(scope, "hy_pos", [HY_EMB, T])
        bf = kit.sb(scope, "hy_bias_freq", [HY_HID, 2, 2])
        hid = Z[0:HY_HID, 2:4, :, :].rearrange("p a b c -> p (a b c)")
        turns = Z[0:HY_HID, 0:2, :, :].rearrange("p a b c -> p (a b c)")
        drow = kit.sb(scope, "hy_d_row", [1, HY_W])
        alt_row = kit.sb(scope, "alt_row", [1, T])
        alt_col = kit.sb(scope, "alt_col", [P, 1])
        wcol = kit.sb(scope, "inv_scale", [P, NT])
        ident = kit.sb(scope, "ident_d", [P, P])
        ones = kit.sb(scope, "ones_d", [P, P])
        absd = kit.sb(scope, "hy_abs", [P, 2, 2, HY_W])
        inv = kit.sb(scope, "hy_inv", [P, HY_W])
        F = decay[:, :, :].rearrange("p (s j) c -> p s j c", s=2)
        tmp = kit.sb(scope, "hy_tmp", [P, 2, HY_W])
        nyq = kit.sb(scope, "hy_nyq", [1, 2 * HY_W])
        znyq = kit.sb(scope, "hy_znyq", [1, HY_W])
        ps = [kit.ps(scope, f"hyps{i}", [P, 512]) for i in range(8)]
        S = {n: kit.sem("h_" + n) for n in ("small_in", "cos_in", "sin_in", "ident", "ones", "vec", "u_ready", "utr", "u_tok", "h1", "h2",
                                            "red", "sined", "h3", "h3_read", "abs", "abs_used", "abs_sum", "x_ready", "nyq", "nyq_out", "znyq", "fwd",
                                            "spec", "z", "inv", "wrote")}
        block = scope.enter_context(nc.Block())
        small = ((w1, "hy_f_w1"), (w2, "hy_f_w2"), (w3, "hy_f_w3"), (zt, "hy_pos"), (bf, "hy_bias_freq"), (decay, "hy_decay"), (drow, "hy_d"),
                 (alt_row, "alt_row"), (alt_col, "alt_col"), (wcol, "inv_scale"))

        @block.sync
        def _(sp):
            for dst, src in small:
                sp.dma_start(dst[:], io[src]).then_inc(S["small_in"], 16)
            sp.dma_start(cos[:, :, :], io["dft_cos"].rearrange("(k p) n -> p k n", p=P)).then_inc(S["cos_in"], 16)
            sp.dma_start(sin[:, :, :], io["dft_sin"].rearrange("(k p) n -> p k n", p=P)).then_inc(S["sin_in"], 16)

        @block.gpsimd
        def _(pool):
            identity(nc, pool, ident, S["ident"])
            nc.gpsimd.memset(ones[:, :], 1.0).then_inc(S["ones"], 1)

        @block.tensor
        def _(pe):
            pe.wait_ge(S["ident"], 2)
            for n in range(4):
                c, half = n // 2, n % 2
                pe.wait_ge(S["u_ready"], c + 1)
                for b in range(4):
                    t = 4 * half + b
                    last = nc.tensor.transpose(ps[4 + n][:, b * P:(b + 1) * P], hyT[:, 4 + c, t * P:(t + 1) * P], ident[:, :])
                last.then_inc(S["utr"], 1)
            pe.wait_ge(S["small_in"], 16 * len(small))
            for i in range(2):
                last = nc.tensor.matmul(ps[i][0:HY_HID, :], w1[:, :], zt[:, i * 512:(i + 1) * 512], start=True, stop=True)
            last.then_inc(S["h1"], 1)
            pe.wait_ge(S["sined"], 1)
            for i in range(2):
                last = nc.tensor.matmul(ps[2 + i][0:HY_HID, :], w2[:, :], hid[:, i * 512:(i + 1) * 512], start=True, stop=True)
            last.then_inc(S["h2"], 1)
            pe.wait_ge(S["sined"], 2)
            pe.wait_ge(S["ones"], 1)
            for k in range(NT + 1):
                if k < NT:
                    if k >= 2:
                        pe.wait_ge(S["h3_read"], k - 1)
                    nc.tensor.matmul(ps[k % 2][:, :], hid[:, k * P:(k + 1) * P], w3[:, :], start=True, stop=True).then_inc(S["h3"], 1)
                if k >= 1:
                    pe.wait_ge(S["abs"], k)
                    nc.tensor.matmul(ps[2][:, :], ones[:, :], absd[:, (k - 1) % 2, :, :].rearrange("p a b -> p (a b)"), start=(k == 1),
                                     stop=(k == NT)).then_inc(S["abs_used"], 1)
            pe.wait_ge(S["x_ready"], 1)
            pe.wait_ge(S["u_tok"], 4)
            for k in range(NT):
                last = nc.tensor.matmul(ps[3][0:1, :], alt_col[:, :], X[:, k, 0:2, :].rearrange("p a b -> p (a b)"), start=(k == 0),
                                        stop=(k == NT - 1))
            last.then_inc(S["nyq"], 1)
            for f in range(NT):
                if f >= 2:
                    pe.wait_ge(S["spec"], f - 1)
                for j, (tab, lo, sem) in enumerate(((cos, 0, "cos_in"), (sin, 1, "sin_in"))):
                    pe.wait_ge(S[sem], 16)
                    for k in range(NT):
                        last = nc.tensor.matmul(ps[4 + 2 * (f % 2) + j][:, :], tab[:, k, f * P:(f + 1) * P],
                                                X[:, k, lo:lo + 2, :].rearrange("p a b -> p (a b)"), start=(k == 0), stop=(k == NT - 1))
                last.then_inc(S["fwd"], 1)
            pe.wait_ge(S["znyq"], 1)
            for q in range(4):
                c, half = q // 2, q % 2
                o, t = ps[q][:, :], slice(half * 512, (half + 1) * 512)
                nc.tensor.matmul(o, znyq[:, c * P:(c + 1) * P], alt_row[:, t], start=True, stop=False)
                for f in range(NT):
                    pe.wait_ge(S["z"], f + 1)
                    nc.tensor.matmul(o, Z[:, f, 0, c * P:(c + 1) * P], cos[:, f, t], start=False, stop=False)
                    last = nc.tensor.matmul(o, Z[:, f, 1, c * P:(c + 1) * P], sin[:, f, t], start=False, stop=(f == NT - 1))
                last.then_inc(S["inv"], 1)

        @block.scalar
        def _(act):
            for n in range(4):
                c, half = n // 2, n % 2
                act.wait_ge(S["utr"], n + 1)
                nc.scalar.copy(X[:, 4 * half:4 * half + 4, 1, c * P:(c + 1) * P],
                               ps[4 + n][:, :].rearrange("p (b c) -> p b c", b=4)).then_inc(S["u_tok"], 1)
            for i in range(2):
                act.wait_ge(S["red"], i + 1)
                nc.scalar.activation(hid[:, :], turns[:, :], ACT.Sin).then_inc(S["sined"], 1)
            for k in range(NT):
                act.wait_ge(S["h3_read"], k + 1)
                if k >= 2:
                    act.wait_ge(S["abs_used"], k - 1)
                nc.scalar.activation(absd[:, k % 2, :, :], X[:, k, 0:3:2, :], ACT.Abs).then_inc(S["abs"], 1)
            act.wait_ge(S["nyq"], 1)
            nc.scalar.copy(nyq[:, :], ps[3][0:1, :]).then_inc(S["nyq_out"], 1)
            for f in range(NT):
                act.wait_ge(S["fwd"], f + 1)
                if f >= 2:
                    act.wait_ge(S["z"], f - 1)
                for j in range(2):
                    last = nc.scalar.copy(F[:, f % 2, 2 * j:2 * j + 2, :].rearrange("p a b -> p (a b)"), ps[4 + 2 * (f % 2) + j][:, :])
                last.then_inc(S["spec"], 1)

        @block.vector
        def _(dve):
            link = linked(dve, S["vec"])
            for c in range(2):
                nc.vector.tensor_tensor(hyT[:, 4 + c, :], hyT[:, 4 + c, :], hyT[:, 2 + c, :], ALU.mult).then_inc(S["u_ready"], 1)
            dve.wait_ge(S["small_in"], 16 * len(small))
            for i, done in enumerate(("h1", "h2")):
                dve.wait_ge(S[done], 1)
                for j in range(2):
                    o = slice(j * 512, (j + 1) * 512)
                    link(nc.vector.tensor_scalar(turns[:, o], ps[2 * i + j][0:HY_HID, :], bf[:, i, 0:1], bf[:, i, 1:2], ALU.add, ALU.mult))
                link(nc.vector.tensor_scalar(hid[:, :], turns[:, :], 1 / (2 * np.pi), ROUND, ALU.mult, ALU.add))
                link(nc.vector.tensor_scalar(hid[:, :], hid[:, :], -ROUND, None, ALU.add))
                link(nc.vector.scalar_tensor_tensor(turns[:, :], hid[:, :], -TWO_PI_HI, turns[:, :], ALU.mult, ALU.add))
                link(nc.vector.scalar_tensor_tensor(turns[:, :], hid[:, :], -TWO_PI_LO, turns[:, :], ALU.mult, ALU.add))
                link(nc.vector.tensor_scalar(turns[:, :], turns[:, :], PI_BELOW, -PI_BELOW, ALU.min, ALU.max))
                dve.sem_inc(S["red"], 1)
            for k in range(NT):
                dve.wait_ge(S["h3"], k + 1)
                nc.vector.tensor_tensor(X[:, k, 0, :], ps[k % 2][:, 0:HY_W], decay[:, k, :], ALU.mult)
                nc.vector.tensor_tensor(X[:, k, 2, :], ps[k % 2][:, HY_W:], decay[:, k, :], ALU.mult).then_inc(S["h3_read"], 1)
            dve.wait_ge(S["abs_used"], NT)
            link(nc.vector.tensor_copy(inv[:, :], ps[2][:, 0:HY_W]))
            link(nc.vector.tensor_tensor(inv[:, :], inv[:, :], ps[2][:, HY_W:], ALU.add))
            link(nc.vector.reciprocal(inv[:, :], inv[:, :]))
            ib = bass.AP(inv[:, :].tensor, inv[:, :].offset, [inv[:, :].ap[0], [0, NT], [1, HY_W]])
            link(nc.vector.tensor_tensor(X[:, :, 0, :], X[:, :, 0, :], ib, ALU.mult))
            link(nc.vector.tensor_tensor(X[:, :, 2, :], X[:, :, 2, :], ib, ALU.mult))
            link(nc.vector.memset(X[0:1, 0, 2, :], 0.0))
            link(nc.vector.tensor_tensor(X[0:1, 0, 0, :], X[0:1, 0, 0, :], drow[:, :], ALU.add))
            link(nc.vector.tensor_tensor(X[:, :, 0, :], X[:, :, 0, :], X[:, :, 2, :], ALU.add))
            link(nc.vector.scalar_tensor_tensor(X[:, :, 2, :], X[:, :, 2, :], -2.0, X[:, :, 0, :], ALU.mult, ALU.add))
            dve.sem_inc(S["x_ready"], 1)
            dve.wait_ge(S["nyq_out"], 1)
            nc.vector.scalar_tensor_tensor(znyq[:, :], nyq[:, 0:HY_W], 1.0 / (2 * T), nyq[:, HY_W:], ALU.mult, ALU.mult).then_inc(S["znyq"], 1)
            for f in range(NT):
                dve.wait_ge(S["spec"], f + 1)
                kr, ur, us, ks = (F[:, f % 2, j, :] for j in range(4))
                w = wcol[:, f:f + 1]
                nc.vector.scalar_tensor_tensor(Z[:, f, 0, :], ur, w, kr, ALU.mult, ALU.mult)
                nc.vector.scalar_tensor_tensor(tmp[:, 0, :], us, w, ks, ALU.mult, ALU.mult)
                nc.vector.scalar_tensor_tensor(Z[:, f, 1, :], ur, w, ks, ALU.mult, ALU.mult)
                link(nc.vector.scalar_tensor_tensor(tmp[:, 1, :], us, w, kr, ALU.mult, ALU.mult))
                link(nc.vector.tensor_tensor(Z[:, f, 0, :], Z[:, f, 0, :], tmp[:, 0, :], ALU.subtract))
                link(nc.vector.tensor_tensor(Z[:, f, 1, :], Z[:, f, 1, :], tmp[:, 1, :], ALU.add))
                dve.sem_inc(S["z"], 1)
            for q in range(4):
                c, half = q // 2, q % 2
                dve.wait_ge(S["inv"], q + 1)
                t = slice(half * 512, (half + 1) * 512)
                last = nc.vector.tensor_tensor(mixT[:, 6 + c, t], ps[q][:, :], hyT[:, c, t], ALU.mult)
            last.then_inc(S["wrote"], 1)
            dve.wait_ge(S["wrote"], 1)


def hyena_constants():
    f32 = np.float32
    t = np.linspace(0.0, 1.0, T, dtype=f32)[:, None]
    w = (f32(2.0 * np.pi) * np.arange(T, dtype=f32)[:, None] / f32(T)).astype(f32)
    bands = (HY_EMB - 1) // 2
    f = np.linspace(1e-4, bands - 1, bands, dtype=f32)[None, :]
    pos = np.concatenate([t, np.cos(f * w), -np.sin(f * w)], axis=1).astype(f32)
    deltas = np.abs(np.linspace(np.log(1e-2) / 1.5, np.log(1e-2) / 0.3, HY_W, dtype=f32))
    decay = np.exp(-t * deltas).astype(f32)
    angle = np.outer(np.arange(T), np.arange(T)) % (2 * T) * (np.pi / T)
    alt = (1.0 - 2.0 * (np.arange(T) % 2)).astype(f32)
    scale = np.full(T, 1.0 / T)
    scale[0] = 0.5 / T
    return {
        "hy_pos": np.ascontiguousarray(pos.T),
        "hy_decay": np.ascontiguousarray(decay.reshape(NT, P, HY_W).transpose(1, 0, 2)),
        "dft_cos": np.cos(angle).astype(f32),
        "dft_sin": np.sin(angle).astype(f32),
        "alt_row": alt[None, :],
        "alt_col": np.ascontiguousarray(alt[:P, None]),
        "inv_scale": np.ascontiguousarray(scale.astype(f32).reshape(NT, P).T),
    }


NBLK = (T * TOPK + NE * (P - 1)) // P + 1
NROW = NBLK * P


def row_of(ap, n, at=0):
    return bass.AP(ap.tensor, ap.offset + at, [[0, P], [1, n]])


def phase_mix(nc, kit, keep, io, dram):
    scope = ExitStack()
    with scope:
        mixT, modT, dest, gate, table = keep["mixT"], keep["modT"], keep["dest"], keep["gate"], keep["table"]
        wout = kit.sb(scope, "w_out", [P, KD, D])
        wr = kit.sb(scope, "w_router", [P, KD, NE])
        brt = kit.sb(scope, "b_router_row", [P, NE])
        gains = kit.sb(scope, "gains_col", [P, 3, KD])
        vcol = kit.sb(scope, "vectors_col", [P, 4, KD])
        vrow = kit.sb(scope, "vectors_rows", [4 * KD, P])
        rows = kit.sb(scope, "vectors_row", [P, 3, D])
        xin = kit.sb(scope, "x_tile", [P, 2, D])
        x1 = kit.sb(scope, "x1_tile", [P, 2, D])
        h2 = kit.sb(scope, "h2_tile", [P, 2, D])
        sq = kit.sb(scope, "mix_squares", [P, 2, D])
        h2T = kit.sb(scope, "h2_t", [P, KD, P])
        st = kit.sb(scope, "mix_stat", [P, NT, 4])
        eps = kit.sb(scope, "eps_e", [P, 1])
        ident = kit.sb(scope, "ident_e", [P, P])
        ones = kit.sb(scope, "ones_e", [P, P])
        before = kit.sb(scope, "tri_strict", [P, P])
        lanes = kit.sb(scope, "expert_number", [P, NE])
        logit = kit.sb(scope, "logits", [P, NE])
        top = kit.sb(scope, "top_logits", [P, NT, 8])
        topi = kit.sb(scope, "top_experts", [P, NT, 8], U32)
        topf = kit.sb(scope, "top_experts_f", [P, NT, TOPK])
        shifted = kit.sb(scope, "top_shifted", [P, NT, TOPK])
        gsum = kit.sb(scope, "gate_sum", [P, NT])
        hot = kit.sb(scope, "one_hot", [P, NT, TOPK, NE])
        mask = kit.sb(scope, "chosen", [P, NT, NE])
        place = kit.sb(scope, "place", [P, NT, NE])
        count = kit.sb(scope, "count_so_far", [P, NT + 1, NE])
        blocks = kit.sb(scope, "blocks", [P, NE])
        cum = kit.sb(scope, "blocks_cum", [P, 2, NE])
        destf = kit.sb(scope, "dest_f", [P, NT, TOPK])
        tokens = kit.sb(scope, "token_number", [P, NT], I32)
        zero = kit.sb(scope, "zero_rows", [P, NBLK], I32)
        psO = [kit.ps(scope, f"psO{i}", [P, D]) for i in range(2)]
        psH = kit.ps(scope, "psH", [P, D])
        psL = kit.ps(scope, "psL", [P, 512])
        psR = kit.ps(scope, "psR", [P, 512])
        S = {n: kit.sem("e_" + n) for n in ("w_in", "small_in", "pool", "vec", "vcol", "vturn", "vrow", "vrow_out", "rows_in", "x_in0", "x_in1",
                                            "proj", "std1", "x1", "std2", "h2", "x1_out0", "x1_out1", "h2_out0", "h2_out1", "h2turn", "h2T",
                                            "logits", "logits_read", "shifted", "exped", "mask", "ranks", "dest", "zeroed", "scattered",
                                            "table")}
        block = scope.enter_context(nc.Block())

        @block.sync
        def _(sp):
            sp.dma_start(gains[:, :, :], io["gains_col"]).then_inc(S["small_in"], 16)
            sp.dma_start(brt[:, :], row_of(io["b_router"], NE)).then_inc(S["small_in"], 16)
            sp.dma_start(wr[:, :, :], io["w_router"].rearrange("(k p) n -> p k n", p=P)).then_inc(S["small_in"], 16)
            sp.dma_start(wout[:, :, :], io["w_out"].rearrange("(k p) n -> p k n", p=P)).then_inc(S["w_in"], 16)
            for t in range(2):
                sp.dma_start(xin[:, t, :], io["x"][t * P:(t + 1) * P, :]).then_inc(S[f"x_in{t}"], 16)
            sp.wait_ge(S["vrow"], 1)
            sp.dma_start(dram["vectors"].rearrange("(r p) -> r p", p=P), vrow[:, :]).then_inc(S["vrow_out"], 16)
            sp.wait_ge(S["vrow_out"], 16)
            for j in range(3):
                sp.dma_start(rows[:, j, :], row_of(dram["vectors"], D, j * D)).then_inc(S["rows_in"], 16)
            for t in range(NT):
                ts = slice(t * P, (t + 1) * P)
                sp.wait_ge(S["x1"], t + 1)
                sp.dma_start(dram["x1"][ts, :], x1[:, t % 2, :]).then_inc(S[f"x1_out{t % 2}"], 16)
                if t + 2 < NT:
                    sp.dma_start(xin[:, t % 2, :], io["x"][(t + 2) * P:(t + 3) * P, :]).then_inc(S[f"x_in{t % 2}"], 16)
                sp.wait_ge(S["h2"], t + 1)
                sp.dma_start(dram["h2"][ts, :], h2[:, t % 2, :]).then_inc(S[f"h2_out{t % 2}"], 16)
            for i in range(2):
                sp.wait_ge(S[f"x1_out{i}"], 16 * NT // 2)
                sp.wait_ge(S[f"h2_out{i}"], 16 * NT // 2)

        @block.gpsimd
        def _(pool):
            link = linked(pool, S["pool"])
            nc.gpsimd.memset(eps[:, :], EPS)
            nc.gpsimd.memset(ident[:, :], 0.0)
            nc.gpsimd.memset(ones[:, :], 1.0)
            nc.gpsimd.memset(zero[:, :], 0)
            nc.gpsimd.iota(lanes[:, :], pattern=[[1, NE]], base=0, channel_multiplier=0, allow_small_or_imprecise_dtypes=True)
            nc.gpsimd.iota(tokens[:, :], pattern=[[P, NT]], base=0, channel_multiplier=1)
            link(nc.gpsimd.memset(before[:, :], 1.0))
            nc.gpsimd.affine_select(out=ident[:, :], in_=ident[:, :], compare_op=ALU.not_equal, fill=1.0, base=0, pattern=[[-1, P]],
                                    channel_multiplier=1)
            link(nc.gpsimd.affine_select(out=before[:, :], in_=before[:, :], compare_op=ALU.is_gt, fill=0.0, base=0, pattern=[[1, P]],
                                         channel_multiplier=-1))
            pool.dma_start(dram["row_token"].rearrange("(p b) o -> p (b o)", p=P), zero[:, :]).then_inc(S["zeroed"], 16)
            pool.wait_ge(S["zeroed"], 16)
            pool.wait_ge(S["dest"], 1)
            for t in range(NT):
                for k in range(TOPK):
                    pool.indirect_dma_start(out=dram["row_token"], out_offset=bass.IndirectOffsetOnAxis(ap=dest[:, t * TOPK + k:t * TOPK + k + 1], axis=0),
                                            in_=tokens[:, t:t + 1], in_offset=None).then_inc(S["scattered"], 16)
            pool.wait_ge(S["scattered"], 16 * NT * TOPK)

        @block.tensor
        def _(pe):
            pe.wait_ge(S["pool"], 2)
            pe.wait_ge(S["vcol"], 1)
            nc.tensor.transpose(psR[0:4 * KD, 0:P], vcol[:, :, :].rearrange("p a k -> p (a k)"), ident[:, :]).then_inc(S["vturn"], 1)
            pe.wait_ge(S["w_in"], 16)

            def project(t):
                if t >= 2:
                    pe.wait_ge(S["x1"], t - 1)
                for n in range(2):
                    for k in range(KD):
                        last = nc.tensor.matmul(psO[t % 2][:, n * 512:(n + 1) * 512], mixT[:, k, t * P:(t + 1) * P],
                                                wout[:, k, n * 512:(n + 1) * 512], start=(k == 0), stop=(k == KD - 1))
                last.then_inc(S["proj"], 1)

            def route(t):
                pe.wait_ge(S["h2"], t + 1)
                if t >= 1:
                    pe.wait_ge(S["h2T"], t)
                for k in range(KD):
                    last = nc.tensor.transpose(psH[:, k * P:(k + 1) * P], h2[:, t % 2, k * P:(k + 1) * P], ident[:, :])
                last.then_inc(S["h2turn"], 1)
                pe.wait_ge(S["h2T"], t + 1)
                pe.wait_ge(S["small_in"], 48)
                if t >= 1:
                    pe.wait_ge(S["logits_read"], t)
                for k in range(KD):
                    last = nc.tensor.matmul(psL[:, 0:NE], h2T[:, k, :], wr[:, k, :], start=(k == 0), stop=(k == KD - 1))
                last.then_inc(S["logits"], 1)

            for t in range(NT + 1):
                if t < NT:
                    project(t)
                if t >= 1:
                    route(t - 1)
            pe.wait_ge(S["mask"], 1)
            m = mask[:, :, :].rearrange("p t e -> p (t e)")
            nc.tensor.matmul(psR[:, 0:NT * NE], before[:, :], m, start=True, stop=True)
            nc.tensor.matmul(psR[:, NT * NE:2 * NT * NE], ones[:, :], m, start=True, stop=True).then_inc(S["ranks"], 1)

        @block.scalar
        def _(act):
            act.wait_ge(S["pool"], 2)
            act.wait_ge(S["vturn"], 1)
            nc.scalar.copy(vrow[:, :], psR[0:4 * KD, 0:P]).then_inc(S["vrow"], 1)
            sqn = kit.sem("e_sq")
            n = 0
            for t in range(NT):
                for src, done, out, j in ((psO[t % 2][:, :], "proj", "std1", 0), (x1[:, t % 2, :], "x1", "std2", 1)):
                    act.wait_ge(S[done], t + 1)
                    nc.scalar.activation(sq[:, j, :], src, ACT.Square, accum_out=st[:, t, 2 * j:2 * j + 1]).then_inc(sqn, 1)
                    n += 1
                    act.wait_ge(sqn, n)
                    nc.scalar.activation(st[:, t, 2 * j + 1:2 * j + 2], st[:, t, 2 * j:2 * j + 1], ACT.Sqrt, bias=eps[:, 0:1],
                                         scale=1.0 / D).then_inc(S[out], 1)
                act.wait_ge(S["h2turn"], t + 1)
                if t >= 1:
                    act.wait_ge(S["logits"], t)
                nc.scalar.copy(h2T[:, :, :].rearrange("p k t -> p (k t)"), psH[:, :]).then_inc(S["h2T"], 1)
            act.wait_ge(S["shifted"], 1)
            nc.scalar.activation(shifted[:, :, :], shifted[:, :, :], ACT.Exp).then_inc(S["exped"], 1)

        @block.vector
        def _(dve):
            link = linked(dve, S["vec"])
            dve.wait_ge(S["small_in"], 48)
            nc.vector.tensor_tensor(vcol[:, 0, :], modT[:, 2 * KD:3 * KD, 0], gains[:, 0, :], ALU.mult)
            link(nc.vector.tensor_scalar(vcol[:, 1, :], modT[:, 4 * KD:5 * KD, 0], 1.0, None, ALU.add))
            nc.vector.tensor_tensor(vcol[:, 1, :], vcol[:, 1, :], gains[:, 1, :], ALU.mult)
            nc.vector.tensor_copy(vcol[:, 2, :], modT[:, 3 * KD:4 * KD, 0])
            nc.vector.tensor_tensor(vcol[:, 3, :], modT[:, 5 * KD:6 * KD, 0], gains[:, 2, :], ALU.mult).then_inc(S["vcol"], 1)
            dve.wait_ge(S["rows_in"], 48)
            for t in range(NT):
                s = t % 2
                dve.wait_ge(S["std1"], t + 1)
                link(nc.vector.reciprocal(st[:, t, 1:2], st[:, t, 1:2]))
                if t >= 2:
                    dve.wait_ge(S[f"x1_out{s}"], 16 * (t // 2))
                link(nc.vector.scalar_tensor_tensor(x1[:, s, :], psO[s][:, :], st[:, t, 1:2], rows[:, 0, :], ALU.mult, ALU.mult))
                dve.wait_ge(S[f"x_in{s}"], 16 * (t // 2 + 1))
                nc.vector.tensor_tensor(x1[:, s, :], x1[:, s, :], xin[:, s, :], ALU.add).then_inc(S["x1"], 1)
                dve.wait_ge(S["std2"], t + 1)
                link(nc.vector.reciprocal(st[:, t, 3:4], st[:, t, 3:4]))
                if t >= 2:
                    dve.wait_ge(S[f"h2_out{s}"], 16 * (t // 2))
                link(nc.vector.scalar_tensor_tensor(h2[:, s, :], x1[:, s, :], st[:, t, 3:4], rows[:, 1, :], ALU.mult, ALU.mult))
                nc.vector.tensor_tensor(h2[:, s, :], h2[:, s, :], rows[:, 2, :], ALU.add).then_inc(S["h2"], 1)
                dve.wait_ge(S["logits"], t + 1)
                link(nc.vector.tensor_tensor(logit[:, :], psL[:, 0:NE], brt[:, :], ALU.add))
                dve.sem_inc(S["logits_read"], 1)
                link(nc.vector.max(top[:, t, :], logit[:, :]))
                link(nc.vector.max_index(topi[:, t, :], top[:, t, :], logit[:, :]))
            first = top[:, :, 0:1]
            nc.vector.tensor_tensor(shifted[:, :, :], top[:, :, 0:TOPK], bass.AP(first.tensor, first.offset, [first.ap[0], [8, NT], [0, TOPK]]),
                                    ALU.subtract).then_inc(S["shifted"], 1)
            link(nc.vector.tensor_copy(topf[:, :, :], topi[:, :, 0:TOPK]))
            tf, ln = topf[:, :, :], lanes[:, :]
            link(nc.vector.tensor_tensor(hot[:, :, :, :].rearrange("p t k e -> p (t k) e"),
                                         bass.AP(tf.tensor, tf.offset, [tf.ap[0], [1, NT * TOPK], [0, NE]]),
                                         bass.AP(ln.tensor, ln.offset, [ln.ap[0], [0, NT * TOPK], [1, NE]]), ALU.is_equal))
            nc.vector.tensor_reduce(mask[:, :, :], hot[:, :, :, :].rearrange("p t k e -> p t e k"), AXX, ALU.add).then_inc(S["mask"], 1)
            dve.wait_ge(S["exped"], 1)
            link(nc.vector.tensor_reduce(gsum[:, :], shifted[:, :, :], AXX, ALU.add))
            link(nc.vector.reciprocal(gsum[:, :], gsum[:, :]))
            gs = gsum[:, :]
            link(nc.vector.tensor_tensor(gate[:, :].rearrange("p (t k) -> p t k", k=TOPK), shifted[:, :, :],
                                         bass.AP(gs.tensor, gs.offset, [gs.ap[0], [1, NT], [0, TOPK]]), ALU.mult))
            dve.wait_ge(S["ranks"], 1)
            link(nc.vector.tensor_copy(place[:, :, :].rearrange("p t e -> p (t e)"), psR[:, 0:NT * NE]))
            link(nc.vector.memset(count[:, 0, :], 0.0))
            for t in range(NT):
                link(nc.vector.tensor_tensor(count[:, t + 1, :], count[:, t, :], psR[:, NT * NE + t * NE:NT * NE + (t + 1) * NE], ALU.add))
            link(nc.vector.tensor_scalar(blocks[:, :], count[:, NT, :], 1.0 / P, (P - 1) / (2.0 * P), ALU.mult, ALU.add))
            link(nc.vector.tensor_scalar(blocks[:, :], blocks[:, :], ROUND, -ROUND, ALU.add, ALU.add))
            link(nc.vector.memset(cum[:, :, :], 0.0))
            link(nc.vector.tensor_copy(cum[:, 0, 1:NE], blocks[:, 0:NE - 1]))
            cur, step = 0, 1
            while step < NE:
                nc.vector.tensor_copy(cum[:, 1 - cur, 0:step], cum[:, cur, 0:step])
                link(nc.vector.tensor_tensor(cum[:, 1 - cur, step:NE], cum[:, cur, step:NE], cum[:, cur, 0:NE - step], ALU.add))
                cur, step = 1 - cur, 2 * step
            nc.vector.tensor_copy(table[:, 0, :], blocks[0:1, :])
            nc.vector.tensor_copy(table[:, 1, :], cum[0:1, cur, :]).then_inc(S["table"], 1)
            c0 = cum[:, cur, :]
            link(nc.vector.tensor_tensor(place[:, :, :], place[:, :, :], count[:, 0:NT, :], ALU.add))
            link(nc.vector.scalar_tensor_tensor(place[:, :, :], bass.AP(c0.tensor, c0.offset, [c0.ap[0], [0, NT], [1, NE]]), float(P),
                                                place[:, :, :], ALU.mult, ALU.add))
            pl = place[:, :, :]
            link(nc.vector.tensor_tensor(hot[:, :, :, :], hot[:, :, :, :],
                                         bass.AP(pl.tensor, pl.offset, [pl.ap[0], [NE, NT], [0, TOPK], [1, NE]]), ALU.mult))
            link(nc.vector.tensor_reduce(destf[:, :, :], hot[:, :, :, :], AXX, ALU.add))
            nc.vector.tensor_copy(dest[:, :], destf[:, :, :].rearrange("p t k -> p (t k)")).then_inc(S["dest"], 1)


BPE = T // P
SLOTS = 2


def phase_experts(nc, kit, keep, io, dram):
    scope = ExitStack()
    with scope:
        table = keep["table"]
        gu = [kit.sb(scope, f"w_gate_up{i}", [P, KD, 2 * DE]) for i in range(SLOTS)]
        down = kit.sb(scope, "w_down", [P, DE // P, D])
        brow = kit.sb(scope, "expert_bias", [P, 2 * DE + D])
        xg = kit.sb(scope, "x_rows", [P, D])
        xT = kit.sb(scope, "x_rows_t", [P, KD, P])
        gated = kit.sb(scope, "gated", [P, 2, 512])
        sig = kit.sb(scope, "sig", [P, 2, 512])
        up = kit.sb(scope, "up", [P, 512])
        actT = kit.sb(scope, "act_t", [P, DE // P, P])
        blank = kit.sb(scope, "blank_rows", [P, D])
        yrow = kit.sb(scope, "y_rows", [P, D])
        rowtok = kit.sb(scope, "row_token", [P, NBLK], I32)
        idx = kit.sb(scope, "row_index", [P, 1], I32)
        ident = kit.sb(scope, "ident_f", [P, P])
        psT = kit.ps(scope, "psT", [P, 2, 512])
        psG = kit.ps(scope, "ps_gate_up", [P, 4, 512])
        psD = kit.ps(scope, "ps_down", [P, 2, 512])
        S = {n: kit.sem("f_" + n) for n in ("rowtok_in", "ident", "gu_in0", "gu_in1", "down_in", "bias_in", "index", "rows_in", "x_turned",
                                            "xT", "gate_up", "vec", "gate_ready", "sig", "act", "act_turned", "actT", "down", "y", "y_out", "blank", "blank_out", "stored",
                                            "gathers")}
        GU_DMAS = 4
        block = scope.enter_context(nc.Block())

        def blocks_of(eng, e):
            n = eng.value_load(table[0:1, 0, bass.ds(e, 1)], min_val=0, max_val=BPE)
            first = eng.value_load(table[0:1, 1, bass.ds(e, 1)], min_val=0, max_val=NBLK - 1)
            return n, first

        def blocks_in_all(eng):
            n, first = blocks_of(eng, NE - 1)
            return eng.snap(n + first)

        @block.sync
        def _(sp):
            def load_gate_up(e, slot):
                w = io["w_gate_up"][bass.ds(e, 1), :, :].rearrange("a (k p) n -> p (a k) n", p=P)
                step = KD // GU_DMAS
                for q in range(GU_DMAS):
                    sp.dma_start(gu[slot][:, q * step:(q + 1) * step, :], w[:, q * step:(q + 1) * step, :]).then_inc(S[f"gu_in{slot}"], 16)

            def load_rest(e):
                _, first = blocks_of(sp, e)
                sp.wait_ge(S["y"], first + 1)
                for src, at, n in ((io["b_gate_up"], 0, 2 * DE), (io["b_down"], 2 * DE, D)):
                    b = src[bass.ds(e, 1), :]
                    sp.dma_start(brow[:, at:at + n], b.broadcast_to([P, n])).then_inc(S["bias_in"], 16)
                w = io["w_down"][bass.ds(e, 1), :, :].rearrange("a (k p) n -> p (a k) n", p=P)
                for q in range(2):
                    sp.dma_start(down[:, 4 * q:4 * q + 4, :], w[:, 4 * q:4 * q + 4, :]).then_inc(S["down_in"], 16)

            load_gate_up(0, 0)
            with sp.Fori(0, NE // 2 - 1) as i:
                for slot in range(SLOTS):
                    e = sp.snap(i * 2 + slot)
                    load_rest(e)
                    load_gate_up(sp.snap(i * 2 + slot + 1), 1 - slot)
            load_rest(NE - 2)
            load_gate_up(NE - 1, 1)
            load_rest(NE - 1)

        @block.gpsimd
        def _(pool):
            identity(nc, pool, ident, S["ident"])
            nc.gpsimd.memset(blank[:, :], 0.0).then_inc(S["blank"], 1)
            pool.dma_start(rowtok[:, :], dram["row_token"].rearrange("(b p) o -> p (b o)", p=P),
                           allow_slow_non_contiguous=True).then_inc(S["rowtok_in"], 16)
            pool.wait_ge(S["rowtok_in"], 16)
            total = blocks_in_all(pool)
            with pool.Fori(0, NBLK) as g:
                with pool.If(g < total):
                    pool.wait_ge(S["x_turned"], g + 1)
                    nc.gpsimd.tensor_copy(idx[:, :], rowtok[:, bass.ds(g, 1)]).then_inc(S["index"], 1)
                    pool.wait_ge(S["index"], g + 1)
                    pool.sem_inc(S["gathers"], 1)
                    pool.indirect_dma_start(out=xg[:, :], out_offset=None, in_=dram["h2"],
                                            in_offset=bass.IndirectOffsetOnAxis(ap=idx[:, 0:1], axis=0)).then_inc(S["rows_in"], 16)

        @block.tensor
        def _(pe):
            pe.sem_inc(S["x_turned"], 1)
            pe.wait_ge(S["ident"], 2)

            def one_block(i, slot, g):
                pe.wait_ge(S["rows_in"], g * 16 + 16)
                for k in range(KD):
                    last = nc.tensor.transpose(psT[:, k // 4, (k % 4) * P:(k % 4 + 1) * P], xg[:, k * P:(k + 1) * P], ident[:, :])
                last.then_inc(S["x_turned"], 1)
                pe.wait_ge(S[f"gu_in{slot}"], i * (16 * GU_DMAS) + 16 * GU_DMAS)
                pe.wait_ge(S["xT"], g + 1)
                for half in range(2):
                    for what in range(2):
                        col = what * DE + half * 512
                        for k in range(KD):
                            last = nc.tensor.matmul(psG[:, 2 * half + what, :], xT[:, k, :], gu[slot][:, k, col:col + 512],
                                                    start=(k == 0), stop=(k == KD - 1))
                        last.then_inc(S["gate_up"], 1)
                for half in range(2):
                    pe.wait_ge(S["act"], g * 2 + half + 1)
                    for k in range(4):
                        last = nc.tensor.transpose(psT[:, half, k * P:(k + 1) * P], gated[:, half, k * P:(k + 1) * P], ident[:, :])
                    last.then_inc(S["act_turned"], 1)
                    pe.wait_ge(S["actT"], g * 2 + half + 1)
                    if half == 0:
                        pe.wait_ge(S["down_in"], i * 64 + 32 * (slot + 1))
                        pe.wait_ge(S["y"], g + 1)
                    for n in range(2):
                        for k in range(4 * half, 4 * half + 4):
                            last = nc.tensor.matmul(psD[:, n, :], actT[:, k, :], down[:, k, n * 512:(n + 1) * 512],
                                                    start=(k == 0), stop=(k == KD - 1))
                last.then_inc(S["down"], 1)

            with pe.Fori(0, NE // 2) as i:
                for slot in range(SLOTS):
                    n, first = blocks_of(pe, pe.snap(i * 2 + slot))
                    with pe.Fori(0, BPE) as b:
                        with pe.If(b < n):
                            one_block(i, slot, pe.snap(first + b))

        @block.scalar
        def _(act):
            total = blocks_in_all(act)
            act.sem_inc(S["y_out"], 16)
            act.wait_ge(S["blank"], 1)
            with act.Fori(0, NBLK) as g:
                with act.If(g >= total):
                    act.dma_start(dram["y"][bass.ds(g * P, P), :], blank[:, :]).then_inc(S["blank_out"], 16)
                with act.Else():
                    act.sem_inc(S["blank_out"], 16)
            with act.Fori(0, NBLK) as g:
                with act.If(g < total):
                    act.wait_ge(S["x_turned"], g + 2)
                    nc.scalar.copy(xT[:, :, :].rearrange("p k t -> p (k t)"), psT[:, :, :].rearrange("p a b -> p (a b)")).then_inc(S["xT"], 1)
                    for half in range(2):
                        act.wait_ge(S["gate_ready"], g * 2 + half + 1)
                        nc.scalar.activation(sig[:, half, :], gated[:, half, :], ACT.Sigmoid, scale=ALPHA).then_inc(S["sig"], 1)
                    for half in range(2):
                        act.wait_ge(S["act_turned"], g * 2 + half + 1)
                        nc.scalar.copy(actT[:, 4 * half:4 * half + 4, :].rearrange("p k t -> p (k t)"), psT[:, half, :]).then_inc(S["actT"], 1)
                    act.wait_ge(S["y"], g + 2)
                    act.dma_start(dram["y"][bass.ds(g * P, P), :], yrow[:, :]).then_inc(S["y_out"], 16)
            act.wait_ge(S["y_out"], total * 16 + 16)
            act.sem_inc(S["stored"], 1)
            act.wait_ge(S["blank_out"], NBLK * 16)
            act.sem_inc(S["stored"], 1)

        @block.vector
        def _(dve):
            STEPS = 12
            dve.sem_inc(S["y"], 1)

            def one_block(i, slot, g):
                done = [0]

                def link(ins):
                    done[0] += 1
                    ins.then_inc(S["vec"], 1)
                    dve.wait_ge(S["vec"], g * STEPS + done[0])

                dve.wait_ge(S["bias_in"], i * 64 + 32 * (slot + 1))
                for half in range(2):
                    c = half * 512
                    dve.wait_ge(S["gate_up"], g * 4 + 2 * half + 1)
                    link(nc.vector.tensor_tensor(gated[:, half, :], psG[:, 2 * half, :], brow[:, c:c + 512], ALU.add))
                    link(nc.vector.tensor_scalar(gated[:, half, :], gated[:, half, :], LIMIT, None, ALU.min))
                    dve.sem_inc(S["gate_ready"], 1)
                    dve.wait_ge(S["gate_up"], g * 4 + 2 * half + 2)
                    link(nc.vector.tensor_tensor(up[:, :], psG[:, 2 * half + 1, :], brow[:, DE + c:DE + c + 512], ALU.add))
                    link(nc.vector.tensor_scalar(up[:, :], up[:, :], LIMIT, -LIMIT, ALU.min, ALU.max))
                    dve.wait_ge(S["sig"], g * 2 + half + 1)
                    link(nc.vector.scalar_tensor_tensor(up[:, :], up[:, :], 1.0, gated[:, half, :], ALU.add, ALU.mult))
                    link(nc.vector.tensor_tensor(gated[:, half, :], up[:, :], sig[:, half, :], ALU.mult))
                    dve.sem_inc(S["act"], 1)
                dve.wait_ge(S["down"], g + 1)
                dve.wait_ge(S["y_out"], g * 16 + 16)
                nc.vector.tensor_tensor(yrow[:, :], psD[:, :, :].rearrange("p a b -> p (a b)"), brow[:, 2 * DE:], ALU.add).then_inc(S["y"], 1)
                assert done[0] == STEPS

            with dve.Fori(0, NE // 2) as i:
                for slot in range(SLOTS):
                    n, first = blocks_of(dve, dve.snap(i * 2 + slot))
                    with dve.Fori(0, BPE) as b:
                        with dve.If(b < n):
                            one_block(i, slot, dve.snap(first + b))


def phase_combine(nc, kit, keep, io, dram, out):
    scope = ExitStack()
    with scope:
        dest, gate = keep["dest"], keep["gate"]
        rows = kit.sb(scope, "g2_row", [P, D])
        yk = kit.sb(scope, "y_of_token", [P, 3, TOPK, D])
        x1 = kit.sb(scope, "x1_again", [P, 2, D])
        f = kit.sb(scope, "ffn_sum", [P, 2, D])
        sq = kit.sb(scope, "ffn_squares", [P, 2, D])
        o = kit.sb(scope, "out_tile", [P, 2, D])
        st = kit.sb(scope, "ffn_stat", [P, NT, 2])
        eps = kit.sb(scope, "eps_g", [P, 1])
        S = {n: kit.sem("g_" + n) for n in ("row_in", "eps", "x_in0", "x_in1", "y_in0", "y_in1", "y_in2", "vec", "summed", "sq", "std", "ready",
                                            "out0", "out1")}
        block = scope.enter_context(nc.Block())

        @block.sync
        def _(sp):
            sp.dma_start(rows[:, :], row_of(dram["vectors"], D, 3 * D)).then_inc(S["row_in"], 16)
            for t in range(NT):
                if t >= 2:
                    sp.wait_ge(S["ready"], t - 1)
                sp.dma_start(x1[:, t % 2, :], dram["x1"][t * P:(t + 1) * P, :]).then_inc(S[f"x_in{t % 2}"], 16)

        @block.gpsimd
        def _(pool):
            nc.gpsimd.memset(eps[:, :], EPS).then_inc(S["eps"], 1)
            for t in range(NT):
                if t >= 3:
                    pool.wait_ge(S["summed"], t - 2)
                for k in range(TOPK):
                    pool.indirect_dma_start(out=yk[:, t % 3, k, :], out_offset=None, in_=dram["y"],
                                            in_offset=bass.IndirectOffsetOnAxis(ap=dest[:, t * TOPK + k:t * TOPK + k + 1], axis=0)
                                            ).then_inc(S[f"y_in{t % 3}"], 16)

        @block.scalar
        def _(act):
            act.wait_ge(S["eps"], 1)
            for t in range(NT):
                act.wait_ge(S["summed"], t + 1)
                if t >= 2:
                    act.wait_ge(S["sq"], t - 1)
                nc.scalar.activation(sq[:, t % 2, :], f[:, t % 2, :], ACT.Square, accum_out=st[:, t, 0:1]).then_inc(S["sq"], 1)
                act.wait_ge(S["sq"], t + 1)
                nc.scalar.activation(st[:, t, 1:2], st[:, t, 0:1], ACT.Sqrt, bias=eps[:, 0:1], scale=1.0 / D).then_inc(S["std"], 1)
                act.wait_ge(S["ready"], t + 1)
                act.dma_start(out[t * P:(t + 1) * P, :], o[:, t % 2, :]).then_inc(S[f"out{t % 2}"], 16)
            for i in range(2):
                act.wait_ge(S[f"out{i}"], 16 * NT // 2)

        @block.vector
        def _(dve):
            link = linked(dve, S["vec"])
            dve.wait_ge(S["row_in"], 16)
            for t in range(NT):
                dve.wait_ge(S[f"y_in{t % 3}"], 16 * TOPK * (t // 3 + 1))
                ft = f[:, t % 2, :]
                link(nc.vector.tensor_scalar(ft, yk[:, t % 3, 0, :], gate[:, t * TOPK:t * TOPK + 1], None, ALU.mult))
                for k in range(1, TOPK):
                    link(nc.vector.scalar_tensor_tensor(ft, yk[:, t % 3, k, :], gate[:, t * TOPK + k:t * TOPK + k + 1], ft, ALU.mult, ALU.add))
                dve.sem_inc(S["summed"], 1)
                dve.wait_ge(S["std"], t + 1)
                link(nc.vector.reciprocal(st[:, t, 1:2], st[:, t, 1:2]))
                if t >= 2:
                    dve.wait_ge(S[f"out{t % 2}"], 16 * (t // 2))
                link(nc.vector.scalar_tensor_tensor(o[:, t % 2, :], ft, st[:, t, 1:2], rows[:, :], ALU.mult, ALU.mult))
                dve.wait_ge(S[f"x_in{t % 2}"], 16 * (t // 2 + 1))
                nc.vector.tensor_tensor(o[:, t % 2, :], o[:, t % 2, :], x1[:, t % 2, :], ALU.add).then_inc(S["ready"], 1)


def attention_constants():
    q = np.arange(GRID_W)
    lo = np.clip(q - NA_COLS // 2, 0, GRID_W - NA_COLS)
    inside = (q[None, :] >= lo[:, None]) & (q[None, :] < lo[:, None] + NA_COLS)
    m = np.where(inside, 0.0, MASKED).astype(np.float32)
    return {"na_col_mask": np.concatenate([m, m])}


def build_layer(nc, io, out):
    top = ExitStack()
    with top:
        kit = Kit(nc, top)
        dram = {
            "vectors": nc.dram_tensor("vectors_dram", [4 * D], F32, kind="Internal").ap(),
            "x1": nc.dram_tensor("x1_dram", [T, D], F32, kind="Internal").ap(),
            "h2": nc.dram_tensor("h2_dram", [T, D], F32, kind="Internal").ap(),
            "row_token": nc.dram_tensor("row_token_dram", [NROW, 1], I32, kind="Internal").ap(),
            "y": nc.dram_tensor("y_dram", [NROW, D], F32, kind="Internal").ap(),
        }
        keep = {"dest": kit.sb(top, "dest", [P, NT * TOPK], I32), "gate": kit.sb(top, "gate", [P, NT * TOPK]),
                "table": kit.sb(top, "table", [1, 2, NE], I32)}
        with ExitStack() as mixed:
            keep["modT"] = kit.sb(mixed, "modT", [P, 6 * KD, 2])
            keep["hT"] = keep["mixT"] = kit.sb(mixed, "hT_mixT", [P, KD, TA])
            with ExitStack() as convolved:
                keep["hyT"] = kit.sb(convolved, "hyT", [P, NHT, T])
                with ExitStack() as scanned:
                    keep["xbcT"] = kit.sb(scanned, "xbcT", [P, NXT, TA])
                    keep["z"] = kit.sb(scanned, "z", [P, NT, SSD_W])
                    keep["dt"] = kit.sb(scanned, "dt", [P, NT + NTC, 2 * SSD_H])
                    with ExitStack() as attended:
                        keep["qT"] = kit.sb(attended, "qT", [P, NQT, T])
                        keep["kT"] = kit.sb(attended, "kT", [P, NQT, TA])
                        keep["v"] = kit.sb(attended, "v", [P, NT + NTC, NA_W])
                        phase_project(nc, kit, keep, io)
                        phase_attention(nc, kit, keep, io)
                    phase_ssd(nc, kit, keep, io)
                kit.recycle()
                phase_hyena(nc, kit, keep, io)
            phase_mix(nc, kit, keep, io, dram)
        kit.recycle()
        phase_experts(nc, kit, keep, io, dram)
        phase_combine(nc, kit, keep, io, dram, out)


def lay_out(x, c, ctx, c_ctx, w_mod, b_mod, norm_g, w_in, ssd_conv_w, ssd_conv_b, ssd_a_log, ssd_dt_bias, ssd_d, ssd_norm_g, na_rpb,
            hy_conv_w, hy_conv_b, hy_f_w1, hy_f_b1, hy_f_w2, hy_f_b2, hy_f_w3, hy_freq, hy_d, w_out, w_router, b_router, w_gate_up,
            b_gate_up, w_down, b_down):
    def col(a):
        return a.reshape(-1, P).T

    def cols(a):
        return a.T.reshape(-1, P, a.shape[0]).transpose(1, 0, 2)

    rpb = np.zeros((NA_H, 2 * NA_ROWS + 1, 2 * GRID_W - 1), np.float32)
    rpb[:, 1:2 * NA_ROWS, GRID_W - NA_COLS:GRID_W + NA_COLS - 1] = na_rpb[0].transpose(2, 0, 1)
    skewed = np.stack([rpb[:, 1 - half:1 - half + 2 * NA_ROWS, GRID_W - 1 - qc:2 * GRID_W - 1 - qc]
                       for half in range(2) for qc in range(GRID_W)])
    g = norm_g[0]
    hy_b = np.stack([hy_f_b1[0], hy_f_b2[0]], -1)
    a = {
        "x": x[0], "x_t": x[0].T, "ctx_t": ctx[0].T, "w_mod": w_mod[0], "w_in": w_in[0],
        "c_col": np.stack([col(c[0]), col(c_ctx)], -1), "b_mod_col": col(b_mod[0]), "gain0_col": col(g[0]),
        "gains_col": g[1:].reshape(3, KD, P).transpose(2, 0, 1),
        "ssd_conv_col": cols(np.concatenate([ssd_conv_w[0], ssd_conv_b])),
        "hy_conv_col": cols(np.concatenate([hy_conv_w[0], hy_conv_b])),
        "rpb_skewed": skewed, "dt_bias": ssd_dt_bias[0].reshape(-1), "a_log": ssd_a_log[0].reshape(-1), "ssd_d": ssd_d[0],
        "ssd_norm_col": col(ssd_norm_g[0]),
        "hy_f_w1": hy_f_w1[0], "hy_f_w2": hy_f_w2[0], "hy_f_w3": hy_f_w3[0],
        "hy_bias_freq": np.stack([hy_b, hy_freq[0].T], -1), "hy_d": hy_d,
        "w_out": w_out[0], "w_router": w_router[0], "b_router": b_router[0], "w_gate_up": w_gate_up[0], "b_gate_up": b_gate_up[0],
        "w_down": w_down[0], "b_down": b_down[0],
    }
    return {**a, **hyena_constants(), **attention_constants()}


def kernel(**inputs):
    import concourse.bacc as bacc
    from concourse.bass_utils import run_bass_kernel_spmd

    nc = bacc.Bacc("TRN2", target_bir_lowering=False, num_devices=1)
    arrays, io = {}, {}
    for name, a in lay_out(**{k: np.asarray(v) for k, v in inputs.items()}).items():
        a = np.ascontiguousarray(a)
        arrays[f"in_{name}"] = a
        io[name] = nc.dram_tensor(f"in_{name}", a.shape, mybir.dt.from_np(a.dtype), kind="ExternalInput").ap()
    out = nc.dram_tensor("out_0", (1, T, D), F32, kind="ExternalOutput").ap()
    build_layer(nc, io, out[0])
    r = run_bass_kernel_spmd(nc, [arrays], core_ids=[0])
    return r.results[0]["out_0"]
```

```python
import numpy as np
import concourse.bass as bass
from concourse import mybir
from contextlib import ExitStack


F32 = mybir.dt.float32
I32 = mybir.dt.int32
U32 = mybir.dt.uint32
ALU = mybir.AluOpType
ACT = mybir.ActivationFunctionType
AXX = mybir.AxisListType.X

P = 128
D = 1024
T = 1024
TC = 256
TA = T + TC
KD = D // P
NT, NTC = T // P, TC // P
EPS = 1e-6
SSD_H, HD, NGRP, NST, SSD_W = 6, 64, 2, 128, 384
GW = SSD_W // NGRP
XBC = SSD_W + 2 * NGRP * NST
NA_W, HY_W = 384, 256
OFF_XBC = SSD_W
OFF_DT = OFF_XBC + XBC
OFF_Q = OFF_DT + 2 * SSD_H
OFF_K, OFF_V = OFF_Q + NA_W, OFF_Q + 2 * NA_W
OFF_HY = OFF_V + NA_W
NXT, NQT, NHT = XBC // P, NA_W // P, 3 * HY_W // P
NXT_CTX = (SSD_W + NGRP * NST) // P
SSD_K, HY_K = 5, 3
NE, TOPK, DE = 32, 4, 1024
LIMIT, ALPHA = 7.0, 1.702


class Kit:

    def __init__(self, nc, top):
        self.nc, self.top, self.sems = nc, top, []

    def sem(self, name):
        self.sems.append(self.nc.alloc_semaphore(name=name))
        return self.sems[-1]

    def recycle(self):
        self.nc.clear_and_free_semaphores(self.sems)
        self.nc.all_engine_barrier()
        self.sems = []

    def sb(self, scope, name, shape, dt=F32, side=None):
        return scope.enter_context(self.nc.sbuf_tensor("sb_" + name, shape, dt, side=side))

    def ps(self, scope, name, shape):
        return scope.enter_context(self.nc.psum_tensor(name, shape, F32))


def linked(eng, sem):
    n = [0]

    def link(ins):
        n[0] += 1
        ins.then_inc(sem, 1)
        eng.wait_ge(sem, n[0])

    return link


def phase_project(nc, kit, keep, io):
    scope = ExitStack()
    with scope:
        hT = keep["hT"]
        ring = kit.sb(scope, "w_ring", [P, 4, KD, 2 * P])
        wtok = kit.sb(scope, "w_tok", [P, KD, NA_W + 2 * SSD_H])
        rstd = kit.sb(scope, "rstd", [P, TA])
        ccol = kit.sb(scope, "c_col", [P, KD, 2])
        scol = kit.sb(scope, "silu_c_col", [P, KD, 2])
        bmod = kit.sb(scope, "b_mod_col", [P, 6 * KD])
        gcol = kit.sb(scope, "gain0_col", [P, KD])
        amul = kit.sb(scope, "norm_scale_col", [P, KD, 2])
        cw = kit.sb(scope, "ssd_conv_col", [P, NXT, SSD_K + 1])
        hw = kit.sb(scope, "hy_conv_col", [P, NHT, HY_K + 1])
        ones = kit.sb(scope, "ones_a", [P, P])
        eps = kit.sb(scope, "eps_a", [P, 1])
        modT, xbcT, qT, kT, hyT = keep["modT"], keep["xbcT"], keep["qT"], keep["kT"], keep["hyT"]
        v, z, dt = keep["v"], keep["z"], keep["dt"]
        acc = [kit.ps(scope, f"acc{i}", [P, 1536]) for i in range(2)]
        pmod = kit.ps(scope, "pmod", [P, 512])

        small_in = kit.sem("a_small_in")
        x_in = [kit.sem(f"a_x_in{k}") for k in range(KD)]
        ring_in = [kit.sem(f"a_ring_in{i}") for i in range(4)]
        ring_used = kit.sem("a_ring_used")
        wtok_in = kit.sem("a_wtok_in")
        consts = kit.sem("a_consts")
        silu_done = kit.sem("a_silu_done")
        sq_done = kit.sem("a_sq_done")
        sq_used = kit.sem("a_sq_used")
        ssq_done = kit.sem("a_ssq_done")
        std_done = kit.sem("a_std_done")
        h_done = kit.sem("a_h_done")
        tile_done = kit.sem("a_tile_done")
        tile_convolved = kit.sem("a_tile_convolved")
        tile_copied = kit.sem("a_tile_copied")
        conv_done = kit.sem("a_conv_done")
        silu_x = kit.sem("a_silu_x")
        vec = kit.sem("a_vec")

        n_mod1 = 2 * KD // 2
        n_mod = 6 * KD // 2
        chan = [("x", m, OFF_XBC + m * P) for m in range(NXT)]
        chan += [("h", m, OFF_HY + m * P) for m in range(NHT)]
        chan += [("q", m, OFF_Q + m * P) for m in range(NQT)] + [("k", m, OFF_K + m * P) for m in range(NQT)]
        loads = [("mod", m) for m in range(n_mod1)] + [("in", c) for c in range(len(chan))]
        loads += [("mod", m) for m in range(n_mod1, n_mod)]
        tok = [("v", t) for t in range(NT + NTC)] + [("z", t) for t in range(NT + NTC)]
        wmod = io["w_mod"].rearrange("(k p) n -> p k n", p=P)
        win = io["w_in"].rearrange("(k p) n -> p k n", p=P)

        n_conv = NXT + NHT

        def accumulator_free(pe, n):
            if n - 2 >= n_conv:
                pe.wait_ge(tile_copied, n - 2 - n_conv + 1)
            elif n >= 2:
                pe.wait_ge(tile_convolved, n - 1)

        def has_ctx(c):
            kind, m, _ = chan[c]
            return kind == "k" or (kind == "x" and m < NXT_CTX)

        block = scope.enter_context(nc.Block())

        @block.sync
        def _(sp):
            sp.dma_start(ccol[:, :, :], io["c_col"]).then_inc(small_in, 16)
            sp.dma_start(bmod[:, :], io["b_mod_col"]).then_inc(small_in, 16)
            sp.dma_start(gcol[:, :], io["gain0_col"]).then_inc(small_in, 16)
            sp.dma_start(cw[:, :, :], io["ssd_conv_col"]).then_inc(small_in, 16)
            sp.dma_start(hw[:, :, :], io["hy_conv_col"]).then_inc(small_in, 16)
            for n, (kind, m) in enumerate(loads):
                if n >= 4:
                    sp.wait_ge(ring_used, n - 3)
                if kind == "mod":
                    sp.dma_start(ring[:, n % 4, :, :], wmod[:, :, 2 * P * m:2 * P * (m + 1)]).then_inc(ring_in[n % 4], 16)
                else:
                    off = chan[m][2]
                    sp.dma_start(ring[:, n % 4, :, 0:P], win[:, :, off:off + P]).then_inc(ring_in[n % 4], 16)
                if n == 3:
                    for k in range(KD):
                        sp.dma_start(hT[:, k, 0:T], io["x_t"][k * P:(k + 1) * P, :]).then_inc(x_in[k], 16)
                        sp.dma_start(hT[:, k, T:TA], io["ctx_t"][k * P:(k + 1) * P, :]).then_inc(x_in[k], 16)
                    sp.dma_start(wtok[:, :, 0:NA_W], win[:, :, OFF_V:OFF_V + NA_W]).then_inc(wtok_in, 16)
            sp.wait_ge(tile_done, NT + NTC)
            sp.dma_start(wtok[:, :, 0:SSD_W], win[:, :, 0:SSD_W]).then_inc(wtok_in, 16)
            sp.dma_start(wtok[:, :, SSD_W:], win[:, :, OFF_DT:OFF_Q]).then_inc(wtok_in, 16)

        @block.gpsimd
        def _(pool):
            nc.gpsimd.memset(ones[:, :], 1.0).then_inc(consts, 1)
            nc.gpsimd.memset(eps[:, :], EPS).then_inc(consts, 1)

        @block.tensor
        def _(pe):
            n = 0

            def mod_tiles(n, m):
                for h in range(2):
                    for k in range(KD):
                        last = nc.tensor.matmul(pmod[:, 2 * (2 * m + h):2 * (2 * m + h) + 2], ring[:, n % 4, k, h * P:(h + 1) * P],
                                                scol[:, k, :], start=(k == 0), stop=(k == KD - 1))
                last.then_inc(ring_used, 1)
                return last

            pe.wait_ge(silu_done, 1)
            used = [0, 0, 0, 0]
            tiles = 0
            for n, (kind, m) in enumerate(loads):
                used[n % 4] += 16
                pe.wait_ge(ring_in[n % 4], used[n % 4])
                if kind == "mod":
                    mod_tiles(n, m)
                    if m == n_mod1 - 1:
                        pe.wait_ge(consts, 2)
                        for k in range(KD):
                            pe.wait_ge(sq_done, k + 1)
                            for a, b in ((0, 512), (512, 1024), (1024, TA)):
                                last = nc.tensor.matmul(acc[0][:, a:b], ones[:, :], xbcT[:, k % 4, a:b],
                                                        start=(k == 0), stop=(k == KD - 1), skip_group_check=True)
                            last.then_inc(sq_used, 1)
                else:
                    if tiles == 0:
                        pe.wait_ge(h_done, 2 * KD)
                    accumulator_free(pe, tiles)
                    a = acc[tiles % 2]
                    for k in range(KD):
                        lhs = ring[:, n % 4, k, 0:P]
                        for lo, hi in ((0, 512), (512, 1024)) + (((1024, TA),) if has_ctx(m) else ()):
                            last = nc.tensor.matmul(a[:, lo:hi], lhs, hT[:, k, lo:hi], start=(k == 0), stop=(k == KD - 1),
                                                    skip_group_check=True)
                    last.then_inc(ring_used, 1)
                    tiles += 1
            for i, (kind, t) in enumerate(tok):
                if i == 0:
                    pe.wait_ge(wtok_in, 16)
                if kind == "z" and t == 0:
                    pe.wait_ge(wtok_in, 48)
                accumulator_free(pe, tiles)
                a = acc[tiles % 2]
                lo, hi = (0, NA_W) if kind == "v" else (0 if t < NT else SSD_W, NA_W + 2 * SSD_H)
                for k in range(KD):
                    last = nc.tensor.matmul(a[:, lo:hi], hT[:, k, t * P:(t + 1) * P], wtok[:, k, lo:hi],
                                            start=(k == 0), stop=(k == KD - 1))
                last.then_inc(tile_done, 1)
                tiles += 1

        n_before = n_mod1

        @block.scalar
        def _(act):
            act.wait_ge(small_in, 80)
            nc.scalar.activation(scol[:, :, :], ccol[:, :, :], ACT.Silu).then_inc(silu_done, 1)
            for k in range(KD):
                act.wait_ge(x_in[k], 32)
                if k >= 4:
                    act.wait_ge(sq_used, k - 3)
                nc.scalar.activation(xbcT[:, k % 4, :], hT[:, k, :], ACT.Square).then_inc(sq_done, 1)
            act.wait_ge(sq_used, KD)
            act.wait_ge(consts, 2)
            nc.scalar.activation(rstd[:, :], acc[0][:, 0:TA], ACT.Sqrt, bias=eps[:, 0:1], scale=1.0 / D).then_inc(std_done, 1)
            for c, (kind, m, _) in enumerate(chan):
                if kind == "x":
                    act.wait_ge(conv_done, m + 1)
                    hi = TA if has_ctx(c) else T
                    nc.scalar.activation(xbcT[:, m, 0:hi], xbcT[:, m, 0:hi], ACT.Silu).then_inc(silu_x, 1)
                elif kind in "qk":
                    act.wait_ge(ring_used, n_before + c + 1)
                    dst = qT[:, m, :] if kind == "q" else kT[:, m, :]
                    nc.scalar.copy(dst, acc[c % 2][:, 0:(T if kind == "q" else TA)]).then_inc(tile_copied, 1)
            for i, (kind, t) in enumerate(tok):
                a = acc[(len(chan) + i) % 2]
                act.wait_ge(tile_done, i + 1)
                if kind == "v":
                    nc.scalar.copy(v[:, t, :], a[:, 0:NA_W]).then_inc(tile_copied, 1)
                else:
                    if t < NT:
                        nc.scalar.copy(z[:, t, :], a[:, 0:SSD_W]).then_inc(silu_x, 1)
                    nc.scalar.copy(dt[:, t, :], a[:, SSD_W:SSD_W + 2 * SSD_H]).then_inc(tile_copied, 1)

        @block.vector
        def _(dve):
            link = linked(dve, vec)
            dve.wait_ge(small_in, 80)

            def add_mod_bias(lo, hi):
                pm = pmod[:, 2 * lo:2 * hi].rearrange("p (m s) -> p m s", s=2)
                for s in range(2):
                    link(nc.vector.tensor_tensor(modT[:, lo:hi, s], pm[:, :, s], bmod[:, lo:hi], ALU.add))

            dve.wait_ge(ring_used, n_mod1)
            add_mod_bias(0, 2 * KD)
            for s in range(2):
                link(nc.vector.tensor_scalar(amul[:, :, s], modT[:, KD:2 * KD, s], 1.0, None, ALU.add))
                link(nc.vector.tensor_tensor(amul[:, :, s], amul[:, :, s], gcol[:, :], ALU.mult))
            dve.wait_ge(std_done, 1)
            link(nc.vector.reciprocal(rstd[:, :], rstd[:, :]))
            for s, (lo, hi) in enumerate(((0, T), (T, TA))):
                for k in range(KD):
                    h = hT[:, k, lo:hi]
                    link(nc.vector.scalar_tensor_tensor(h, h, amul[:, k, s:s + 1], rstd[:, lo:hi], ALU.mult, ALU.mult))
                    nc.vector.tensor_scalar(h, h, modT[:, k, s:s + 1], None, ALU.add).then_inc(h_done, 1)

            def conv(dst, src, w, taps):
                mid, width = taps // 2, src.shape[-1]
                link(nc.vector.tensor_scalar(dst, src, w[:, mid:mid + 1], w[:, taps:taps + 1], ALU.mult, ALU.add))
                for j in [j for j in range(taps) if j != mid]:
                    s = j - mid
                    o, i = (dst[:, 0:width - s], src[:, s:width]) if s > 0 else (dst[:, -s:width], src[:, 0:width + s])
                    last = nc.vector.scalar_tensor_tensor(o, i, w[:, j:j + 1], o, ALU.mult, ALU.add)
                    link(last)

            for c, (kind, m, _) in enumerate(chan):
                if kind == "x" or kind == "h":
                    dve.wait_ge(ring_used, n_before + c + 1)
                    a = acc[c % 2]
                    if kind == "x":
                        if has_ctx(c):
                            conv(xbcT[:, m, T:TA], a[:, T:TA], cw[:, m, :], SSD_K)
                        conv(xbcT[:, m, 0:T], a[:, 0:T], cw[:, m, :], SSD_K)
                        dve.sem_inc(conv_done, 1)
                    else:
                        conv(hyT[:, m, :], a[:, 0:T], hw[:, m, :], HY_K)
                    dve.sem_inc(tile_convolved, 1)
            dve.wait_ge(ring_used, len(loads))
            add_mod_bias(2 * KD, 6 * KD)


GRID_W, ROWS, NA_ROWS, NA_COLS, NA_H = 64, T // 64, 8, 16, 6
MASKED = -1e30


def identity(nc, pool, tile, sem):
    nc.gpsimd.memset(tile[:, :], 0.0).then_inc(sem, 1)
    pool.wait_ge(sem, 1)
    nc.gpsimd.affine_select(out=tile[:, :], in_=tile[:, :], compare_op=ALU.not_equal, fill=1.0, base=0,
                            pattern=[[-1, P]], channel_multiplier=1).then_inc(sem, 1)


def phase_attention(nc, kit, keep, io):
    scope = ExitStack()
    with scope:
        qT, kT, v, mixT = keep["qT"], keep["kT"], keep["v"], keep["mixT"]
        NS = 2 * NA_ROWS
        bias = kit.sb(scope, "na_bias", [P, NA_H, NS, GRID_W])
        cmask = kit.sb(scope, "na_col_mask", [P, GRID_W])
        ident = kit.sb(scope, "ident_na", [P, P])
        probs = kit.sb(scope, "na_probs", [P, 2, 832])
        pT = kit.sb(scope, "na_probs_t", [P, 2, 7, P])
        y = kit.sb(scope, "na_y", [P, NT, NA_W])
        items = [(m, h) for m in range(NT) for h in range(NA_H)]
        NI = len(items)
        mx = kit.sb(scope, "na_max", [P, NI, 4])
        sm = kit.sb(scope, "na_sum", [P, NI, 4])
        score = [kit.ps(scope, f"na_score{i}", [P, 1024]) for i in range(2)]
        trA = kit.ps(scope, "na_trA", [P, 512])
        trB = kit.ps(scope, "na_trB", [P, 512])
        out = [kit.ps(scope, f"na_out{i}", [P, 512]) for i in range(2)]
        S = {n: kit.sem("n_" + n) for n in ("bias_in", "mask_in", "ident", "bias_ready", "scored", "max_ready", "exped", "trA_done",
                                            "trB_done", "evA", "evB", "pv", "y_ready", "vec", "mtA", "mtB", "mcA", "mcB")}
        CTX0 = 576

        def key_rows(m):
            first = max(0, min(2 * m - NA_ROWS // 2, ROWS - NA_ROWS))
            return first, (9 if 2 * m - 4 >= 0 and 2 * m - 3 <= ROWS - NA_ROWS else 8)

        block = scope.enter_context(nc.Block())

        @block.sync
        def _(sp):
            sp.dma_start(cmask[:, :], io["na_col_mask"]).then_inc(S["mask_in"], 16)
            for h in range(NA_H):
                sp.dma_start(bias[:, h, :, :], io["rpb_skewed"][:, h, :, :]).then_inc(S["bias_in"], 16)

        @block.gpsimd
        def _(pool):
            identity(nc, pool, ident, S["ident"])
            pool.wait_ge(S["mask_in"], 16)
            pool.wait_ge(S["bias_in"], 16 * NA_H)
            for h in range(NA_H):
                m = bass.AP(cmask[:, :].tensor, cmask[:, :].offset, [cmask[:, :].ap[0], [0, NS], [1, GRID_W]])
                nc.gpsimd.tensor_tensor(bias[:, h, :, :], bias[:, h, :, :], m, ALU.add).then_inc(S["bias_ready"], 1)

        @block.tensor
        def _(pe):
            pe.wait_ge(S["ident"], 2)

            def scores(i):
                m, h = items[i]
                r0, nr = key_rows(m)
                lo = (h % 2) * HD
                if i >= 2:
                    pe.wait_ge(S["exped"], i - 1)
                q = qT[lo:lo + HD, h // 2, m * P:(m + 1) * P]
                ps = score[i % 2]
                k0 = r0 * GRID_W
                nc.tensor.matmul(ps[:, 0:512], q, kT[lo:lo + HD, h // 2, k0:k0 + 512], start=True, stop=True)
                if nr == 9:
                    nc.tensor.matmul(ps[:, 512:576], q, kT[lo:lo + HD, h // 2, k0 + 512:k0 + 576], start=True, stop=True)
                nc.tensor.matmul(ps[:, 768:1024], q, kT[lo:lo + HD, h // 2, T:TA], start=True, stop=True).then_inc(S["scored"], 1)

            def transposes(i):
                m, h = items[i]
                pe.wait_ge(S["exped"], i + 1)
                if i >= 1:
                    pe.wait_ge(S["evA"], i)
                    pe.wait_ge(S["evB"], i)
                pr = probs[:, i % 2, :]
                for b in range(4):
                    last = nc.tensor.transpose(trA[:, b * P:(b + 1) * P], pr[:, b * P:(b + 1) * P], ident[:, :])
                last.then_inc(S["trA_done"], 1)
                if key_rows(m)[1] == 9:
                    nc.tensor.transpose(trB[0:64, 0:P], pr[:, 512:576], ident[:, :])
                for b in range(2):
                    last = nc.tensor.transpose(trB[:, (b + 1) * P:(b + 2) * P], pr[:, CTX0 + b * P:CTX0 + (b + 1) * P], ident[:, :])
                last.then_inc(S["trB_done"], 1)

            def values(i):
                m, h = items[i]
                r0, nr = key_rows(m)
                pe.wait_ge(S["evA"], i + 1)
                pe.wait_ge(S["evB"], i + 1)
                if i >= 2:
                    pe.wait_ge(S["y_ready"], i - 1)
                o = out[i % 2][:, 0:HD]
                hc = slice(h * HD, (h + 1) * HD)
                t0 = r0 // 2
                for b in range(4):
                    nc.tensor.matmul(o, pT[:, i % 2, b, :], v[:, t0 + b, hc], start=(b == 0), stop=False)
                if nr == 9:
                    nc.tensor.matmul(o, pT[0:64, i % 2, 4, :], v[0:64, t0 + 4, hc], start=False, stop=False)
                for b in range(2):
                    last = nc.tensor.matmul(o, pT[:, i % 2, 5 + b, :], v[:, NT + b, hc], start=False, stop=(b == 1))
                last.then_inc(S["pv"], 1)

            for i in range(NI + 2):
                if i < NI:
                    scores(i)
                if 1 <= i <= NI:
                    transposes(i - 1)
                if i >= 2:
                    values(i - 2)
            for g in range(6):
                c, half = g // 2, g % 2
                pe.wait_ge(S["y_ready"], NI)
                if g >= 2:
                    pe.wait_ge(S["mcA" if half == 0 else "mcB"], g // 2)
                ps = trA if half == 0 else trB
                for b in range(4):
                    last = nc.tensor.transpose(ps[:, b * P:(b + 1) * P], y[:, 4 * half + b, c * P:(c + 1) * P], ident[:, :])
                last.then_inc(S["mtA" if half == 0 else "mtB"], 1)

        @block.scalar
        def _(act):
            for i in range(NI + 1):
                if i >= 1:
                    j = i - 1
                    act.wait_ge(S["trB_done"], j + 1)
                    if j >= 2:
                        act.wait_ge(S["pv"], j - 1)
                    if key_rows(items[j][0])[1] == 9:
                        nc.scalar.copy(pT[0:64, j % 2, 4, :], trB[0:64, 0:P])
                    nc.scalar.copy(pT[:, j % 2, 5:7, :], trB[:, P:3 * P]).then_inc(S["evB"], 1)
                if i < NI:
                    m, h = items[i]
                    w = key_rows(m)[1] * GRID_W
                    act.wait_ge(S["max_ready"], i + 1)
                    pr = probs[:, i % 2, :]
                    nc.scalar.activation(pr[:, 0:w], pr[:, 0:w], ACT.Exp, bias=mx[:, i, 3:4], accum_out=sm[:, i, 0:1])
                    nc.scalar.activation(pr[:, CTX0:832], score[i % 2][:, 768:1024], ACT.Exp, bias=mx[:, i, 3:4],
                                         scale=HD ** -0.5, accum_out=sm[:, i, 1:2]).then_inc(S["exped"], 1)
            for g in range(1, 6, 2):
                act.wait_ge(S["mtB"], g // 2 + 1)
                nc.scalar.copy(mixT[:, 3 + g // 2, T // 2:T], trB[:, :]).then_inc(S["mcB"], 1)

        @block.vector
        def _(dve):
            link = linked(dve, S["vec"])
            dve.wait_ge(S["bias_ready"], NA_H)
            for i in range(NI + 2):
                if i < NI:
                    m, h = items[i]
                    r0, nr = key_rows(m)
                    w = nr * GRID_W
                    s0 = r0 - 2 * m + NA_ROWS - 1
                    dve.wait_ge(S["scored"], i + 1)
                    if i >= 2:
                        dve.wait_ge(S["trB_done"], i - 1)
                    pr, ps = probs[:, i % 2, :], score[i % 2]
                    b = bias[:, h, s0:s0 + nr, :].rearrange("p r c -> p (r c)")
                    link(nc.vector.scalar_tensor_tensor(pr[:, 0:w], ps[:, 0:w], HD ** -0.5, b, ALU.mult, ALU.add))
                    if nr == 9:
                        nc.vector.memset(pr[64:128, 0:64], MASKED)
                        link(nc.vector.memset(pr[0:64, 512:576], MASKED))
                    nc.vector.tensor_reduce(mx[:, i, 0:1], pr[:, 0:w], AXX, ALU.max)
                    link(nc.vector.tensor_reduce(mx[:, i, 1:2], ps[:, 768:1024], AXX, ALU.max))
                    link(nc.vector.tensor_scalar(mx[:, i, 2:3], mx[:, i, 1:2], HD ** -0.5, mx[:, i, 0:1], ALU.mult, ALU.max))
                    nc.vector.tensor_scalar(mx[:, i, 3:4], mx[:, i, 2:3], -1.0, None, ALU.mult).then_inc(S["max_ready"], 1)
                if 1 <= i <= NI:
                    j = i - 1
                    dve.wait_ge(S["trA_done"], j + 1)
                    if j >= 2:
                        dve.wait_ge(S["pv"], j - 1)
                    nc.vector.tensor_copy(pT[:, j % 2, 0:4, :].rearrange("p a b -> p (a b)"), trA[:, :]).then_inc(S["evA"], 1)
                if i >= 2:
                    j = i - 2
                    m, h = items[j]
                    dve.wait_ge(S["exped"], j + 1)
                    link(nc.vector.tensor_tensor(sm[:, j, 2:3], sm[:, j, 0:1], sm[:, j, 1:2], ALU.add))
                    link(nc.vector.reciprocal(sm[:, j, 3:4], sm[:, j, 2:3]))
                    dve.wait_ge(S["pv"], j + 1)
                    nc.vector.tensor_scalar(y[:, m, h * HD:(h + 1) * HD], out[j % 2][:, 0:HD], sm[:, j, 3:4], None,
                                            ALU.mult).then_inc(S["y_ready"], 1)
            for g in range(0, 6, 2):
                dve.wait_ge(S["mtA"], g // 2 + 1)
                nc.vector.tensor_copy(mixT[:, 3 + g // 2, 0:T // 2], trA[:, :]).then_inc(S["mcA"], 1)


BF16 = mybir.dt.bfloat16


def phase_ssd(nc, kit, keep, io):
    scope = ExitStack()
    with scope:
        xbcT, z, dt, mixT = keep["xbcT"], keep["z"], keep["dt"], keep["mixT"]
        NC = NT + NTC
        H2 = 2 * SSD_H
        brow = kit.sb(scope, "dt_bias_row", [P, H2])
        arow = kit.sb(scope, "a_row", [P, H2])
        drow = kit.sb(scope, "d_skip_row", [P, SSD_H])
        ncol = kit.sb(scope, "ssd_norm_col", [P, 3])
        one = kit.sb(scope, "one_c", [P, 1])
        eps = kit.sb(scope, "eps_c", [P, 1])
        ones = kit.sb(scope, "ones_c", [P, P])
        tri = kit.sb(scope, "tri", [P, 2, P])
        ident = kit.sb(scope, "ident_c", [P, P])
        identb = kit.sb(scope, "ident_bf", [P, P], BF16)
        outside = kit.sb(scope, "outside_bf", [P, 2, P], BF16)
        sp_a = kit.sb(scope, "softplus_a", [P, NC, H2])
        sp_b = kit.sb(scope, "softplus_b", [P, NC, H2])
        dta = kit.sb(scope, "dta", [P, NC, H2])
        acs = kit.sb(scope, "acs", [P, NC, H2])
        nacs = kit.sb(scope, "neg_acs", [P, NC, H2])
        eacs = kit.sb(scope, "exp_acs", [P, NC, H2])
        wdec = kit.sb(scope, "state_weight", [P, NC, H2])
        dec = kit.sb(scope, "chunk_decay", [P, NC, H2])
        xs = kit.sb(scope, "xs_tok", [P, NC, SSD_W])
        btok = kit.sb(scope, "b_tok", [P, 2, NGRP * NST])
        xdec = kit.sb(scope, "x_decayed", [P, 2, 2, SSD_W])
        st = kit.sb(scope, "chunk_state", [P, NC, 2, SSD_W])
        run = kit.sb(scope, "run_state", [P, 2, SSD_W])
        start = kit.sb(scope, "start_state", [P, NT, NGRP, 2, GW])
        trirhs = kit.sb(scope, "tri_dta", [P, 2, SSD_H, P])
        E = xdec[:, :, :, :].rearrange("p a b c -> p (a b c)").rearrange("p (d h i) -> p d h i", d=2, h=SSD_H)
        W = E
        xdt = run
        t1 = kit.sb(scope, "ssd_t1", [P, SSD_W])
        t2 = btok[:, :, :].rearrange("p a b -> p (a b)")[:, 0:SSD_W]
        ssq = kit.sb(scope, "ssd_ssq", [P, NT, NGRP])
        squares = st
        y = z
        psG = kit.ps(scope, "psG", [P, 512])
        psY = kit.ps(scope, "psY", [P, 512])
        psI = kit.ps(scope, "psI", [P, 2, 512])
        psA = [kit.ps(scope, f"psA{d}", [P, 2, 512]) for d in range(2)]
        S = {n: kit.sem("s_" + n) for n in ("small_in", "pool", "vec", "actv", "dta_ready", "cum", "acs_ready", "exps", "tr", "ev", "xdec",
                                            "st", "st_ev", "scan", "tri_ready", "G", "A", "E", "W", "intra", "inter", "y_used", "gated",
                                            "ssq", "std", "scaled", "ytr", "mixed", "i_used")}

        def head_cols(ap):
            return bass.AP(ap.tensor, ap.offset, [ap.ap[0], [1, SSD_H], [0, HD]])

        def by_head(ap):
            return ap.rearrange("p (h d) -> p h d", d=HD)

        def g_bcast(g):
            a = psG[:, g * P:(g + 1) * P]
            return bass.AP(a.tensor, a.offset, [a.ap[0], [0, 3], [1, P]])

        def group_squares(act, c):
            act.wait_ge(S["gated"], c + 1)
            for g in range(NGRP):
                last = nc.scalar.activation(squares[:, c, 0, g * GW:(g + 1) * GW], y[:, c, g * GW:(g + 1) * GW], ACT.Square, accum_out=ssq[:, c, g:g + 1])
            last.then_inc(S["ssq"], 1)

        block = scope.enter_context(nc.Block())

        @block.sync
        def _(sp):
            for dst, src in ((brow, "dt_bias"), (arow, "a_log"), (drow, "ssd_d")):
                a = io[src]
                sp.dma_start(dst[:, :], bass.AP(a.tensor, a.offset, [[0, P], [1, a.shape[0]]])).then_inc(S["small_in"], 16)
            sp.dma_start(ncol[:, :], io["ssd_norm_col"]).then_inc(S["small_in"], 16)

        @block.gpsimd
        def _(pool):
            link = linked(pool, S["pool"])
            nc.gpsimd.memset(one[:, :], 1.0)
            nc.gpsimd.memset(eps[:, :], EPS)
            nc.gpsimd.memset(ones[:, :], 1.0)
            nc.gpsimd.memset(outside[:, :, :], 0.0)
            nc.gpsimd.memset(ident[:, :], 0.0)
            nc.gpsimd.memset(identb[:, :], 0.0)
            link(nc.gpsimd.memset(tri[:, :, :], 1.0))
            for m in (ident, identb):
                nc.gpsimd.affine_select(out=m[:, :], in_=m[:, :], compare_op=ALU.not_equal, fill=1.0, base=0,
                                        pattern=[[-1, P]], channel_multiplier=1)
            for m, fill in ((tri, 0.0), (outside, MASKED)):
                nc.gpsimd.affine_select(out=m[:, 0, :], in_=m[:, 0, :], compare_op=ALU.is_ge, fill=fill, base=0,
                                        pattern=[[1, P]], channel_multiplier=-1)
                last = nc.gpsimd.affine_select(out=m[:, 1, :], in_=m[:, 1, :], compare_op=ALU.is_ge, fill=fill, base=0,
                                               pattern=[[-1, P]], channel_multiplier=1)
            link(last)
            pool.wait_ge(S["dta_ready"], 1)
            for c in range(NT):
                if c >= 1:
                    pool.wait_ge(S["A"], c)
                for d in range(2):
                    a = dta[:, c, d * SSD_H:(d + 1) * SSD_H]
                    tr = tri[:, d, :]
                    nc.gpsimd.tensor_tensor(trirhs[:, d, :, :], bass.AP(tr.tensor, tr.offset, [tr.ap[0], [0, SSD_H], [1, P]]),
                                            bass.AP(a.tensor, a.offset, [a.ap[0], [1, SSD_H], [0, P]]),
                                            ALU.mult).then_inc(S["tri_ready"], 1)

        @block.tensor
        def _(pe):
            pe.wait_ge(S["pool"], 2)
            pe.wait_ge(S["dta_ready"], 1)
            for d in range(2):
                hs = slice(d * SSD_H, (d + 1) * SSD_H)
                nc.tensor.matmul(psA[0][:, d, 0:NC * SSD_H].rearrange("p (c h) -> p c h", h=SSD_H), tri[:, d, :], dta[:, :, hs],
                                 start=True, stop=True)
            nc.tensor.matmul(psA[1][:, 0, 0:NC * H2], ones[:, :], dta[:, :, :].rearrange("p c h -> p (c h)"), start=True,
                             stop=True).then_inc(S["cum"], 1)

            def turn(c):
                if c >= 1:
                    pe.wait_ge(S["ev"], c)
                for j in range(3):
                    nc.tensor.transpose(psY[:, j * P:(j + 1) * P], xbcT[:, j, c * P:(c + 1) * P], ident[:, :])
                for g in range(NGRP):
                    last = nc.tensor.transpose(psG[:, g * P:(g + 1) * P], xbcT[:, 3 + g, c * P:(c + 1) * P], ident[:, :])
                last.then_inc(S["tr"], 1)

            def states(c):
                pe.wait_ge(S["xdec"], c + 1)
                if c >= 1:
                    pe.wait_ge(S["st_ev"], c)
                for g in range(NGRP):
                    for d in range(2):
                        last = nc.tensor.matmul(psI[:, d, g * GW:(g + 1) * GW], btok[:, c % 2, g * P:(g + 1) * P],
                                                xdec[:, c % 2, d, g * GW:(g + 1) * GW], start=True, stop=True)
                last.then_inc(S["st"], 1)

            for c in range(NC + 1):
                if c < NC:
                    turn(c)
                if c >= 1:
                    states(c - 1)

            def decays(c):
                if c >= 1:
                    pe.wait_ge(S["W"], 4 * c)
                for g in range(NGRP):
                    last = nc.tensor.matmul(psG[:, g * P:(g + 1) * P], xbcT[:, 3 + g, c * P:(c + 1) * P],
                                            xbcT[:, 5 + g, c * P:(c + 1) * P], start=True, stop=True)
                last.then_inc(S["G"], 1)
                pe.wait_ge(S["exps"], 1)
                if c >= 1:
                    pe.wait_ge(S["E"], 2 * c)
                for d in range(2):
                    pe.wait_ge(S["tri_ready"], 2 * c + d + 1)
                    for h in range(2):
                        nc.tensor.matmul(psA[d][:, h, 0:3 * P], ones[:, :], trirhs[:, d, 3 * h:3 * h + 3, :], start=True, stop=False)
                    for h in range(2):
                        o = outside[:, d, :]
                        last = nc.tensor.matmul(psA[d][:, h, 0:3 * P].rearrange("p (a b) -> p a b", a=3), identb[:, :],
                                                bass.AP(o.tensor, o.offset, [o.ap[0], [0, 3], [1, P]]), start=False, stop=True)
                last.then_inc(S["A"], 1)

            def outputs(c):
                pe.wait_ge(S["scan"], 1)
                if c >= 1:
                    pe.wait_ge(S["i_used"], c)
                for g in range(NGRP):
                    last = nc.tensor.matmul(psI[:, g, 0:2 * GW], xbcT[:, 5 + g, c * P:(c + 1) * P],
                                            start_flat(c, g), start=True, stop=True)
                last.then_inc(S["inter"], 1)
                pe.wait_ge(S["W"], 4 * c + 4)
                if c >= 1:
                    pe.wait_ge(S["y_used"], c)
                for h in range(SSD_H):
                    for d in range(2):
                        last = nc.tensor.matmul(psY[:, h * HD:(h + 1) * HD], W[:, d, h, :], xdt[:, d, h * HD:(h + 1) * HD],
                                                start=(d == 0), stop=(d == 1))
                last.then_inc(S["intra"], 1)

            def start_flat(c, g):
                return start[:, c, g, :, :].rearrange("p d w -> p (d w)")

            for c in range(NT):
                decays(c)
                outputs(c)
            pe.wait_ge(S["scaled"], 1)
            for n in range(6):
                j, half = n // 2, n % 2
                ps = psY if half == 0 else psG
                if n >= 2:
                    pe.wait_ge(S["mixed"], n - 1)
                for b in range(4):
                    last = nc.tensor.transpose(ps[:, b * P:(b + 1) * P], y[:, 4 * half + b, j * P:(j + 1) * P], ident[:, :])
                last.then_inc(S["ytr"], 1)

        @block.scalar
        def _(act):
            link = linked(act, S["actv"])
            act.wait_ge(S["pool"], 2)
            act.wait_ge(S["small_in"], 64)
            nc.scalar.activation(z[:, :, :], z[:, :, :], ACT.Silu)
            act.wait_ge(S["vec"], 2)
            link(nc.scalar.activation(sp_b[:, :, :], sp_b[:, :, :], ACT.Exp, scale=-1.0))
            link(nc.scalar.activation(arow[:, :], arow[:, :], ACT.Exp))
            link(nc.scalar.activation(acs[:, :, :], sp_b[:, :, :], ACT.Ln, bias=one[:, 0:1]))
            for c in range(NC):
                act.wait_ge(S["tr"], c + 1)
                if c >= 2:
                    act.wait_ge(S["st"], c - 1)
                nc.scalar.copy(xs[:, c, :], psY[:, 0:SSD_W])
                nc.scalar.copy(btok[:, c % 2, :], psG[:, 0:2 * P]).then_inc(S["ev"], 1)
                if c == 0:
                    act.wait_ge(S["acs_ready"], 1)
                    nc.scalar.activation(eacs[:, :, :], acs[:, :, :], ACT.Exp)
                    nc.scalar.activation(wdec[:, :, :], wdec[:, :, :], ACT.Exp)
                    nc.scalar.activation(dec[:, :, :], dec[:, :, :], ACT.Exp).then_inc(S["exps"], 1)
                if c >= 1:
                    act.wait_ge(S["st"], c)
                    nc.scalar.copy(st[:, c - 1, :, :], psI[:, :, 0:SSD_W]).then_inc(S["st_ev"], 1)
            act.wait_ge(S["st"], NC)
            nc.scalar.copy(st[:, NC - 1, :, :], psI[:, :, 0:SSD_W]).then_inc(S["st_ev"], 1)
            for c in range(NT):
                act.wait_ge(S["A"], c + 1)
                if c >= 1:
                    act.wait_ge(S["intra"], c)
                for d in range(2):
                    for h in range(SSD_H):
                        last = nc.scalar.activation(E[:, d, h, :], psA[d][:, h // 3, (h % 3) * P:(h % 3 + 1) * P], ACT.Exp,
                                                    bias=nacs[:, c, d * SSD_H + h:d * SSD_H + h + 1])
                    last.then_inc(S["E"], 1)
                if c >= 1:
                    group_squares(act, c - 1)
            group_squares(act, NT - 1)
            act.wait_ge(S["ssq"], NT)
            nc.scalar.activation(ssq[:, :, :], ssq[:, :, :], ACT.Sqrt, bias=eps[:, 0:1], scale=1.0 / GW).then_inc(S["std"], 1)
            for n in range(6):
                act.wait_ge(S["ytr"], n + 1)
                j, half = n // 2, n % 2
                nc.scalar.activation(mixT[:, j, half * 512:(half + 1) * 512], (psY if half == 0 else psG)[:, :], ACT.Copy,
                                     scale=ncol[:, j:j + 1]).then_inc(S["mixed"], 1)

        @block.vector
        def _(dve):
            link = linked(dve, S["vec"])
            dve.wait_ge(S["small_in"], 64)
            b = bass.AP(brow[:, :].tensor, brow[:, :].offset, [brow[:, :].ap[0], [0, NC], [1, H2]])
            link(nc.vector.tensor_tensor(sp_a[:, :, :], dt[:, :, :], b, ALU.add))
            link(nc.vector.scalar_tensor_tensor(sp_b[:, :, :], sp_a[:, :, :], -1.0, sp_a[:, :, :], ALU.mult, ALU.max))
            dve.wait_ge(S["actv"], 3)
            link(nc.vector.tensor_scalar(nacs[:, :, :], sp_b[:, :, :], 1.0, None, ALU.add))
            link(nc.vector.tensor_scalar(eacs[:, :, :], nacs[:, :, :], -1.0, None, ALU.add))
            link(nc.vector.tensor_tensor(sp_b[:, :, :], sp_b[:, :, :], eacs[:, :, :], ALU.subtract))
            link(nc.vector.reciprocal(nacs[:, :, :], nacs[:, :, :]))
            link(nc.vector.tensor_tensor(sp_b[:, :, :], sp_b[:, :, :], nacs[:, :, :], ALU.mult))
            link(nc.vector.tensor_tensor(sp_b[:, :, :], sp_b[:, :, :], acs[:, :, :], ALU.add))
            link(nc.vector.scalar_tensor_tensor(dt[:, :, :], sp_a[:, :, :], 0.0, sp_b[:, :, :], ALU.max, ALU.add))
            a = bass.AP(arow[:, :].tensor, arow[:, :].offset, [arow[:, :].ap[0], [0, NC], [1, H2]])
            nc.vector.scalar_tensor_tensor(dta[:, :, :], dt[:, :, :], -1.0, a, ALU.mult, ALU.mult).then_inc(S["dta_ready"], 1)
            dve.wait_ge(S["cum"], 1)
            for d in range(2):
                hs = slice(d * SSD_H, (d + 1) * SSD_H)
                link(nc.vector.tensor_copy(acs[:, :, hs], psA[0][:, d, 0:NC * SSD_H].rearrange("p (c h) -> p c h", h=SSD_H)))
            link(nc.vector.tensor_copy(dec[:, :, :].rearrange("p c h -> p (c h)"), psA[1][:, 0, 0:NC * H2]))
            link(nc.vector.tensor_scalar(nacs[:, :, :], acs[:, :, :], -1.0, None, ALU.mult))
            nc.vector.tensor_tensor(wdec[:, :, :], dec[:, :, :], nacs[:, :, :], ALU.add).then_inc(S["acs_ready"], 1)
            dve.wait_ge(S["exps"], 1)
            link(nc.vector.tensor_tensor(wdec[:, :, :], wdec[:, :, :], dt[:, :, :], ALU.mult))
            for c in range(NC):
                dve.wait_ge(S["ev"], c + 1)
                if c >= 2:
                    dve.wait_ge(S["st"], c - 1)
                for d in range(2):
                    last = nc.vector.tensor_tensor(by_head(xdec[:, c % 2, d, :]), by_head(xs[:, c, :]),
                                                   head_cols(wdec[:, c, d * SSD_H:(d + 1) * SSD_H]), ALU.mult)
                last.then_inc(S["xdec"], 1)
            link(nc.vector.memset(run[:, :, :], 0.0))
            dve.wait_ge(S["st_ev"], NC)
            for n in range(NC):
                for d in range(2):
                    c = (NT + n if n < NTC else n - NTC) if d == 0 else (NT + NTC - 1 - n if n < NTC else NT - 1 - (n - NTC))
                    if n >= NTC:
                        nc.vector.tensor_copy(start[:, c, :, d, :], run[:, d, :].rearrange("p (g w) -> p g w", g=NGRP))
                    if n < NC - 1:
                        link(nc.vector.tensor_tensor(by_head(run[:, d, :]), by_head(run[:, d, :]),
                                                     head_cols(dec[:, c, d * SSD_H:(d + 1) * SSD_H]), ALU.mult))
                        link(nc.vector.tensor_tensor(run[:, d, :], run[:, d, :], st[:, c, d, :], ALU.add))
            link(nc.vector.memset(t1[:, :], 0.0))
            dve.sem_inc(S["scan"], 1)
            for c in range(NT):
                if c >= 1:
                    dve.wait_ge(S["intra"], c)
                for d in range(2):
                    nc.vector.tensor_tensor(by_head(xdt[:, d, :]), by_head(xs[:, c, :]),
                                            head_cols(dt[:, c, d * SSD_H:(d + 1) * SSD_H]), ALU.mult)
                dve.wait_ge(S["G"], c + 1)
                for d in range(2):
                    dve.wait_ge(S["E"], 2 * c + d + 1)
                    for g in range(NGRP):
                        nc.vector.tensor_tensor(W[:, d, 3 * g:3 * g + 3, :], E[:, d, 3 * g:3 * g + 3, :], g_bcast(g),
                                                ALU.mult).then_inc(S["W"], 1)
                dve.wait_ge(S["inter"], c + 1)
                for d, t in ((0, t1[:, :]), (1, t2)):
                    src = psI[:, :, d * GW:(d + 1) * GW].rearrange("p g (h e) -> p g h e", e=HD)
                    e = eacs[:, c, d * SSD_H:(d + 1) * SSD_H]
                    e = bass.AP(e.tensor, e.offset, [e.ap[0], [3, NGRP], [1, 3], [0, HD]])
                    link(nc.vector.tensor_tensor(t.rearrange("p (g h e) -> p g h e", g=NGRP, e=HD), src, e, ALU.mult))
                dve.sem_inc(S["i_used"], 1)
                link(nc.vector.tensor_tensor(t1[:, :], t1[:, :], t2, ALU.add))
                link(nc.vector.tensor_tensor(by_head(t2), by_head(xs[:, c, :]), head_cols(drow[:, :]), ALU.mult))
                link(nc.vector.tensor_tensor(t1[:, :], t1[:, :], t2, ALU.add))
                dve.wait_ge(S["intra"], c + 1)
                link(nc.vector.tensor_tensor(t1[:, :], t1[:, :], psY[:, 0:SSD_W], ALU.add))
                dve.sem_inc(S["y_used"], 1)
                link(nc.vector.tensor_tensor(y[:, c, :], t1[:, :], z[:, c, :], ALU.mult))
                dve.sem_inc(S["gated"], 1)
            dve.wait_ge(S["std"], 1)
            link(nc.vector.reciprocal(ssq[:, :, :], ssq[:, :, :]))
            for c in range(NT):
                for g in range(NGRP):
                    last = nc.vector.tensor_scalar(y[:, c, g * GW:(g + 1) * GW], y[:, c, g * GW:(g + 1) * GW], ssq[:, c, g:g + 1], None,
                                                   ALU.mult)
            last.then_inc(S["scaled"], 1)


HY_EMB, HY_HID = 33, 64
TWO_PI_HI = 6.28125
TWO_PI_LO = 2 * np.pi - 6.28125
PI_BELOW = float(np.nextafter(np.float32(np.pi), np.float32(0)))
ROUND = 1.5 * 2.0 ** 23


def phase_hyena(nc, kit, keep, io):
    scope = ExitStack()
    with scope:
        hyT, mixT = keep["hyT"], keep["mixT"]
        cos = kit.sb(scope, "dft_cos", [P, NT, T])
        sin = kit.sb(scope, "dft_sin", [P, NT, T])
        X = kit.sb(scope, "hy_x", [P, NT, 3, HY_W])
        Z = kit.sb(scope, "hy_z", [P, NT, 2, HY_W])
        decay = kit.sb(scope, "hy_decay", [P, NT, HY_W])
        w1 = kit.sb(scope, "hy_w1", [HY_EMB, HY_HID])
        w2 = kit.sb(scope, "hy_w2", [HY_HID, HY_HID])
        w3 = kit.sb(scope, "hy_w3", [HY_HID, 2 * HY_W])
        zt = kit.sb(scope, "hy_pos", [HY_EMB, T])
        bf = kit.sb(scope, "hy_bias_freq", [HY_HID, 2, 2])
        hid = Z[0:HY_HID, 2:4, :, :].rearrange("p a b c -> p (a b c)")
        turns = Z[0:HY_HID, 0:2, :, :].rearrange("p a b c -> p (a b c)")
        drow = kit.sb(scope, "hy_d_row", [1, HY_W])
        alt_row = kit.sb(scope, "alt_row", [1, T])
        alt_col = kit.sb(scope, "alt_col", [P, 1])
        wcol = kit.sb(scope, "inv_scale", [P, NT])
        ident = kit.sb(scope, "ident_d", [P, P])
        ones = kit.sb(scope, "ones_d", [P, P])
        absd = kit.sb(scope, "hy_abs", [P, 2, 2, HY_W])
        inv = kit.sb(scope, "hy_inv", [P, HY_W])
        F = decay[:, :, :].rearrange("p (s j) c -> p s j c", s=2)
        tmp = kit.sb(scope, "hy_tmp", [P, 2, HY_W])
        nyq = kit.sb(scope, "hy_nyq", [1, 2 * HY_W])
        znyq = kit.sb(scope, "hy_znyq", [1, HY_W])
        ps = [kit.ps(scope, f"hyps{i}", [P, 512]) for i in range(8)]
        S = {n: kit.sem("h_" + n) for n in ("small_in", "cos_in", "sin_in", "ident", "ones", "vec", "u_ready", "utr", "u_tok", "h1", "h2",
                                            "red", "sined", "h3", "h3_read", "abs", "abs_used", "abs_sum", "x_ready", "nyq", "nyq_out", "znyq", "fwd",
                                            "spec", "z", "inv", "wrote")}
        block = scope.enter_context(nc.Block())
        small = ((w1, "hy_f_w1"), (w2, "hy_f_w2"), (w3, "hy_f_w3"), (zt, "hy_pos"), (bf, "hy_bias_freq"), (decay, "hy_decay"), (drow, "hy_d"),
                 (alt_row, "alt_row"), (alt_col, "alt_col"), (wcol, "inv_scale"))

        @block.sync
        def _(sp):
            for dst, src in small:
                sp.dma_start(dst[:], io[src]).then_inc(S["small_in"], 16)
            sp.dma_start(cos[:, :, :], io["dft_cos"].rearrange("(k p) n -> p k n", p=P)).then_inc(S["cos_in"], 16)
            sp.dma_start(sin[:, :, :], io["dft_sin"].rearrange("(k p) n -> p k n", p=P)).then_inc(S["sin_in"], 16)

        @block.gpsimd
        def _(pool):
            identity(nc, pool, ident, S["ident"])
            nc.gpsimd.memset(ones[:, :], 1.0).then_inc(S["ones"], 1)

        @block.tensor
        def _(pe):
            pe.wait_ge(S["ident"], 2)
            for n in range(4):
                c, half = n // 2, n % 2
                pe.wait_ge(S["u_ready"], c + 1)
                for b in range(4):
                    t = 4 * half + b
                    last = nc.tensor.transpose(ps[4 + n][:, b * P:(b + 1) * P], hyT[:, 4 + c, t * P:(t + 1) * P], ident[:, :])
                last.then_inc(S["utr"], 1)
            pe.wait_ge(S["small_in"], 16 * len(small))
            for i in range(2):
                last = nc.tensor.matmul(ps[i][0:HY_HID, :], w1[:, :], zt[:, i * 512:(i + 1) * 512], start=True, stop=True)
            last.then_inc(S["h1"], 1)
            pe.wait_ge(S["sined"], 1)
            for i in range(2):
                last = nc.tensor.matmul(ps[2 + i][0:HY_HID, :], w2[:, :], hid[:, i * 512:(i + 1) * 512], start=True, stop=True)
            last.then_inc(S["h2"], 1)
            pe.wait_ge(S["sined"], 2)
            pe.wait_ge(S["ones"], 1)
            for k in range(NT + 1):
                if k < NT:
                    if k >= 2:
                        pe.wait_ge(S["h3_read"], k - 1)
                    nc.tensor.matmul(ps[k % 2][:, :], hid[:, k * P:(k + 1) * P], w3[:, :], start=True, stop=True).then_inc(S["h3"], 1)
                if k >= 1:
                    pe.wait_ge(S["abs"], k)
                    nc.tensor.matmul(ps[2][:, :], ones[:, :], absd[:, (k - 1) % 2, :, :].rearrange("p a b -> p (a b)"), start=(k == 1),
                                     stop=(k == NT)).then_inc(S["abs_used"], 1)
            pe.wait_ge(S["x_ready"], 1)
            pe.wait_ge(S["u_tok"], 4)
            for k in range(NT):
                last = nc.tensor.matmul(ps[3][0:1, :], alt_col[:, :], X[:, k, 0:2, :].rearrange("p a b -> p (a b)"), start=(k == 0),
                                        stop=(k == NT - 1))
            last.then_inc(S["nyq"], 1)
            for f in range(NT):
                if f >= 2:
                    pe.wait_ge(S["spec"], f - 1)
                for j, (tab, lo, sem) in enumerate(((cos, 0, "cos_in"), (sin, 1, "sin_in"))):
                    pe.wait_ge(S[sem], 16)
                    for k in range(NT):
                        last = nc.tensor.matmul(ps[4 + 2 * (f % 2) + j][:, :], tab[:, k, f * P:(f + 1) * P],
                                                X[:, k, lo:lo + 2, :].rearrange("p a b -> p (a b)"), start=(k == 0), stop=(k == NT - 1))
                last.then_inc(S["fwd"], 1)
            pe.wait_ge(S["znyq"], 1)
            for q in range(4):
                c, half = q // 2, q % 2
                o, t = ps[q][:, :], slice(half * 512, (half + 1) * 512)
                nc.tensor.matmul(o, znyq[:, c * P:(c + 1) * P], alt_row[:, t], start=True, stop=False)
                for f in range(NT):
                    pe.wait_ge(S["z"], f + 1)
                    nc.tensor.matmul(o, Z[:, f, 0, c * P:(c + 1) * P], cos[:, f, t], start=False, stop=False)
                    last = nc.tensor.matmul(o, Z[:, f, 1, c * P:(c + 1) * P], sin[:, f, t], start=False, stop=(f == NT - 1))
                last.then_inc(S["inv"], 1)

        @block.scalar
        def _(act):
            for n in range(4):
                c, half = n // 2, n % 2
                act.wait_ge(S["utr"], n + 1)
                nc.scalar.copy(X[:, 4 * half:4 * half + 4, 1, c * P:(c + 1) * P],
                               ps[4 + n][:, :].rearrange("p (b c) -> p b c", b=4)).then_inc(S["u_tok"], 1)
            for i in range(2):
                act.wait_ge(S["red"], i + 1)
                nc.scalar.activation(hid[:, :], turns[:, :], ACT.Sin).then_inc(S["sined"], 1)
            for k in range(NT):
                act.wait_ge(S["h3_read"], k + 1)
                if k >= 2:
                    act.wait_ge(S["abs_used"], k - 1)
                nc.scalar.activation(absd[:, k % 2, :, :], X[:, k, 0:3:2, :], ACT.Abs).then_inc(S["abs"], 1)
            act.wait_ge(S["nyq"], 1)
            nc.scalar.copy(nyq[:, :], ps[3][0:1, :]).then_inc(S["nyq_out"], 1)
            for f in range(NT):
                act.wait_ge(S["fwd"], f + 1)
                if f >= 2:
                    act.wait_ge(S["z"], f - 1)
                for j in range(2):
                    last = nc.scalar.copy(F[:, f % 2, 2 * j:2 * j + 2, :].rearrange("p a b -> p (a b)"), ps[4 + 2 * (f % 2) + j][:, :])
                last.then_inc(S["spec"], 1)

        @block.vector
        def _(dve):
            link = linked(dve, S["vec"])
            for c in range(2):
                nc.vector.tensor_tensor(hyT[:, 4 + c, :], hyT[:, 4 + c, :], hyT[:, 2 + c, :], ALU.mult).then_inc(S["u_ready"], 1)
            dve.wait_ge(S["small_in"], 16 * len(small))
            for i, done in enumerate(("h1", "h2")):
                dve.wait_ge(S[done], 1)
                for j in range(2):
                    o = slice(j * 512, (j + 1) * 512)
                    link(nc.vector.tensor_scalar(turns[:, o], ps[2 * i + j][0:HY_HID, :], bf[:, i, 0:1], bf[:, i, 1:2], ALU.add, ALU.mult))
                link(nc.vector.tensor_scalar(hid[:, :], turns[:, :], 1 / (2 * np.pi), ROUND, ALU.mult, ALU.add))
                link(nc.vector.tensor_scalar(hid[:, :], hid[:, :], -ROUND, None, ALU.add))
                link(nc.vector.scalar_tensor_tensor(turns[:, :], hid[:, :], -TWO_PI_HI, turns[:, :], ALU.mult, ALU.add))
                link(nc.vector.scalar_tensor_tensor(turns[:, :], hid[:, :], -TWO_PI_LO, turns[:, :], ALU.mult, ALU.add))
                link(nc.vector.tensor_scalar(turns[:, :], turns[:, :], PI_BELOW, -PI_BELOW, ALU.min, ALU.max))
                dve.sem_inc(S["red"], 1)
            for k in range(NT):
                dve.wait_ge(S["h3"], k + 1)
                nc.vector.tensor_tensor(X[:, k, 0, :], ps[k % 2][:, 0:HY_W], decay[:, k, :], ALU.mult)
                nc.vector.tensor_tensor(X[:, k, 2, :], ps[k % 2][:, HY_W:], decay[:, k, :], ALU.mult).then_inc(S["h3_read"], 1)
            dve.wait_ge(S["abs_used"], NT)
            link(nc.vector.tensor_copy(inv[:, :], ps[2][:, 0:HY_W]))
            link(nc.vector.tensor_tensor(inv[:, :], inv[:, :], ps[2][:, HY_W:], ALU.add))
            link(nc.vector.reciprocal(inv[:, :], inv[:, :]))
            ib = bass.AP(inv[:, :].tensor, inv[:, :].offset, [inv[:, :].ap[0], [0, NT], [1, HY_W]])
            link(nc.vector.tensor_tensor(X[:, :, 0, :], X[:, :, 0, :], ib, ALU.mult))
            link(nc.vector.tensor_tensor(X[:, :, 2, :], X[:, :, 2, :], ib, ALU.mult))
            link(nc.vector.memset(X[0:1, 0, 2, :], 0.0))
            link(nc.vector.tensor_tensor(X[0:1, 0, 0, :], X[0:1, 0, 0, :], drow[:, :], ALU.add))
            link(nc.vector.tensor_tensor(X[:, :, 0, :], X[:, :, 0, :], X[:, :, 2, :], ALU.add))
            link(nc.vector.scalar_tensor_tensor(X[:, :, 2, :], X[:, :, 2, :], -2.0, X[:, :, 0, :], ALU.mult, ALU.add))
            dve.sem_inc(S["x_ready"], 1)
            dve.wait_ge(S["nyq_out"], 1)
            nc.vector.scalar_tensor_tensor(znyq[:, :], nyq[:, 0:HY_W], 1.0 / (2 * T), nyq[:, HY_W:], ALU.mult, ALU.mult).then_inc(S["znyq"], 1)
            for f in range(NT):
                dve.wait_ge(S["spec"], f + 1)
                kr, ur, us, ks = (F[:, f % 2, j, :] for j in range(4))
                w = wcol[:, f:f + 1]
                nc.vector.scalar_tensor_tensor(Z[:, f, 0, :], ur, w, kr, ALU.mult, ALU.mult)
                nc.vector.scalar_tensor_tensor(tmp[:, 0, :], us, w, ks, ALU.mult, ALU.mult)
                nc.vector.scalar_tensor_tensor(Z[:, f, 1, :], ur, w, ks, ALU.mult, ALU.mult)
                link(nc.vector.scalar_tensor_tensor(tmp[:, 1, :], us, w, kr, ALU.mult, ALU.mult))
                link(nc.vector.tensor_tensor(Z[:, f, 0, :], Z[:, f, 0, :], tmp[:, 0, :], ALU.subtract))
                link(nc.vector.tensor_tensor(Z[:, f, 1, :], Z[:, f, 1, :], tmp[:, 1, :], ALU.add))
                dve.sem_inc(S["z"], 1)
            for q in range(4):
                c, half = q // 2, q % 2
                dve.wait_ge(S["inv"], q + 1)
                t = slice(half * 512, (half + 1) * 512)
                last = nc.vector.tensor_tensor(mixT[:, 6 + c, t], ps[q][:, :], hyT[:, c, t], ALU.mult)
            last.then_inc(S["wrote"], 1)
            dve.wait_ge(S["wrote"], 1)


def hyena_constants():
    f32 = np.float32
    t = np.linspace(0.0, 1.0, T, dtype=f32)[:, None]
    w = (f32(2.0 * np.pi) * np.arange(T, dtype=f32)[:, None] / f32(T)).astype(f32)
    bands = (HY_EMB - 1) // 2
    f = np.linspace(1e-4, bands - 1, bands, dtype=f32)[None, :]
    pos = np.concatenate([t, np.cos(f * w), -np.sin(f * w)], axis=1).astype(f32)
    deltas = np.abs(np.linspace(np.log(1e-2) / 1.5, np.log(1e-2) / 0.3, HY_W, dtype=f32))
    decay = np.exp(-t * deltas).astype(f32)
    angle = np.outer(np.arange(T), np.arange(T)) % (2 * T) * (np.pi / T)
    alt = (1.0 - 2.0 * (np.arange(T) % 2)).astype(f32)
    scale = np.full(T, 1.0 / T)
    scale[0] = 0.5 / T
    return {
        "hy_pos": np.ascontiguousarray(pos.T),
        "hy_decay": np.ascontiguousarray(decay.reshape(NT, P, HY_W).transpose(1, 0, 2)),
        "dft_cos": np.cos(angle).astype(f32),
        "dft_sin": np.sin(angle).astype(f32),
        "alt_row": alt[None, :],
        "alt_col": np.ascontiguousarray(alt[:P, None]),
        "inv_scale": np.ascontiguousarray(scale.astype(f32).reshape(NT, P).T),
    }


HALF = P // 2
NUNIT = (T * TOPK + NE * (HALF - 1)) // HALF
NBLK = (T * TOPK + NE * (P - 1)) // P
NROW = NUNIT * HALF
ROW_LIST = -(-NROW // P) * P + P


def row_of(ap, n, at=0):
    return bass.AP(ap.tensor, ap.offset + at, [[0, P], [1, n]])


QUARTERS = tuple((half, what) for half in range(2) for what in range(2))


def gate_up_quarter(io, e, q):
    half, what = QUARTERS[q]
    at = what * DE + half * 512
    return io["w_gate_up"][bass.ds(e, 1), :, at:at + 512].rearrange("a (k p) n -> p (a k) n", p=P)


def first_weights(kit, scope):
    return {"gate_up": kit.sb(scope, "w_gate_up0", [P, 4, KD, 512], side="right"),
            "in": [kit.sem(f"f_gate_up_in0{q}") for q in range(4)]}


def load_first_weights(sp, weights, io):
    for q in range(4):
        sp.dma_start(weights["gate_up"][:, q, :, :], gate_up_quarter(io, 0, q)).then_inc(weights["in"][q], 16)


def phase_mix(nc, kit, keep, io, dram, weights):
    scope = ExitStack()
    with scope:
        mixT, modT, dest, gate, table = keep["mixT"], keep["modT"], keep["dest"], keep["gate"], keep["table"]
        wout = kit.sb(scope, "w_out", [P, KD, D])
        wr = kit.sb(scope, "w_router", [P, KD, NE])
        brt = kit.sb(scope, "b_router_row", [P, NE])
        gains = kit.sb(scope, "gains_col", [P, 3, KD])
        vcol = kit.sb(scope, "vectors_col", [P, 4, KD])
        vrow = kit.sb(scope, "vectors_rows", [4 * KD, P])
        rows = kit.sb(scope, "vectors_row", [P, 3, D])
        xin = kit.sb(scope, "x_tile", [P, 2, D])
        x1 = kit.sb(scope, "x1_tile", [P, 2, D])
        h2 = kit.sb(scope, "h2_tile", [P, 2, D])
        sq = kit.sb(scope, "mix_squares", [P, 2, D])
        h2T = kit.sb(scope, "h2_t", [P, KD, P])
        st = kit.sb(scope, "mix_stat", [P, NT, 4])
        eps = kit.sb(scope, "eps_e", [P, 1])
        ident = kit.sb(scope, "ident_e", [P, P])
        ones = kit.sb(scope, "ones_e", [P, P])
        before = kit.sb(scope, "tri_strict", [P, P])
        lanes = kit.sb(scope, "expert_number", [P, NE])
        logit = kit.sb(scope, "logits", [P, NE])
        top = kit.sb(scope, "top_logits", [P, NT, 8])
        topi = kit.sb(scope, "top_experts", [P, NT, 8], U32)
        topf = kit.sb(scope, "top_experts_f", [P, NT, TOPK])
        shifted = kit.sb(scope, "top_shifted", [P, NT, TOPK])
        gsum = kit.sb(scope, "gate_sum", [P, NT])
        hot = kit.sb(scope, "one_hot", [P, NT, TOPK, NE])
        mask = kit.sb(scope, "chosen", [P, NT, NE])
        place = kit.sb(scope, "place", [P, NT, NE])
        count = kit.sb(scope, "count_so_far", [P, NT + 1, NE])
        amount = kit.sb(scope, "units_and_blocks", [P, 2, NE])
        cum = kit.sb(scope, "amount_before", [P, 2, 2, NE])
        destf = kit.sb(scope, "dest_f", [P, NT, TOPK])
        tokens = kit.sb(scope, "token_number", [P, NT], I32)
        zero = kit.sb(scope, "zero_rows", [P, ROW_LIST // P], I32)
        psO = [kit.ps(scope, f"psO{i}", [P, D]) for i in range(2)]
        psH = kit.ps(scope, "psH", [P, D])
        psL = kit.ps(scope, "psL", [P, 512])
        psR = kit.ps(scope, "psR", [P, 512])
        S = {n: kit.sem("e_" + n) for n in ("w_in", "small_in", "pool", "vec", "vcol", "vturn", "vrow", "vrow_out", "rows_in", "x_in0", "x_in1",
                                            "proj", "std1", "x1", "std2", "h2", "x1_out0", "x1_out1", "h2_out0", "h2_out1", "h2turn", "h2T",
                                            "logits", "logits_read", "shifted", "exped", "mask", "ranks", "dest", "zeroed", "scattered",
                                            "table")}
        block = scope.enter_context(nc.Block())

        @block.sync
        def _(sp):
            sp.dma_start(gains[:, :, :], io["gains_col"]).then_inc(S["small_in"], 16)
            sp.dma_start(brt[:, :], row_of(io["b_router"], NE)).then_inc(S["small_in"], 16)
            sp.dma_start(wr[:, :, :], io["w_router"].rearrange("(k p) n -> p k n", p=P)).then_inc(S["small_in"], 16)
            sp.dma_start(wout[:, :, :], io["w_out"].rearrange("(k p) n -> p k n", p=P)).then_inc(S["w_in"], 16)
            for t in range(2):
                sp.dma_start(xin[:, t, :], io["x"][t * P:(t + 1) * P, :]).then_inc(S[f"x_in{t}"], 16)
            load_first_weights(sp, weights, io)
            sp.wait_ge(S["vrow"], 1)
            sp.dma_start(dram["vectors"].rearrange("(r p) -> r p", p=P), vrow[:, :]).then_inc(S["vrow_out"], 16)
            sp.wait_ge(S["vrow_out"], 16)
            for j in range(3):
                sp.dma_start(rows[:, j, :], row_of(dram["vectors"], D, j * D)).then_inc(S["rows_in"], 16)
            for t in range(NT):
                ts = slice(t * P, (t + 1) * P)
                sp.wait_ge(S["x1"], t + 1)
                sp.dma_start(dram["x1"][ts, :], x1[:, t % 2, :]).then_inc(S[f"x1_out{t % 2}"], 16)
                if t + 2 < NT:
                    sp.dma_start(xin[:, t % 2, :], io["x"][(t + 2) * P:(t + 3) * P, :]).then_inc(S[f"x_in{t % 2}"], 16)
                sp.wait_ge(S["h2"], t + 1)
                sp.dma_start(dram["h2"][ts, :], h2[:, t % 2, :]).then_inc(S[f"h2_out{t % 2}"], 16)
            for i in range(2):
                sp.wait_ge(S[f"x1_out{i}"], 16 * NT // 2)
                sp.wait_ge(S[f"h2_out{i}"], 16 * NT // 2)

        @block.gpsimd
        def _(pool):
            link = linked(pool, S["pool"])
            nc.gpsimd.memset(eps[:, :], EPS)
            nc.gpsimd.memset(ident[:, :], 0.0)
            nc.gpsimd.memset(ones[:, :], 1.0)
            nc.gpsimd.memset(zero[:, :], 0)
            nc.gpsimd.iota(lanes[:, :], pattern=[[1, NE]], base=0, channel_multiplier=0, allow_small_or_imprecise_dtypes=True)
            nc.gpsimd.iota(tokens[:, :], pattern=[[P, NT]], base=0, channel_multiplier=1)
            link(nc.gpsimd.memset(before[:, :], 1.0))
            nc.gpsimd.affine_select(out=ident[:, :], in_=ident[:, :], compare_op=ALU.not_equal, fill=1.0, base=0, pattern=[[-1, P]],
                                    channel_multiplier=1)
            link(nc.gpsimd.affine_select(out=before[:, :], in_=before[:, :], compare_op=ALU.is_gt, fill=0.0, base=0, pattern=[[1, P]],
                                         channel_multiplier=-1))
            pool.dma_start(dram["row_token"].rearrange("(p b) o -> p (b o)", p=P), zero[:, :]).then_inc(S["zeroed"], 16)
            pool.wait_ge(S["zeroed"], 16)
            pool.wait_ge(S["dest"], 1)
            for t in range(NT):
                for k in range(TOPK):
                    pool.indirect_dma_start(out=dram["row_token"], out_offset=bass.IndirectOffsetOnAxis(ap=dest[:, t * TOPK + k:t * TOPK + k + 1], axis=0),
                                            in_=tokens[:, t:t + 1], in_offset=None).then_inc(S["scattered"], 16)
            pool.wait_ge(S["scattered"], 16 * NT * TOPK)

        @block.tensor
        def _(pe):
            pe.wait_ge(S["pool"], 2)
            pe.wait_ge(S["vcol"], 1)
            nc.tensor.transpose(psR[0:4 * KD, 0:P], vcol[:, :, :].rearrange("p a k -> p (a k)"), ident[:, :]).then_inc(S["vturn"], 1)
            pe.wait_ge(S["w_in"], 16)

            def project(t):
                if t >= 2:
                    pe.wait_ge(S["x1"], t - 1)
                for n in range(2):
                    for k in range(KD):
                        last = nc.tensor.matmul(psO[t % 2][:, n * 512:(n + 1) * 512], mixT[:, k, t * P:(t + 1) * P],
                                                wout[:, k, n * 512:(n + 1) * 512], start=(k == 0), stop=(k == KD - 1))
                last.then_inc(S["proj"], 1)

            def route(t):
                pe.wait_ge(S["h2"], t + 1)
                if t >= 1:
                    pe.wait_ge(S["h2T"], t)
                for k in range(KD):
                    last = nc.tensor.transpose(psH[:, k * P:(k + 1) * P], h2[:, t % 2, k * P:(k + 1) * P], ident[:, :])
                last.then_inc(S["h2turn"], 1)
                pe.wait_ge(S["h2T"], t + 1)
                pe.wait_ge(S["small_in"], 48)
                if t >= 1:
                    pe.wait_ge(S["logits_read"], t)
                for k in range(KD):
                    last = nc.tensor.matmul(psL[:, 0:NE], h2T[:, k, :], wr[:, k, :], start=(k == 0), stop=(k == KD - 1))
                last.then_inc(S["logits"], 1)

            for t in range(NT + 1):
                if t < NT:
                    project(t)
                if t >= 1:
                    route(t - 1)
            pe.wait_ge(S["mask"], 1)
            m = mask[:, :, :].rearrange("p t e -> p (t e)")
            nc.tensor.matmul(psR[:, 0:NT * NE], before[:, :], m, start=True, stop=True)
            nc.tensor.matmul(psR[:, NT * NE:2 * NT * NE], ones[:, :], m, start=True, stop=True).then_inc(S["ranks"], 1)

        @block.scalar
        def _(act):
            act.wait_ge(S["pool"], 2)
            act.wait_ge(S["vturn"], 1)
            nc.scalar.copy(vrow[:, :], psR[0:4 * KD, 0:P]).then_inc(S["vrow"], 1)
            sqn = kit.sem("e_sq")
            n = 0
            for t in range(NT):
                for src, done, out, j in ((psO[t % 2][:, :], "proj", "std1", 0), (x1[:, t % 2, :], "x1", "std2", 1)):
                    act.wait_ge(S[done], t + 1)
                    nc.scalar.activation(sq[:, j, :], src, ACT.Square, accum_out=st[:, t, 2 * j:2 * j + 1]).then_inc(sqn, 1)
                    n += 1
                    act.wait_ge(sqn, n)
                    nc.scalar.activation(st[:, t, 2 * j + 1:2 * j + 2], st[:, t, 2 * j:2 * j + 1], ACT.Sqrt, bias=eps[:, 0:1],
                                         scale=1.0 / D).then_inc(S[out], 1)
                act.wait_ge(S["h2turn"], t + 1)
                if t >= 1:
                    act.wait_ge(S["logits"], t)
                nc.scalar.copy(h2T[:, :, :].rearrange("p k t -> p (k t)"), psH[:, :]).then_inc(S["h2T"], 1)
            act.wait_ge(S["shifted"], 1)
            nc.scalar.activation(shifted[:, :, :], shifted[:, :, :], ACT.Exp).then_inc(S["exped"], 1)

        @block.vector
        def _(dve):
            link = linked(dve, S["vec"])
            dve.wait_ge(S["small_in"], 48)
            nc.vector.tensor_tensor(vcol[:, 0, :], modT[:, 2 * KD:3 * KD, 0], gains[:, 0, :], ALU.mult)
            link(nc.vector.tensor_scalar(vcol[:, 1, :], modT[:, 4 * KD:5 * KD, 0], 1.0, None, ALU.add))
            nc.vector.tensor_tensor(vcol[:, 1, :], vcol[:, 1, :], gains[:, 1, :], ALU.mult)
            nc.vector.tensor_copy(vcol[:, 2, :], modT[:, 3 * KD:4 * KD, 0])
            nc.vector.tensor_tensor(vcol[:, 3, :], modT[:, 5 * KD:6 * KD, 0], gains[:, 2, :], ALU.mult).then_inc(S["vcol"], 1)
            dve.wait_ge(S["rows_in"], 48)
            for t in range(NT):
                s = t % 2
                dve.wait_ge(S["std1"], t + 1)
                link(nc.vector.reciprocal(st[:, t, 1:2], st[:, t, 1:2]))
                if t >= 2:
                    dve.wait_ge(S[f"x1_out{s}"], 16 * (t // 2))
                link(nc.vector.scalar_tensor_tensor(x1[:, s, :], psO[s][:, :], st[:, t, 1:2], rows[:, 0, :], ALU.mult, ALU.mult))
                dve.wait_ge(S[f"x_in{s}"], 16 * (t // 2 + 1))
                nc.vector.tensor_tensor(x1[:, s, :], x1[:, s, :], xin[:, s, :], ALU.add).then_inc(S["x1"], 1)
                dve.wait_ge(S["std2"], t + 1)
                link(nc.vector.reciprocal(st[:, t, 3:4], st[:, t, 3:4]))
                if t >= 2:
                    dve.wait_ge(S[f"h2_out{s}"], 16 * (t // 2))
                link(nc.vector.scalar_tensor_tensor(h2[:, s, :], x1[:, s, :], st[:, t, 3:4], rows[:, 1, :], ALU.mult, ALU.mult))
                nc.vector.tensor_tensor(h2[:, s, :], h2[:, s, :], rows[:, 2, :], ALU.add).then_inc(S["h2"], 1)
                dve.wait_ge(S["logits"], t + 1)
                link(nc.vector.tensor_tensor(logit[:, :], psL[:, 0:NE], brt[:, :], ALU.add))
                dve.sem_inc(S["logits_read"], 1)
                link(nc.vector.max(top[:, t, :], logit[:, :]))
                link(nc.vector.max_index(topi[:, t, :], top[:, t, :], logit[:, :]))
            first = top[:, :, 0:1]
            nc.vector.tensor_tensor(shifted[:, :, :], top[:, :, 0:TOPK], bass.AP(first.tensor, first.offset, [first.ap[0], [8, NT], [0, TOPK]]),
                                    ALU.subtract).then_inc(S["shifted"], 1)
            link(nc.vector.tensor_copy(topf[:, :, :], topi[:, :, 0:TOPK]))
            tf, ln = topf[:, :, :], lanes[:, :]
            link(nc.vector.tensor_tensor(hot[:, :, :, :].rearrange("p t k e -> p (t k) e"),
                                         bass.AP(tf.tensor, tf.offset, [tf.ap[0], [1, NT * TOPK], [0, NE]]),
                                         bass.AP(ln.tensor, ln.offset, [ln.ap[0], [0, NT * TOPK], [1, NE]]), ALU.is_equal))
            nc.vector.tensor_reduce(mask[:, :, :], hot[:, :, :, :].rearrange("p t k e -> p t e k"), AXX, ALU.add).then_inc(S["mask"], 1)
            dve.wait_ge(S["exped"], 1)
            link(nc.vector.tensor_reduce(gsum[:, :], shifted[:, :, :], AXX, ALU.add))
            link(nc.vector.reciprocal(gsum[:, :], gsum[:, :]))
            gs = gsum[:, :]
            link(nc.vector.tensor_tensor(gate[:, :].rearrange("p (t k) -> p t k", k=TOPK), shifted[:, :, :],
                                         bass.AP(gs.tensor, gs.offset, [gs.ap[0], [1, NT], [0, TOPK]]), ALU.mult))
            dve.wait_ge(S["ranks"], 1)
            link(nc.vector.tensor_copy(place[:, :, :].rearrange("p t e -> p (t e)"), psR[:, 0:NT * NE]))
            link(nc.vector.memset(count[:, 0, :], 0.0))
            for t in range(NT):
                link(nc.vector.tensor_tensor(count[:, t + 1, :], count[:, t, :], psR[:, NT * NE + t * NE:NT * NE + (t + 1) * NE], ALU.add))
            link(nc.vector.tensor_scalar(amount[:, 0, :], count[:, NT, :], 1.0 / HALF, (HALF - 1) / (2.0 * HALF), ALU.mult, ALU.add))
            link(nc.vector.tensor_scalar(amount[:, 0, :], amount[:, 0, :], ROUND, -ROUND, ALU.add, ALU.add))
            link(nc.vector.tensor_scalar(amount[:, 1, :], amount[:, 0, :], 0.5, 0.25, ALU.mult, ALU.add))
            link(nc.vector.tensor_scalar(amount[:, 1, :], amount[:, 1, :], ROUND, -ROUND, ALU.add, ALU.add))
            link(nc.vector.memset(cum[:, :, :, :], 0.0))
            link(nc.vector.tensor_copy(cum[:, 0, :, 1:NE], amount[:, :, 0:NE - 1]))
            cur, step = 0, 1
            while step < NE:
                nc.vector.tensor_copy(cum[:, 1 - cur, :, 0:step], cum[:, cur, :, 0:step])
                link(nc.vector.tensor_tensor(cum[:, 1 - cur, :, step:NE], cum[:, cur, :, step:NE], cum[:, cur, :, 0:NE - step], ALU.add))
                cur, step = 1 - cur, 2 * step
            nc.vector.tensor_copy(table[:, 0:2, :], amount[0:1, :, :])
            nc.vector.tensor_copy(table[:, 2:4, :], cum[0:1, cur, :, :]).then_inc(S["table"], 1)
            c0 = cum[:, cur, 0, :]
            link(nc.vector.tensor_tensor(place[:, :, :], place[:, :, :], count[:, 0:NT, :], ALU.add))
            link(nc.vector.scalar_tensor_tensor(place[:, :, :], bass.AP(c0.tensor, c0.offset, [c0.ap[0], [0, NT], [1, NE]]), float(HALF),
                                                place[:, :, :], ALU.mult, ALU.add))
            pl = place[:, :, :]
            link(nc.vector.tensor_tensor(hot[:, :, :, :], hot[:, :, :, :],
                                         bass.AP(pl.tensor, pl.offset, [pl.ap[0], [NE, NT], [0, TOPK], [1, NE]]), ALU.mult))
            link(nc.vector.tensor_reduce(destf[:, :, :], hot[:, :, :, :], AXX, ALU.add))
            nc.vector.tensor_copy(dest[:, :], destf[:, :, :].rearrange("p t k -> p (t k)")).then_inc(S["dest"], 1)


BPE = T // P
SLOTS = 2


def phase_experts(nc, kit, keep, weights, io, dram):
    scope = ExitStack()
    with scope:
        table = keep["table"]
        gu = [weights["gate_up"], kit.sb(scope, "w_gate_up1", [P, 4, KD, 512])]
        gu_in = [weights["in"], [kit.sem(f"f_gate_up_in1{q}") for q in range(4)]]
        down = kit.sb(scope, "w_down", [P, 2, 4, D])
        bias = [kit.sb(scope, f"gate_up_bias{i}", [P, 2 * DE]) for i in range(SLOTS)]
        down_bias = kit.sb(scope, "down_bias", [P, D])
        xg = kit.sb(scope, "x_rows", [P, D])
        xT = kit.sb(scope, "x_rows_t", [P, KD, P])
        gated = kit.sb(scope, "gated", [P, 2, 512])
        sig = kit.sb(scope, "sig", [P, 2, 512])
        up = kit.sb(scope, "up", [P, 512])
        actT = kit.sb(scope, "act_t", [P, DE // P, P])
        yrow = kit.sb(scope, "y_rows", [P, D])
        rowtok = kit.sb(scope, "row_token", [P, NUNIT + 1], I32)
        idx = kit.sb(scope, "row_index", [P, 1], I32)
        ident = kit.sb(scope, "ident_f", [P, P])
        psT = kit.ps(scope, "psT", [P, 2, 512])
        psG = kit.ps(scope, "ps_gate_up", [P, 4, 512])
        psD = kit.ps(scope, "ps_down", [P, 2, 512])
        S = {n: kit.sem("f_" + n) for n in ("rowtok_in", "ident", "down_in0", "down_in1", "down_bias_in", "bias_in0", "bias_in1", "index", "rows_in", "x_turned",
                                            "xT", "gate_up", "vec", "gate_ready", "sig", "act", "act_turned", "actT", "down", "y", "y_out",
                                            "blank", "blank_out", "stored", "gathers", "pieces_in")}
        block = scope.enter_context(nc.Block())

        def units_of(eng, e):
            n = eng.value_load(table[0:1, 0, bass.ds(e, 1)], min_val=0, max_val=2 * BPE)
            return n, eng.value_load(table[0:1, 2, bass.ds(e, 1)], min_val=0, max_val=NUNIT)

        def blocks_of(eng, e):
            n = eng.value_load(table[0:1, 1, bass.ds(e, 1)], min_val=0, max_val=BPE)
            return n, eng.value_load(table[0:1, 3, bass.ds(e, 1)], min_val=0, max_val=NBLK)

        def blocks_to(eng, e):
            n, first = blocks_of(eng, e)
            return eng.snap(n + first)

        def units_in_all(eng):
            n, first = units_of(eng, NE - 1)
            return nc.s_assert_within(eng.snap(n + first), 0, NUNIT)

        def each_block(eng, whole, half, rows=False):
            with eng.Fori(0, NE // 2) as i:
                for slot in range(SLOTS):
                    e = eng.snap(i * 2 + slot)
                    units = eng.value_load(table[0:1, 0, bass.ds(e, 1)], min_val=0, max_val=2 * BPE)
                    first = eng.value_load(table[0:1, 3, bass.ds(e, 1)], min_val=0, max_val=NBLK)
                    if rows:
                        first_unit = eng.value_load(table[0:1, 2, bass.ds(e, 1)], min_val=0, max_val=NUNIT)
                    with eng.Fori(0, BPE) as b:
                        with eng.If(b * 2 < units):
                            block = [eng.snap(first + b)]
                            if rows:
                                block.append(nc.s_assert_within(eng.snap(first_unit + b * 2), 0, NUNIT - 1))
                            if half is None:
                                whole(i, slot, *block)
                            else:
                                with eng.If(b * 2 + 1 < units):
                                    whole(i, slot, *block)
                                with eng.Else():
                                    half(i, slot, *block)

        @block.sync
        def _(sp):
            def load_bias(e, slot):
                sp.dma_start(bias[slot][:, :], io["b_gate_up"][bass.ds(e, 1), :].broadcast_to([P, 2 * DE])).then_inc(S[f"bias_in{slot}"], 16)

            def load_down_bias(e):
                sp.dma_start(down_bias[:, :], io["b_down"][bass.ds(e, 1), :].broadcast_to([P, D])).then_inc(S["down_bias_in"], 16)

            def load_down(e, half):
                w = io["w_down"][bass.ds(e, 1), half * 512:(half + 1) * 512, :].rearrange("a (k p) n -> p (a k) n", p=P)
                sp.dma_start(down[:, half, :, :], w).then_inc(S[f"down_in{half}"], 16)

            def load_gate_up(e, slot, q):
                sp.dma_start(gu[slot][:, q, :, :], gate_up_quarter(io, e, q)).then_inc(gu_in[slot][q], 16)

            for half in range(2):
                load_down(0, half)
            load_bias(0, 0)
            load_down_bias(0)
            for q in range(4):
                load_gate_up(1, 1, q)
            load_bias(1, 1)
            with sp.Fori(0, NE // 2 - 1) as i:
                for slot in range(SLOTS):
                    e, later = sp.snap(i * 2 + slot + 1), sp.snap(i * 2 + slot + 2)
                    end = blocks_to(sp, sp.snap(i * 2 + slot))
                    for q in range(4):
                        sp.wait_ge(gu_in[slot][q], i * 16 + 16)
                        sp.sem_inc(S["pieces_in"], 1)
                        sp.wait_ge(S["gate_up"], end * 4 + q + 1)
                        load_gate_up(later, slot, q)
                    for half in range(2):
                        sp.wait_ge(S[f"down_in{half}"], e * 16)
                        sp.sem_inc(S["pieces_in"], 1)
                        sp.wait_ge(S["down"], end * 2 + half + 1)
                        load_down(e, half)
                    sp.wait_ge(S[f"bias_in{slot}"], i * 16 + 16)
                    sp.sem_inc(S["pieces_in"], 1)
                    sp.wait_ge(S["down_bias_in"], e * 16)
                    sp.sem_inc(S["pieces_in"], 1)
                    sp.wait_ge(S["y"], end + 1)
                    load_down_bias(e)
                    load_bias(later, slot)
            end = blocks_to(sp, NE - 2)
            for half in range(2):
                sp.wait_ge(S[f"down_in{half}"], 16 * (NE - 1))
                sp.wait_ge(S["down"], end * 2 + half + 1)
                load_down(NE - 1, half)
            sp.wait_ge(S["down_bias_in"], 16 * (NE - 1))
            sp.wait_ge(S["y"], end + 1)
            load_down_bias(NE - 1)
            for half in range(2):
                sp.wait_ge(S[f"down_in{half}"], 16 * NE)
            sp.wait_ge(S["down_bias_in"], 16 * NE)
            for slot in range(SLOTS):
                sp.wait_ge(S[f"bias_in{slot}"], 16 * (NE // 2))
                for q in range(4):
                    sp.wait_ge(gu_in[slot][q], 16 * (NE // 2))

        @block.gpsimd
        def _(pool):
            nc.gpsimd.memset(yrow[:, :], 0.0).then_inc(S["blank"], 1)
            pool.dma_start(rowtok[:, :], bass.AP(dram["row_token"].tensor, dram["row_token"].offset, [[1, P], [HALF, NUNIT + 1], [1, 1]]),
                           allow_slow_non_contiguous=True).then_inc(S["rowtok_in"], 16)
            identity(nc, pool, ident, S["ident"])
            pool.wait_ge(S["rowtok_in"], 16)

            def gather(i, slot, g, unit):
                pool.wait_ge(S["x_turned"], g + 1)
                nc.gpsimd.tensor_copy(idx[:, :], rowtok[:, bass.ds(unit, 1)]).then_inc(S["index"], 1)
                pool.wait_ge(S["index"], g + 1)
                pool.sem_inc(S["gathers"], 1)
                pool.indirect_dma_start(out=xg[:, :], out_offset=None, in_=dram["h2"],
                                        in_offset=bass.IndirectOffsetOnAxis(ap=idx[:, 0:1], axis=0)).then_inc(S["rows_in"], 16)

            each_block(pool, gather, None, rows=True)
            gather(None, None, blocks_to(pool, NE - 1), units_in_all(pool))

        @block.tensor
        def _(pe):
            pe.sem_inc(S["gate_up"], 4)
            pe.sem_inc(S["down"], 2)
            pe.sem_inc(S["x_turned"], 1)
            pe.wait_ge(S["ident"], 2)

            def turn_rows():
                for k in range(KD):
                    last = nc.tensor.transpose(psT[:, k // 4, (k % 4) * P:(k % 4 + 1) * P], xg[:, k * P:(k + 1) * P], ident[:, :])
                last.then_inc(S["x_turned"], 1)

            def turn_activations(half, g):
                pe.wait_ge(S["act"], g * 2 + half + 1)
                for k in range(4):
                    last = nc.tensor.transpose(psG[:, half, k * P:(k + 1) * P], gated[:, half, k * P:(k + 1) * P], ident[:, :])
                last.then_inc(S["act_turned"], 1)

            def multiply_down(half, n):
                for k in range(4):
                    last = nc.tensor.matmul(psD[:, n, :], actT[:, 4 * half + k, :], down[:, half, k, n * 512:(n + 1) * 512],
                                            start=(half == 0 and k == 0), stop=(half == 1 and k == 3))
                return last

            def one_block(i, slot, g):
                pe.wait_ge(S["xT"], g + 1)
                for q in range(4):
                    pe.wait_ge(gu_in[slot][q], i * 16 + 16)
                    for k in range(KD):
                        last = nc.tensor.matmul(psG[:, q, :], xT[:, k, :], gu[slot][:, q, k, :], start=(k == 0), stop=(k == KD - 1))
                    last.then_inc(S["gate_up"], 1)
                turn_activations(0, g)
                pe.wait_ge(S["rows_in"], g * 16 + 32)
                turn_rows()
                pe.wait_ge(S["actT"], g * 2 + 1)
                pe.wait_ge(S["down_in0"], i * 32 + 16 * (slot + 1))
                pe.wait_ge(S["y"], g + 1)
                multiply_down(0, 0)
                turn_activations(1, g)
                multiply_down(0, 1).then_inc(S["down"], 1)
                pe.wait_ge(S["actT"], g * 2 + 2)
                pe.wait_ge(S["down_in1"], i * 32 + 16 * (slot + 1))
                multiply_down(1, 0)
                multiply_down(1, 1).then_inc(S["down"], 1)

            def half_block(i, slot, g):
                pe.wait_ge(S["xT"], g + 1)
                for what in range(2):
                    for half in range(2):
                        pe.wait_ge(gu_in[slot][2 * half + what], i * 16 + 16)
                    for k in range(KD):
                        for half in range(2):
                            last = nc.tensor.matmul(psG[half * HALF:(half + 1) * HALF, what, :], xT[:, k, 0:HALF],
                                                    gu[slot][:, 2 * half + what, k, :], start=(k == 0), stop=(k == KD - 1))
                    last.then_inc(S["gate_up"], 1 if what == 0 else 3)
                pe.wait_ge(S["rows_in"], g * 16 + 32)
                turn_rows()
                for part in range(2):
                    pe.wait_ge(S["act"], g * 2 + 1 + part)
                    for k in (2 * part, 2 * part + 1):
                        last = nc.tensor.transpose(psG[:, 2 + part, (k % 2) * P:(k % 2 + 1) * P], gated[:, 0, k * P:(k + 1) * P], ident[:, :])
                    last.then_inc(S["act_turned"], 1)
                for half in range(2):
                    pe.wait_ge(S[f"down_in{half}"], i * 32 + 16 * (slot + 1))
                pe.wait_ge(S["y"], g + 1)
                for k in range(4):
                    if k % 2 == 0:
                        pe.wait_ge(S["actT"], g * 2 + 1 + k // 2)
                    for half in range(2):
                        for n in range(2):
                            last = nc.tensor.matmul(psD[n * HALF:(n + 1) * HALF, 0, :], actT[:, k, half * HALF:(half + 1) * HALF],
                                                    down[:, half, k, n * 512:(n + 1) * 512], start=(half == 0 and k == 0),
                                                    stop=(half == 1 and k == 3))
                last.then_inc(S["down"], 2)

            pe.wait_ge(S["rows_in"], 16)
            turn_rows()
            each_block(pe, one_block, half_block)

        @block.scalar
        def _(act):
            act.sem_inc(S["y_out"], 32)

            def move_rows():
                nc.scalar.copy(xT[:, :, :].rearrange("p k t -> p (k t)"), psT[:, :, :].rearrange("p a b -> p (a b)")).then_inc(S["xT"], 1)

            def move_activations(half, g):
                act.wait_ge(S["act_turned"], g * 2 + half + 1)
                nc.scalar.copy(actT[:, 4 * half:4 * half + 4, :].rearrange("p k t -> p (k t)"), psG[:, half, :]).then_inc(S["actT"], 1)

            act.wait_ge(S["blank"], 1)
            units = units_in_all(act)
            with act.Fori(0, NUNIT) as u:
                with act.If(u >= units):
                    act.dma_start(dram["y"][bass.ds(u * HALF, HALF), :], yrow[0:HALF, :]).then_inc(S["blank_out"], 16)
                with act.Else():
                    act.sem_inc(S["blank_out"], 16)
            act.wait_ge(S["x_turned"], 2)
            move_rows()

            def one_block(i, slot, g, unit):
                for half in range(2):
                    act.wait_ge(S["gate_ready"], g * 2 + half + 1)
                    nc.scalar.activation(sig[:, half, :], gated[:, half, :], ACT.Sigmoid, scale=ALPHA).then_inc(S["sig"], 1)
                move_activations(0, g)
                act.wait_ge(S["x_turned"], g + 3)
                move_rows()
                move_activations(1, g)
                act.wait_ge(S["y"], g + 2)
                unit = nc.s_assert_within(unit, 0, NUNIT - 2)
                for rows in range(2):
                    act.dma_start(dram["y"][bass.ds(unit * HALF + rows * HALF, HALF), :],
                                  yrow[rows * HALF:(rows + 1) * HALF, :]).then_inc(S["y_out"], 16)

            def half_block(i, slot, g, unit):
                act.wait_ge(S["gate_ready"], g * 2 + 2)
                nc.scalar.activation(sig[:, 0, :], gated[:, 0, :], ACT.Sigmoid, scale=ALPHA).then_inc(S["sig"], 2)
                act.wait_ge(S["x_turned"], g + 3)
                move_rows()
                for part in range(2):
                    act.wait_ge(S["act_turned"], g * 2 + 1 + part)
                    nc.scalar.copy(actT[:, 2 * part:2 * part + 2, :].rearrange("p k t -> p (k t)"),
                                   psG[:, 2 + part, 0:2 * P]).then_inc(S["actT"], 1)
                act.wait_ge(S["y"], g + 2)
                for n in range(2):
                    act.dma_start(dram["y"][bass.ds(unit * HALF, HALF), n * 512:(n + 1) * 512],
                                  yrow[n * HALF:(n + 1) * HALF, 0:512]).then_inc(S["y_out"], 16)

            each_block(act, one_block, half_block, rows=True)
            act.wait_ge(S["y_out"], blocks_to(act, NE - 1) * 32 + 32)
            act.sem_inc(S["stored"], 1)

        @block.vector
        def _(dve):
            STEPS = 12
            dve.sem_inc(S["y"], 1)

            def counted(g):
                done = [0]

                def link(ins, by=1):
                    done[0] += by
                    ins.then_inc(S["vec"], by)
                    dve.wait_ge(S["vec"], g * STEPS + done[0])
                    assert done[0] <= STEPS

                return link

            def one_block(i, slot, g):
                brow, link = bias[slot], counted(g)
                dve.wait_ge(S[f"bias_in{slot}"], i * 16 + 16)
                for half in range(2):
                    c = half * 512
                    dve.wait_ge(S["gate_up"], g * 4 + 4 + 2 * half + 1)
                    link(nc.vector.tensor_tensor(gated[:, half, :], psG[:, 2 * half, :], brow[:, c:c + 512], ALU.add))
                    link(nc.vector.tensor_scalar(gated[:, half, :], gated[:, half, :], LIMIT, None, ALU.min))
                    dve.sem_inc(S["gate_ready"], 1)
                    dve.wait_ge(S["sig"], g * 2 + half + 1)
                    link(nc.vector.tensor_tensor(gated[:, half, :], gated[:, half, :], sig[:, half, :], ALU.mult))
                    dve.wait_ge(S["gate_up"], g * 4 + 4 + 2 * half + 2)
                    link(nc.vector.tensor_tensor(up[:, :], psG[:, 2 * half + 1, :], brow[:, DE + c:DE + c + 512], ALU.add))
                    link(nc.vector.tensor_scalar(up[:, :], up[:, :], LIMIT, -LIMIT, ALU.min, ALU.max))
                    link(nc.vector.scalar_tensor_tensor(gated[:, half, :], up[:, :], 1.0, gated[:, half, :], ALU.add, ALU.mult))
                    dve.sem_inc(S["act"], 1)
                dve.wait_ge(S["down_bias_in"], i * 32 + 16 * (slot + 1))
                dve.wait_ge(S["down"], g * 2 + 4)
                dve.wait_ge(S["y_out"], g * 32 + 32)
                nc.vector.tensor_tensor(yrow[:, :], psD[:, :, :].rearrange("p a b -> p (a b)"), down_bias[:, :], ALU.add).then_inc(S["y"], 1)

            def half_block(i, slot, g):
                brow, link = bias[slot], counted(g)

                def add_bias(out, ps, row, at):
                    for half in range(2):
                        part = slice(half * HALF, (half + 1) * HALF)
                        c = at + half * 512
                        last = nc.vector.tensor_tensor(out[part, :], ps[part, :], row[part, c:c + 512], ALU.add)
                    return last

                dve.wait_ge(S[f"bias_in{slot}"], i * 16 + 16)
                dve.wait_ge(S["gate_up"], g * 4 + 4 + 1)
                link(add_bias(gated[:, 0, :], psG[:, 0, :], brow, 0))
                link(nc.vector.tensor_scalar(gated[:, 0, :], gated[:, 0, :], LIMIT, None, ALU.min))
                dve.sem_inc(S["gate_ready"], 2)
                dve.wait_ge(S["sig"], g * 2 + 2)
                link(nc.vector.tensor_tensor(gated[:, 0, :], gated[:, 0, :], sig[:, 0, :], ALU.mult))
                dve.wait_ge(S["gate_up"], g * 4 + 4 + 4)
                link(add_bias(up[:, :], psG[:, 1, :], brow, DE))
                link(nc.vector.tensor_scalar(up[:, :], up[:, :], LIMIT, -LIMIT, ALU.min, ALU.max))
                for part in range(2):
                    c = slice(part * 256, (part + 1) * 256)
                    link(nc.vector.scalar_tensor_tensor(gated[:, 0, c], up[:, c], 1.0, gated[:, 0, c], ALU.add, ALU.mult),
                         1 if part == 0 else STEPS - 6)
                    dve.sem_inc(S["act"], 1)
                dve.wait_ge(S["down_bias_in"], i * 32 + 16 * (slot + 1))
                dve.wait_ge(S["down"], g * 2 + 4)
                dve.wait_ge(S["y_out"], g * 32 + 32)
                add_bias(yrow[:, 0:512], psD[:, 0, :], down_bias, 0).then_inc(S["y"], 1)

            dve.wait_ge(S["blank_out"], NUNIT * 16)
            each_block(dve, one_block, half_block)


def phase_combine(nc, kit, keep, io, dram, out):
    scope = ExitStack()
    with scope:
        dest, gate = keep["dest"], keep["gate"]
        rows = kit.sb(scope, "g2_row", [P, D])
        yk = kit.sb(scope, "y_of_token", [P, 3, TOPK, D])
        x1 = kit.sb(scope, "x1_again", [P, 2, D])
        f = kit.sb(scope, "ffn_sum", [P, 2, D])
        sq = kit.sb(scope, "ffn_squares", [P, 2, D])
        o = kit.sb(scope, "out_tile", [P, 2, D])
        st = kit.sb(scope, "ffn_stat", [P, NT, 2])
        eps = kit.sb(scope, "eps_g", [P, 1])
        S = {n: kit.sem("g_" + n) for n in ("row_in", "eps", "x_in0", "x_in1", "y_in0", "y_in1", "y_in2", "vec", "summed", "sq", "std", "ready",
                                            "out0", "out1")}
        block = scope.enter_context(nc.Block())

        @block.sync
        def _(sp):
            sp.dma_start(rows[:, :], row_of(dram["vectors"], D, 3 * D)).then_inc(S["row_in"], 16)
            for t in range(NT):
                if t >= 2:
                    sp.wait_ge(S["ready"], t - 1)
                sp.dma_start(x1[:, t % 2, :], dram["x1"][t * P:(t + 1) * P, :]).then_inc(S[f"x_in{t % 2}"], 16)

        @block.gpsimd
        def _(pool):
            nc.gpsimd.memset(eps[:, :], EPS).then_inc(S["eps"], 1)
            for t in range(NT):
                if t >= 3:
                    pool.wait_ge(S["summed"], t - 2)
                for k in range(TOPK):
                    pool.indirect_dma_start(out=yk[:, t % 3, k, :], out_offset=None, in_=dram["y"],
                                            in_offset=bass.IndirectOffsetOnAxis(ap=dest[:, t * TOPK + k:t * TOPK + k + 1], axis=0)
                                            ).then_inc(S[f"y_in{t % 3}"], 16)

        @block.scalar
        def _(act):
            act.wait_ge(S["eps"], 1)
            for t in range(NT):
                act.wait_ge(S["summed"], t + 1)
                if t >= 2:
                    act.wait_ge(S["sq"], t - 1)
                nc.scalar.activation(sq[:, t % 2, :], f[:, t % 2, :], ACT.Square, accum_out=st[:, t, 0:1]).then_inc(S["sq"], 1)
                act.wait_ge(S["sq"], t + 1)
                nc.scalar.activation(st[:, t, 1:2], st[:, t, 0:1], ACT.Sqrt, bias=eps[:, 0:1], scale=1.0 / D).then_inc(S["std"], 1)
                act.wait_ge(S["ready"], t + 1)
                act.dma_start(out[t * P:(t + 1) * P, :], o[:, t % 2, :]).then_inc(S[f"out{t % 2}"], 16)
            for i in range(2):
                act.wait_ge(S[f"out{i}"], 16 * NT // 2)

        @block.vector
        def _(dve):
            link = linked(dve, S["vec"])
            dve.wait_ge(S["row_in"], 16)
            for t in range(NT):
                dve.wait_ge(S[f"y_in{t % 3}"], 16 * TOPK * (t // 3 + 1))
                ft = f[:, t % 2, :]
                link(nc.vector.tensor_scalar(ft, yk[:, t % 3, 0, :], gate[:, t * TOPK:t * TOPK + 1], None, ALU.mult))
                for k in range(1, TOPK):
                    link(nc.vector.scalar_tensor_tensor(ft, yk[:, t % 3, k, :], gate[:, t * TOPK + k:t * TOPK + k + 1], ft, ALU.mult, ALU.add))
                dve.sem_inc(S["summed"], 1)
                dve.wait_ge(S["std"], t + 1)
                link(nc.vector.reciprocal(st[:, t, 1:2], st[:, t, 1:2]))
                if t >= 2:
                    dve.wait_ge(S[f"out{t % 2}"], 16 * (t // 2))
                link(nc.vector.scalar_tensor_tensor(o[:, t % 2, :], ft, st[:, t, 1:2], rows[:, :], ALU.mult, ALU.mult))
                dve.wait_ge(S[f"x_in{t % 2}"], 16 * (t // 2 + 1))
                nc.vector.tensor_tensor(o[:, t % 2, :], o[:, t % 2, :], x1[:, t % 2, :], ALU.add).then_inc(S["ready"], 1)


def attention_constants():
    q = np.arange(GRID_W)
    lo = np.clip(q - NA_COLS // 2, 0, GRID_W - NA_COLS)
    inside = (q[None, :] >= lo[:, None]) & (q[None, :] < lo[:, None] + NA_COLS)
    m = np.where(inside, 0.0, MASKED).astype(np.float32)
    return {"na_col_mask": np.concatenate([m, m])}


def build_layer(nc, io, out):
    top = ExitStack()
    with top:
        kit = Kit(nc, top)
        dram = {
            "vectors": nc.dram_tensor("vectors_dram", [4 * D], F32, kind="Internal").ap(),
            "x1": nc.dram_tensor("x1_dram", [T, D], F32, kind="Internal").ap(),
            "h2": nc.dram_tensor("h2_dram", [T, D], F32, kind="Internal").ap(),
            "row_token": nc.dram_tensor("row_token_dram", [ROW_LIST, 1], I32, kind="Internal").ap(),
            "y": nc.dram_tensor("y_dram", [NROW, D], F32, kind="Internal").ap(),
        }
        keep = {"dest": kit.sb(top, "dest", [P, NT * TOPK], I32), "gate": kit.sb(top, "gate", [P, NT * TOPK]),
                "table": kit.sb(top, "table", [1, 4, NE], I32)}
        with ExitStack() as mixed:
            keep["modT"] = kit.sb(mixed, "modT", [P, 6 * KD, 2])
            keep["hT"] = keep["mixT"] = kit.sb(mixed, "hT_mixT", [P, KD, TA])
            with ExitStack() as convolved:
                keep["hyT"] = kit.sb(convolved, "hyT", [P, NHT, T])
                with ExitStack() as scanned:
                    keep["xbcT"] = kit.sb(scanned, "xbcT", [P, NXT, TA])
                    keep["z"] = kit.sb(scanned, "z", [P, NT, SSD_W])
                    keep["dt"] = kit.sb(scanned, "dt", [P, NT + NTC, 2 * SSD_H])
                    with ExitStack() as attended:
                        keep["qT"] = kit.sb(attended, "qT", [P, NQT, T])
                        keep["kT"] = kit.sb(attended, "kT", [P, NQT, TA])
                        keep["v"] = kit.sb(attended, "v", [P, NT + NTC, NA_W])
                        phase_project(nc, kit, keep, io)
                        phase_attention(nc, kit, keep, io)
                    phase_ssd(nc, kit, keep, io)
                kit.recycle()
                phase_hyena(nc, kit, keep, io)
            weights = first_weights(kit, top)
            phase_mix(nc, kit, keep, io, dram, weights)
        phase_experts(nc, kit, keep, weights, io, dram)
        phase_combine(nc, kit, keep, io, dram, out)


def lay_out(x, c, ctx, c_ctx, w_mod, b_mod, norm_g, w_in, ssd_conv_w, ssd_conv_b, ssd_a_log, ssd_dt_bias, ssd_d, ssd_norm_g, na_rpb,
            hy_conv_w, hy_conv_b, hy_f_w1, hy_f_b1, hy_f_w2, hy_f_b2, hy_f_w3, hy_freq, hy_d, w_out, w_router, b_router, w_gate_up,
            b_gate_up, w_down, b_down):
    def col(a):
        return a.reshape(-1, P).T

    def cols(a):
        return a.T.reshape(-1, P, a.shape[0]).transpose(1, 0, 2)

    rpb = np.zeros((NA_H, 2 * NA_ROWS + 1, 2 * GRID_W - 1), np.float32)
    rpb[:, 1:2 * NA_ROWS, GRID_W - NA_COLS:GRID_W + NA_COLS - 1] = na_rpb[0].transpose(2, 0, 1)
    skewed = np.stack([rpb[:, 1 - half:1 - half + 2 * NA_ROWS, GRID_W - 1 - qc:2 * GRID_W - 1 - qc]
                       for half in range(2) for qc in range(GRID_W)])
    g = norm_g[0]
    hy_b = np.stack([hy_f_b1[0], hy_f_b2[0]], -1)
    a = {
        "x": x[0], "x_t": x[0].T, "ctx_t": ctx[0].T, "w_mod": w_mod[0], "w_in": w_in[0],
        "c_col": np.stack([col(c[0]), col(c_ctx)], -1), "b_mod_col": col(b_mod[0]), "gain0_col": col(g[0]),
        "gains_col": g[1:].reshape(3, KD, P).transpose(2, 0, 1),
        "ssd_conv_col": cols(np.concatenate([ssd_conv_w[0], ssd_conv_b])),
        "hy_conv_col": cols(np.concatenate([hy_conv_w[0], hy_conv_b])),
        "rpb_skewed": skewed, "dt_bias": ssd_dt_bias[0].reshape(-1), "a_log": ssd_a_log[0].reshape(-1), "ssd_d": ssd_d[0],
        "ssd_norm_col": col(ssd_norm_g[0]),
        "hy_f_w1": hy_f_w1[0], "hy_f_w2": hy_f_w2[0], "hy_f_w3": hy_f_w3[0],
        "hy_bias_freq": np.stack([hy_b, hy_freq[0].T], -1), "hy_d": hy_d,
        "w_out": w_out[0], "w_router": w_router[0], "b_router": b_router[0], "w_gate_up": w_gate_up[0], "b_gate_up": b_gate_up[0],
        "w_down": w_down[0], "b_down": b_down[0],
    }
    return {**a, **hyena_constants(), **attention_constants()}


def kernel(**inputs):
    import concourse.bacc as bacc
    from concourse.bass_utils import run_bass_kernel_spmd

    nc = bacc.Bacc("TRN2", target_bir_lowering=False, num_devices=1)
    arrays, io = {}, {}
    for name, a in lay_out(**{k: np.asarray(v) for k, v in inputs.items()}).items():
        a = np.ascontiguousarray(a)
        arrays[f"in_{name}"] = a
        io[name] = nc.dram_tensor(f"in_{name}", a.shape, mybir.dt.from_np(a.dtype), kind="ExternalInput").ap()
    out = nc.dram_tensor("out_0", (1, T, D), F32, kind="ExternalOutput").ap()
    build_layer(nc, io, out[0])
    r = run_bass_kernel_spmd(nc, [arrays], core_ids=[0])
    return r.results[0]["out_0"]
```

```python
import numpy as np
import concourse.bass as bass
from concourse import mybir
from contextlib import ExitStack


F32 = mybir.dt.float32
I32 = mybir.dt.int32
U32 = mybir.dt.uint32
ALU = mybir.AluOpType
ACT = mybir.ActivationFunctionType
AXX = mybir.AxisListType.X

P = 128
Q = P // 4
D = 1024
T = 1024
TC = 256
TA = T + TC
KD = D // P
NT, NTC = T // P, TC // P
EPS = 1e-6
SSD_H, HD, NGRP, NST, SSD_W = 6, 64, 2, 128, 384
GW = SSD_W // NGRP
XBC = SSD_W + 2 * NGRP * NST
NA_W, HY_W = 384, 256
OFF_XBC = SSD_W
OFF_DT = OFF_XBC + XBC
OFF_Q = OFF_DT + 2 * SSD_H
OFF_K, OFF_V = OFF_Q + NA_W, OFF_Q + 2 * NA_W
OFF_HY = OFF_V + NA_W
NXT, NQT, NHT = XBC // P, NA_W // P, 3 * HY_W // P
NXT_CTX = (SSD_W + NGRP * NST) // P
SSD_K, HY_K = 5, 3
NE, TOPK, DE = 32, 4, 1024
LIMIT, ALPHA = 7.0, 1.702


class Kit:

    def __init__(self, nc, top):
        self.nc, self.top, self.sems = nc, top, []

    def sem(self, name):
        self.sems.append(self.nc.alloc_semaphore(name=name))
        return self.sems[-1]

    def recycle(self):
        self.nc.clear_and_free_semaphores(self.sems)
        self.nc.all_engine_barrier()
        self.sems = []

    def sb(self, scope, name, shape, dt=F32, side=None):
        return scope.enter_context(self.nc.sbuf_tensor("sb_" + name, shape, dt, side=side))

    def ps(self, scope, name, shape):
        return scope.enter_context(self.nc.psum_tensor(name, shape, F32))


def linked(eng, sem):
    n = [0]

    def link(ins):
        n[0] += 1
        ins.then_inc(sem, 1)
        eng.wait_ge(sem, n[0])

    return link


def phase_project(nc, kit, keep, io):
    scope = ExitStack()
    with scope:
        hT = keep["hT"]
        ring = kit.sb(scope, "w_ring", [P, 4, KD, 2 * P])
        wtok = kit.sb(scope, "w_tok", [P, KD, NA_W])
        rstd = kit.sb(scope, "rstd", [P, TA])
        ccol = kit.sb(scope, "c_col", [P, KD, 2])
        scol = kit.sb(scope, "silu_c_col", [P, KD, Q])
        mod_part = kit.sb(scope, "mod_parts", [P, 2 * P])
        fold = kit.sb(scope, "fold", [P, 2])
        bmod = kit.sb(scope, "b_mod_col", [P, 6 * KD])
        gcol = kit.sb(scope, "gain0_col", [P, KD])
        amul = kit.sb(scope, "norm_scale_col", [P, KD, 2])
        cw = kit.sb(scope, "ssd_conv_col", [P, NXT, SSD_K + 1])
        hw = kit.sb(scope, "hy_conv_col", [P, NHT, HY_K + 1])
        ones = kit.sb(scope, "ones_a", [P, P])
        eps = kit.sb(scope, "eps_a", [P, 1])
        modT, xbcT, qT, kT, hyT = keep["modT"], keep["xbcT"], keep["qT"], keep["kT"], keep["hyT"]
        v, z, dt = keep["v"], keep["z"], keep["dt"]
        acc = [kit.ps(scope, f"acc{i}", [P, 1536]) for i in range(2)]
        pmod = kit.ps(scope, "pmod", [P, 512])
        ppart = kit.ps(scope, "pmod_parts", [P, 512])

        small_in = kit.sem("a_small_in")
        x_in = [kit.sem(f"a_x_in{k}") for k in range(KD)]
        ring_in = [kit.sem(f"a_ring_in{i}") for i in range(4)]
        ring_used = kit.sem("a_ring_used")
        wtok_in = kit.sem("a_wtok_in")
        consts = kit.sem("a_consts")
        silu_done = kit.sem("a_silu_done")
        part_copied = kit.sem("a_part_copied")
        folded = kit.sem("a_folded")
        fold_ready = kit.sem("a_fold_ready")
        sq_done = kit.sem("a_sq_done")
        sq_used = kit.sem("a_sq_used")
        std_done = kit.sem("a_std_done")
        h_done = kit.sem("a_h_done")
        tile_done = kit.sem("a_tile_done")
        tile_convolved = kit.sem("a_tile_convolved")
        tile_copied = kit.sem("a_tile_copied")
        conv_done = kit.sem("a_conv_done")
        silu_x = kit.sem("a_silu_x")
        vec = kit.sem("a_vec")

        n_mod1 = 2 * KD // 2
        n_mod = 6 * KD // 2
        chan = [("x", m, OFF_XBC + m * P) for m in range(NXT)]
        chan += [("h", m, OFF_HY + m * P) for m in range(NHT)]
        chan += [("q", m, OFF_Q + m * P) for m in range(NQT)] + [("k", m, OFF_K + m * P) for m in range(NQT)]
        loads = [("mod", m) for m in range(n_mod1)]
        for c in range(len(chan)):
            loads.append(("in", c))
            if n_mod1 + c < n_mod:
                loads.append(("mod", n_mod1 + c))
        position = {c: n + 1 for n, (kind, c) in enumerate(loads) if kind == "in"}
        mod_position = {m: n + 1 for n, (kind, m) in enumerate(loads) if kind == "mod"}
        z_slots = (len(loads) % 4, (len(loads) + 1) % 4)
        Z0 = 2 * P
        tok = [("v", t) for t in range(NT + NTC)] + [("z", t) for t in range(NT + NTC)]
        wmod = io["w_mod"].rearrange("(k p) n -> p k n", p=P)
        win = io["w_in"].rearrange("(k p) n -> p k n", p=P)

        n_conv = NXT + NHT

        def accumulator_free(pe, n):
            if n - 2 >= n_conv:
                pe.wait_ge(tile_copied, n - 2 - n_conv + 1)
            elif n >= 2:
                pe.wait_ge(tile_convolved, n - 1)

        def has_ctx(c):
            kind, m, _ = chan[c]
            return kind == "k" or (kind == "x" and m < NXT_CTX)

        block = scope.enter_context(nc.Block())

        @block.sync
        def _(sp):
            sp.dma_start(ccol[:, :, :], io["c_col"]).then_inc(small_in, 16)
            sp.dma_start(bmod[:, :], io["b_mod_col"]).then_inc(small_in, 16)
            sp.dma_start(gcol[:, :], io["gain0_col"]).then_inc(small_in, 16)
            sp.dma_start(cw[:, :, :], io["ssd_conv_col"]).then_inc(small_in, 16)
            sp.dma_start(hw[:, :, :], io["hy_conv_col"]).then_inc(small_in, 16)
            for k in range(KD):
                sp.dma_start(hT[:, k, 0:T], io["x_t"][k * P:(k + 1) * P, :]).then_inc(x_in[k], 16)
                sp.dma_start(hT[:, k, T:TA], io["ctx_t"][k * P:(k + 1) * P, :]).then_inc(x_in[k], 16)
            for n, (kind, m) in enumerate(loads):
                if n >= 4:
                    sp.wait_ge(ring_used, n - 3)
                if kind == "mod":
                    sp.dma_start(ring[:, n % 4, :, :], wmod[:, :, 2 * P * m:2 * P * (m + 1)]).then_inc(ring_in[n % 4], 16)
                else:
                    off = chan[m][2]
                    sp.dma_start(ring[:, n % 4, :, 0:P], win[:, :, off:off + P]).then_inc(ring_in[n % 4], 16)
            sp.dma_start(wtok[:, :, :], win[:, :, OFF_V:OFF_V + NA_W]).then_inc(wtok_in, 16)
            sp.wait_ge(ring_used, len(loads) - 2)
            a, b = z_slots
            sp.dma_start(ring[:, a, :, :], win[:, :, 0:Z0]).then_inc(ring_in[a], 16)
            sp.dma_start(ring[:, b, :, 0:SSD_W - Z0], win[:, :, Z0:SSD_W]).then_inc(ring_in[b], 16)
            sp.dma_start(ring[:, b, :, SSD_W - Z0:SSD_W - Z0 + 2 * SSD_H], win[:, :, OFF_DT:OFF_Q]).then_inc(ring_in[b], 16)

        @block.gpsimd
        def _(pool):
            nc.gpsimd.memset(fold[:, :], 0.0).then_inc(fold_ready, 1)
            nc.gpsimd.memset(scol[:, :, :], 0.0).then_inc(consts, 1)
            for j in range(P // Q):
                pool.wait_ge(fold_ready, j + 1)
                nc.gpsimd.affine_select(out=fold[:, :], in_=fold[:, :], compare_op=ALU.not_equal, fill=1.0, base=-Q * j,
                                        pattern=[[-1, 2]], channel_multiplier=1).then_inc(fold_ready, 1)
            nc.gpsimd.memset(ones[:, :], 1.0).then_inc(consts, 1)
            nc.gpsimd.memset(eps[:, :], EPS).then_inc(consts, 1)

        @block.tensor
        def _(pe):
            n = 0

            def multiply_mod(n, m):
                for k in range(KD):
                    q = slice(k % 4 * Q, (k % 4 + 1) * Q)
                    last = nc.tensor.matmul(ppart[q, 0:2 * P], scol[:, k, :], ring[:, n % 4, k, :], start=(k < 4), stop=(k >= 4))
                last.then_inc(ring_used, 1)

            def fold_mod(m):
                pe.wait_ge(part_copied, m + 1)
                for h in range(2):
                    at = 2 * (2 * m + h)
                    last = nc.tensor.matmul(pmod[:, at:at + 2], mod_part[:, h * P:(h + 1) * P], fold[:, :], start=True, stop=True)
                last.then_inc(folded, 1)

            pe.wait_ge(consts, 3)
            for k in range(KD):
                pe.wait_ge(sq_done, k + 1)
                for a, b in ((0, 512), (512, 1024), (1024, TA)):
                    last = nc.tensor.matmul(acc[0][:, a:b], ones[:, :], xbcT[:, k % 4, a:b],
                                            start=(k == 0), stop=(k == KD - 1), skip_group_check=True)
                last.then_inc(sq_used, 1)
            pe.wait_ge(silu_done, 1)
            pe.wait_ge(fold_ready, 1 + P // Q)
            used = [0, 0, 0, 0]
            tiles = 0
            for n, (kind, m) in enumerate(loads):
                used[n % 4] += 16
                pe.wait_ge(ring_in[n % 4], used[n % 4])
                if kind == "mod":
                    if m >= 1 and m != n_mod1:
                        fold_mod(m - 1)
                    multiply_mod(n, m)
                    if m in (n_mod1 - 1, n_mod - 1):
                        fold_mod(m)
                    continue
                if tiles == 0:
                    pe.wait_ge(std_done, 1)
                accumulator_free(pe, tiles)
                a = acc[tiles % 2]
                parts = [((0, 512), (512, T))] + ([((T, TA),)] if has_ctx(m) else [])
                for part, columns in enumerate(parts):
                    for k in range(KD):
                        if tiles == 0:
                            pe.wait_ge(h_done, part * KD + k + 1)
                        for lo, hi in columns:
                            last = nc.tensor.matmul(a[:, lo:hi], ring[:, n % 4, k, 0:P], hT[:, k, lo:hi], start=(k == 0), stop=(k == KD - 1),
                                                    skip_group_check=True)
                last.then_inc(ring_used, 1)
                tiles += 1
            for i, (kind, t) in enumerate(tok):
                if i == 0:
                    pe.wait_ge(wtok_in, 16)
                if kind == "z" and t == 0:
                    pe.wait_ge(ring_in[z_slots[0]], used[z_slots[0]] + 16)
                    pe.wait_ge(ring_in[z_slots[1]], used[z_slots[1]] + 32)
                accumulator_free(pe, tiles)
                a = acc[tiles % 2]
                if kind == "v":
                    parts = [(0, NA_W, wtok, 0)]
                else:
                    parts = [(0, Z0, ring[:, z_slots[0]], 0)] if t < NT else []
                    lo = Z0 if t < NT else SSD_W
                    parts.append((lo, SSD_W + 2 * SSD_H, ring[:, z_slots[1]], lo - Z0))
                for lo, hi, w, at in parts:
                    for k in range(KD):
                        last = nc.tensor.matmul(a[:, lo:hi], hT[:, k, t * P:(t + 1) * P], w[:, k, at:at + hi - lo],
                                                start=(k == 0), stop=(k == KD - 1), skip_group_check=True)
                last.then_inc(tile_done, 1)
                tiles += 1

        @block.scalar
        def _(act):
            act.wait_ge(small_in, 80)
            act.wait_ge(consts, 3)
            nc.scalar.activation(scol[:, :, 0:2], ccol[:, :, :], ACT.Silu).then_inc(silu_done, 1)
            for k in range(KD):
                act.wait_ge(x_in[k], 32)
                if k >= 4:
                    act.wait_ge(sq_used, k - 3)
                nc.scalar.activation(xbcT[:, k % 4, :], hT[:, k, :], ACT.Square).then_inc(sq_done, 1)
            act.wait_ge(sq_used, KD)
            act.wait_ge(consts, 3)
            nc.scalar.activation(rstd[:, :], acc[0][:, 0:TA], ACT.Sqrt, bias=eps[:, 0:1], scale=1.0 / D).then_inc(std_done, 1)

            def copy_part(m):
                act.wait_ge(ring_used, mod_position[m])
                if m >= 1:
                    act.wait_ge(folded, m)
                nc.scalar.copy(mod_part[:, :], ppart[:, 0:2 * P]).then_inc(part_copied, 1)

            for m in range(n_mod1):
                copy_part(m)
            for c, (kind, m, _) in enumerate(chan):
                if kind == "x":
                    act.wait_ge(conv_done, m + 1)
                    hi = TA if has_ctx(c) else T
                    nc.scalar.activation(xbcT[:, m, 0:hi], xbcT[:, m, 0:hi], ACT.Silu).then_inc(silu_x, 1)
                elif kind in "qk":
                    act.wait_ge(ring_used, position[c])
                    dst = qT[:, m, :] if kind == "q" else kT[:, m, :]
                    nc.scalar.copy(dst, acc[c % 2][:, 0:(T if kind == "q" else TA)]).then_inc(tile_copied, 1)
                if n_mod1 + c < n_mod:
                    copy_part(n_mod1 + c)
            for i, (kind, t) in enumerate(tok):
                a = acc[(len(chan) + i) % 2]
                act.wait_ge(tile_done, i + 1)
                if kind == "v":
                    nc.scalar.copy(v[:, t, :], a[:, 0:NA_W]).then_inc(tile_copied, 1)
                else:
                    if t < NT:
                        nc.scalar.copy(z[:, t, :], a[:, 0:SSD_W]).then_inc(silu_x, 1)
                    nc.scalar.copy(dt[:, t, :], a[:, SSD_W:SSD_W + 2 * SSD_H]).then_inc(tile_copied, 1)

        @block.vector
        def _(dve):
            link = linked(dve, vec)
            dve.wait_ge(small_in, 80)

            def add_mod_bias(lo, hi):
                pm = pmod[:, 2 * lo:2 * hi].rearrange("p (m s) -> p m s", s=2)
                for s in range(2):
                    link(nc.vector.tensor_tensor(modT[:, lo:hi, s], pm[:, :, s], bmod[:, lo:hi], ALU.add))

            dve.wait_ge(folded, n_mod1)
            add_mod_bias(0, 2 * KD)
            for s in range(2):
                link(nc.vector.tensor_scalar(amul[:, :, s], modT[:, KD:2 * KD, s], 1.0, None, ALU.add))
                link(nc.vector.tensor_tensor(amul[:, :, s], amul[:, :, s], gcol[:, :], ALU.mult))
            dve.wait_ge(std_done, 1)
            link(nc.vector.reciprocal(rstd[:, :], rstd[:, :]))
            for s, (lo, hi) in enumerate(((0, T), (T, TA))):
                for k in range(KD):
                    h = hT[:, k, lo:hi]
                    link(nc.vector.scalar_tensor_tensor(h, h, amul[:, k, s:s + 1], rstd[:, lo:hi], ALU.mult, ALU.mult))
                    nc.vector.tensor_scalar(h, h, modT[:, k, s:s + 1], None, ALU.add).then_inc(h_done, 1)

            def conv(dst, src, w, taps):
                mid, width = taps // 2, src.shape[-1]
                link(nc.vector.tensor_scalar(dst, src, w[:, mid:mid + 1], w[:, taps:taps + 1], ALU.mult, ALU.add))
                for j in [j for j in range(taps) if j != mid]:
                    s = j - mid
                    o, i = (dst[:, 0:width - s], src[:, s:width]) if s > 0 else (dst[:, -s:width], src[:, 0:width + s])
                    last = nc.vector.scalar_tensor_tensor(o, i, w[:, j:j + 1], o, ALU.mult, ALU.add)
                    link(last)

            for c, (kind, m, _) in enumerate(chan):
                if kind == "x" or kind == "h":
                    dve.wait_ge(ring_used, position[c])
                    a = acc[c % 2]
                    if kind == "x":
                        if has_ctx(c):
                            conv(xbcT[:, m, T:TA], a[:, T:TA], cw[:, m, :], SSD_K)
                        conv(xbcT[:, m, 0:T], a[:, 0:T], cw[:, m, :], SSD_K)
                        dve.sem_inc(conv_done, 1)
                    else:
                        conv(hyT[:, m, :], a[:, 0:T], hw[:, m, :], HY_K)
                    dve.sem_inc(tile_convolved, 1)
            dve.wait_ge(folded, n_mod)
            add_mod_bias(2 * KD, 6 * KD)


GRID_W, ROWS, NA_ROWS, NA_COLS, NA_H = 64, T // 64, 8, 16, 6
MASKED = -1e30


def identity(nc, pool, tile, sem):
    nc.gpsimd.memset(tile[:, :], 0.0).then_inc(sem, 1)
    pool.wait_ge(sem, 1)
    nc.gpsimd.affine_select(out=tile[:, :], in_=tile[:, :], compare_op=ALU.not_equal, fill=1.0, base=0,
                            pattern=[[-1, P]], channel_multiplier=1).then_inc(sem, 1)


def phase_attention(nc, kit, keep, io):
    scope = ExitStack()
    with scope:
        qT, kT, v, mixT = keep["qT"], keep["kT"], keep["v"], keep["mixT"]
        NS = 2 * NA_ROWS
        bias = kit.sb(scope, "na_bias", [P, NA_H, NS, GRID_W])
        cmask = kit.sb(scope, "na_col_mask", [P, GRID_W])
        ident = kit.sb(scope, "ident_na", [P, P])
        probs = kit.sb(scope, "na_probs", [P, 2, 832])
        pT = kit.sb(scope, "na_probs_t", [P, 2, 7, P])
        over_sum = kit.sb(scope, "na_over_sum", [P, 2, P])
        items = [(m, h) for h in range(NA_H) for m in range(NT)]
        NI = len(items)
        mx = kit.sb(scope, "na_max", [P, NI, 4])
        sm = kit.sb(scope, "na_sum", [P, NI, 4])
        score = [kit.ps(scope, f"na_score{i}", [P, 1024]) for i in range(2)]
        trA = kit.ps(scope, "na_trA", [P, 512])
        trB = kit.ps(scope, "na_trB", [P, 512])
        out = [kit.ps(scope, f"na_out{i}", [P, 512]) for i in range(2)]
        S = {n: kit.sem("n_" + n) for n in ("mask_in", "ident", "bias_ready", "scored", "max_ready", "exped", "trA_done",
                                            "trB_done", "evA", "evB", "pv", "over_sum", "out_read", "vec")}
        bias_in = [kit.sem(f"n_bias_in{h}") for h in range(NA_H)]
        CTX0 = 576

        def key_rows(m):
            first = max(0, min(2 * m - NA_ROWS // 2, ROWS - NA_ROWS))
            return first, (9 if 2 * m - 4 >= 0 and 2 * m - 3 <= ROWS - NA_ROWS else 8)

        block = scope.enter_context(nc.Block())

        @block.sync
        def _(sp):
            sp.dma_start(cmask[:, :], io["na_col_mask"]).then_inc(S["mask_in"], 16)
            for h in range(NA_H):
                sp.dma_start(bias[:, h, :, :], io["rpb_skewed"][:, h, :, :]).then_inc(bias_in[h], 16)

        @block.gpsimd
        def _(pool):
            identity(nc, pool, ident, S["ident"])
            pool.wait_ge(S["mask_in"], 16)
            for h in range(NA_H):
                pool.wait_ge(bias_in[h], 16)
                m = bass.AP(cmask[:, :].tensor, cmask[:, :].offset, [cmask[:, :].ap[0], [0, NS], [1, GRID_W]])
                nc.gpsimd.tensor_tensor(bias[:, h, :, :], bias[:, h, :, :], m, ALU.add).then_inc(S["bias_ready"], 1)

        @block.tensor
        def _(pe):
            pe.wait_ge(S["ident"], 2)

            def scores(i):
                m, h = items[i]
                r0, nr = key_rows(m)
                lo = (h % 2) * HD
                if i >= 2:
                    pe.wait_ge(S["exped"], i - 1)
                q = qT[lo:lo + HD, h // 2, m * P:(m + 1) * P]
                ps = score[i % 2]
                k0 = r0 * GRID_W
                nc.tensor.matmul(ps[:, 0:512], q, kT[lo:lo + HD, h // 2, k0:k0 + 512], start=True, stop=True)
                if nr == 9:
                    nc.tensor.matmul(ps[:, 512:576], q, kT[lo:lo + HD, h // 2, k0 + 512:k0 + 576], start=True, stop=True)
                nc.tensor.matmul(ps[:, 768:1024], q, kT[lo:lo + HD, h // 2, T:TA], start=True, stop=True).then_inc(S["scored"], 1)

            def transposes(i):
                m, h = items[i]
                pe.wait_ge(S["over_sum"], i + 1)
                if i >= 1:
                    pe.wait_ge(S["evA"], i)
                    pe.wait_ge(S["evB"], i)
                pr, by = probs[:, i % 2, :], over_sum[:, i % 2, :]
                for b in range(4):
                    last = nc.tensor.matmul(trA[:, b * P:(b + 1) * P], pr[:, b * P:(b + 1) * P], by, start=True, stop=True)
                last.then_inc(S["trA_done"], 1)
                if key_rows(m)[1] == 9:
                    nc.tensor.matmul(trB[0:64, 0:P], pr[:, 512:576], by, start=True, stop=True)
                for b in range(2):
                    last = nc.tensor.matmul(trB[:, (b + 1) * P:(b + 2) * P], pr[:, CTX0 + b * P:CTX0 + (b + 1) * P], by,
                                            start=True, stop=True)
                last.then_inc(S["trB_done"], 1)

            def values(i):
                m, h = items[i]
                r0, nr = key_rows(m)
                pe.wait_ge(S["evA"], i + 1)
                pe.wait_ge(S["evB"], i + 1)
                if i >= 2:
                    pe.wait_ge(S["out_read"], i - 1)
                lo = (h % 2) * HD
                o = out[i % 2][lo:lo + HD, 0:P]
                hc = slice(h * HD, (h + 1) * HD)
                t0 = r0 // 2
                for b in range(4):
                    nc.tensor.matmul(o, v[:, t0 + b, hc], pT[:, i % 2, b, :], start=(b == 0), stop=False)
                if nr == 9:
                    nc.tensor.matmul(o, v[0:64, t0 + 4, hc], pT[0:64, i % 2, 4, :], start=False, stop=False)
                for b in range(2):
                    last = nc.tensor.matmul(o, v[:, NT + b, hc], pT[:, i % 2, 5 + b, :], start=False, stop=(b == 1))
                last.then_inc(S["pv"], 1)

            for i in range(NI + 2):
                if i < NI:
                    scores(i)
                if i >= 2:
                    values(i - 2)
                if 1 <= i <= NI:
                    transposes(i - 1)

        @block.scalar
        def _(act):
            for i in range(NI + 2):
                if i < NI:
                    m, h = items[i]
                    w = key_rows(m)[1] * GRID_W
                    act.wait_ge(S["max_ready"], i + 1)
                    pr = probs[:, i % 2, :]
                    nc.scalar.activation(pr[:, 0:w], pr[:, 0:w], ACT.Exp, bias=mx[:, i, 3:4], accum_out=sm[:, i, 0:1])
                    nc.scalar.activation(pr[:, CTX0:832], score[i % 2][:, 768:1024], ACT.Exp, bias=mx[:, i, 3:4],
                                         scale=HD ** -0.5, accum_out=sm[:, i, 1:2]).then_inc(S["exped"], 1)
                if 1 <= i <= NI:
                    j = i - 1
                    act.wait_ge(S["trB_done"], j + 1)
                    if j >= 2:
                        act.wait_ge(S["pv"], j - 1)
                    if key_rows(items[j][0])[1] == 9:
                        nc.scalar.copy(pT[0:64, j % 2, 4, :], trB[0:64, 0:P])
                    nc.scalar.copy(pT[:, j % 2, 5:7, :], trB[:, P:3 * P]).then_inc(S["evB"], 1)
                if i >= 2:
                    j = i - 2
                    m, h = items[j]
                    half = slice((h % 2) * HD, (h % 2 + 1) * HD)
                    act.wait_ge(S["pv"], j + 1)
                    nc.scalar.copy(mixT[half, 3 + h // 2, m * P:(m + 1) * P], out[j % 2][half, 0:P]).then_inc(S["out_read"], 1)

        @block.vector
        def _(dve):
            link = linked(dve, S["vec"])
            for i in range(NI + 1):
                if i >= 1:
                    j = i - 1
                    dve.wait_ge(S["exped"], j + 1)
                    link(nc.vector.tensor_tensor(sm[:, j, 2:3], sm[:, j, 0:1], sm[:, j, 1:2], ALU.add))
                    link(nc.vector.reciprocal(sm[:, j, 3:4], sm[:, j, 2:3]))
                    if j >= 2:
                        dve.wait_ge(S["trB_done"], j - 1)
                    nc.vector.tensor_scalar(over_sum[:, j % 2, :], ident[:, :], sm[:, j, 3:4], None, ALU.mult).then_inc(S["over_sum"], 1)
                if i < NI:
                    m, h = items[i]
                    r0, nr = key_rows(m)
                    w = nr * GRID_W
                    s0 = r0 - 2 * m + NA_ROWS - 1
                    if m == 0:
                        dve.wait_ge(S["bias_ready"], h + 1)
                    dve.wait_ge(S["scored"], i + 1)
                    if i >= 2:
                        dve.wait_ge(S["trB_done"], i - 1)
                    pr, ps = probs[:, i % 2, :], score[i % 2]
                    b = bias[:, h, s0:s0 + nr, :].rearrange("p r c -> p (r c)")
                    link(nc.vector.scalar_tensor_tensor(pr[:, 0:w], ps[:, 0:w], HD ** -0.5, b, ALU.mult, ALU.add))
                    if nr == 9:
                        nc.vector.memset(pr[64:128, 0:64], MASKED)
                        link(nc.vector.memset(pr[0:64, 512:576], MASKED))
                    nc.vector.tensor_reduce(mx[:, i, 0:1], pr[:, 0:w], AXX, ALU.max)
                    link(nc.vector.tensor_reduce(mx[:, i, 1:2], ps[:, 768:1024], AXX, ALU.max))
                    link(nc.vector.tensor_scalar(mx[:, i, 2:3], mx[:, i, 1:2], HD ** -0.5, mx[:, i, 0:1], ALU.mult, ALU.max))
                    nc.vector.tensor_scalar(mx[:, i, 3:4], mx[:, i, 2:3], -1.0, None, ALU.mult).then_inc(S["max_ready"], 1)
                if i >= 1:
                    j = i - 1
                    dve.wait_ge(S["trA_done"], j + 1)
                    if j >= 2:
                        dve.wait_ge(S["pv"], j - 1)
                    nc.vector.tensor_copy(pT[:, j % 2, 0:4, :].rearrange("p a b -> p (a b)"), trA[:, :]).then_inc(S["evA"], 1)


BF16 = mybir.dt.bfloat16


def phase_ssd(nc, kit, keep, io):
    scope = ExitStack()
    with scope:
        xbcT, z, dt, mixT = keep["xbcT"], keep["z"], keep["dt"], keep["mixT"]
        NC = NT + NTC
        order = [NT + n for n in range(NTC)] + list(range(NT))
        H2 = 2 * SSD_H
        brow = kit.sb(scope, "dt_bias_row", [P, H2])
        arow = kit.sb(scope, "a_row", [P, H2])
        drow = kit.sb(scope, "d_skip_row", [P, SSD_H])
        ncol = kit.sb(scope, "ssd_norm_col", [P, 3])
        one = kit.sb(scope, "one_c", [P, 1])
        eps = kit.sb(scope, "eps_c", [P, 1])
        ones = kit.sb(scope, "ones_c", [P, P])
        tri = kit.sb(scope, "tri", [P, 2, P])
        ident = kit.sb(scope, "ident_c", [P, P])
        identb = kit.sb(scope, "ident_bf", [P, P], BF16)
        outside = kit.sb(scope, "outside_bf", [P, 2, P], BF16)
        sp_a = kit.sb(scope, "softplus_a", [P, NC, H2])
        sp_b = kit.sb(scope, "softplus_b", [P, NC, H2])
        dta = kit.sb(scope, "dta", [P, NC, H2])
        acs = kit.sb(scope, "acs", [P, NC, H2])
        nacs = kit.sb(scope, "neg_acs", [P, NC, H2])
        eacs = kit.sb(scope, "exp_acs", [P, NC, H2])
        wdec = kit.sb(scope, "state_weight", [P, NC, H2])
        dec = kit.sb(scope, "chunk_decay", [P, NC, H2])
        xs = kit.sb(scope, "xs_tok", [P, NC, SSD_W])
        btok = kit.sb(scope, "b_tok", [P, 2, NGRP * NST])
        xdec = kit.sb(scope, "x_decayed", [P, 2, 2, SSD_W])
        st = kit.sb(scope, "chunk_state", [P, NC, 2, SSD_W])
        run = kit.sb(scope, "run_state", [P, 2, SSD_W])
        start = kit.sb(scope, "start_state", [P, NT, NGRP, 2, GW])
        trirhs = kit.sb(scope, "tri_dta", [P, 2, SSD_H, P])
        decay = [a.rearrange("p a b c -> p (a b c)").rearrange("p (d h i) -> p d h i", d=2, h=SSD_H)
                 for a in (xdec[:, :, :, :], st[:, NT:NC, :, :])]
        xdt = [run[:, :, :], st[:, 0:2, 1, :]]
        t1 = kit.sb(scope, "ssd_t1", [P, SSD_W])
        t2 = btok[:, :, :].rearrange("p a b -> p (a b)")[:, 0:SSD_W]
        ssq = kit.sb(scope, "ssd_ssq", [P, NT, NGRP])
        squares = st
        y = z
        psG = kit.ps(scope, "psG", [P, 512])
        psY = kit.ps(scope, "psY", [P, 512])
        psI = kit.ps(scope, "psI", [P, 2, 512])
        psA = [kit.ps(scope, f"psA{d}", [P, 2, 512]) for d in range(2)]
        S = {n: kit.sem("s_" + n) for n in ("small_in", "pool", "vec", "actv", "dta_ready", "cum", "acs_ready", "exps", "tr", "ev", "xdec",
                                            "st", "st_ev", "scan", "tri_ready", "G", "A", "E", "W", "intra", "inter", "y_used", "gated",
                                            "ssq", "std", "scaled", "ytr", "mixed", "i_used")}

        def head_cols(ap):
            return bass.AP(ap.tensor, ap.offset, [ap.ap[0], [1, SSD_H], [0, HD]])

        def by_head(ap):
            return ap.rearrange("p (h d) -> p h d", d=HD)

        def g_bcast(g):
            a = psG[:, g * P:(g + 1) * P]
            return bass.AP(a.tensor, a.offset, [a.ap[0], [0, 3], [1, P]])

        def group_squares(act, c):
            act.wait_ge(S["gated"], c + 1)
            for g in range(NGRP):
                last = nc.scalar.activation(squares[:, c, 0, g * GW:(g + 1) * GW], y[:, c, g * GW:(g + 1) * GW], ACT.Square, accum_out=ssq[:, c, g:g + 1])
            last.then_inc(S["ssq"], 1)

        block = scope.enter_context(nc.Block())

        @block.sync
        def _(sp):
            for dst, src in ((brow, "dt_bias"), (arow, "a_log"), (drow, "ssd_d")):
                a = io[src]
                sp.dma_start(dst[:, :], bass.AP(a.tensor, a.offset, [[0, P], [1, a.shape[0]]])).then_inc(S["small_in"], 16)
            sp.dma_start(ncol[:, :], io["ssd_norm_col"]).then_inc(S["small_in"], 16)

        @block.gpsimd
        def _(pool):
            link = linked(pool, S["pool"])
            nc.gpsimd.memset(one[:, :], 1.0)
            nc.gpsimd.memset(eps[:, :], EPS)
            nc.gpsimd.memset(ones[:, :], 1.0)
            nc.gpsimd.memset(outside[:, :, :], 0.0)
            nc.gpsimd.memset(ident[:, :], 0.0)
            nc.gpsimd.memset(identb[:, :], 0.0)
            link(nc.gpsimd.memset(tri[:, :, :], 1.0))
            for m in (ident, identb):
                nc.gpsimd.affine_select(out=m[:, :], in_=m[:, :], compare_op=ALU.not_equal, fill=1.0, base=0,
                                        pattern=[[-1, P]], channel_multiplier=1)
            for m, fill in ((tri, 0.0), (outside, MASKED)):
                nc.gpsimd.affine_select(out=m[:, 0, :], in_=m[:, 0, :], compare_op=ALU.is_ge, fill=fill, base=0,
                                        pattern=[[1, P]], channel_multiplier=-1)
                last = nc.gpsimd.affine_select(out=m[:, 1, :], in_=m[:, 1, :], compare_op=ALU.is_ge, fill=fill, base=0,
                                               pattern=[[-1, P]], channel_multiplier=1)
            link(last)
            pool.wait_ge(S["dta_ready"], 1)
            for c in range(NT):
                if c >= 1:
                    pool.wait_ge(S["A"], c)
                for d in range(2):
                    a = dta[:, c, d * SSD_H:(d + 1) * SSD_H]
                    tr = tri[:, d, :]
                    nc.gpsimd.tensor_tensor(trirhs[:, d, :, :], bass.AP(tr.tensor, tr.offset, [tr.ap[0], [0, SSD_H], [1, P]]),
                                            bass.AP(a.tensor, a.offset, [a.ap[0], [1, SSD_H], [0, P]]),
                                            ALU.mult).then_inc(S["tri_ready"], 1)

        @block.tensor
        def _(pe):
            pe.wait_ge(S["pool"], 2)
            pe.wait_ge(S["dta_ready"], 1)
            for d in range(2):
                hs = slice(d * SSD_H, (d + 1) * SSD_H)
                nc.tensor.matmul(psA[0][:, d, 0:NC * SSD_H].rearrange("p (c h) -> p c h", h=SSD_H), tri[:, d, :], dta[:, :, hs],
                                 start=True, stop=True)
            nc.tensor.matmul(psA[1][:, 0, 0:NC * H2], ones[:, :], dta[:, :, :].rearrange("p c h -> p (c h)"), start=True,
                             stop=True).then_inc(S["cum"], 1)

            def turn(n):
                c = order[n]
                if n >= 1:
                    pe.wait_ge(S["ev"], n)
                for j in range(3):
                    nc.tensor.transpose(psY[:, j * P:(j + 1) * P], xbcT[:, j, c * P:(c + 1) * P], ident[:, :])
                for g in range(NGRP):
                    last = nc.tensor.transpose(psG[:, g * P:(g + 1) * P], xbcT[:, 3 + g, c * P:(c + 1) * P], ident[:, :])
                last.then_inc(S["tr"], 1)

            def states(n):
                pe.wait_ge(S["xdec"], n + 1)
                if n >= 1:
                    pe.wait_ge(S["st_ev"], n)
                for g in range(NGRP):
                    for d in range(2):
                        last = nc.tensor.matmul(psI[:, d, g * GW:(g + 1) * GW], btok[:, n % 2, g * P:(g + 1) * P],
                                                xdec[:, n % 2, d, g * GW:(g + 1) * GW], start=True, stop=True)
                last.then_inc(S["st"], 1)

            for n in range(NC + 1):
                if n < NC:
                    turn(n)
                if n >= 1:
                    states(n - 1)

            def products(c):
                if c >= 1:
                    pe.wait_ge(S["W"], 4 * c)
                for g in range(NGRP):
                    last = nc.tensor.matmul(psG[:, g * P:(g + 1) * P], xbcT[:, 3 + g, c * P:(c + 1) * P],
                                            xbcT[:, 5 + g, c * P:(c + 1) * P], start=True, stop=True)
                last.then_inc(S["G"], 1)

            def decays(c):
                pe.wait_ge(S["exps"], 1)
                if c >= 1:
                    pe.wait_ge(S["E"], 2 * c)
                for d in range(2):
                    pe.wait_ge(S["tri_ready"], 2 * c + d + 1)
                    for h in range(2):
                        nc.tensor.matmul(psA[d][:, h, 0:3 * P], ones[:, :], trirhs[:, d, 3 * h:3 * h + 3, :], start=True, stop=False)
                    for h in range(2):
                        o = outside[:, d, :]
                        last = nc.tensor.matmul(psA[d][:, h, 0:3 * P].rearrange("p (a b) -> p a b", a=3), identb[:, :],
                                                bass.AP(o.tensor, o.offset, [o.ap[0], [0, 3], [1, P]]), start=False, stop=True)
                last.then_inc(S["A"], 1)

            def outputs(c):
                pe.wait_ge(S["scan"], 1)
                if c >= 1:
                    pe.wait_ge(S["i_used"], c)
                for g in range(NGRP):
                    last = nc.tensor.matmul(psI[:, g, 0:2 * GW], xbcT[:, 5 + g, c * P:(c + 1) * P],
                                            start_flat(c, g), start=True, stop=True)
                last.then_inc(S["inter"], 1)
                pe.wait_ge(S["W"], 4 * c + 4)
                if c >= 1:
                    pe.wait_ge(S["y_used"], c)
                for h in range(SSD_H):
                    for d in range(2):
                        last = nc.tensor.matmul(psY[:, h * HD:(h + 1) * HD], decay[c % 2][:, d, h, :], xdt[c % 2][:, d, h * HD:(h + 1) * HD],
                                                start=(d == 0), stop=(d == 1))
                last.then_inc(S["intra"], 1)

            def start_flat(c, g):
                return start[:, c, g, :, :].rearrange("p d w -> p (d w)")

            decays(0)
            for c in range(NT):
                products(c)
                if c + 1 < NT:
                    decays(c + 1)
                outputs(c)
            pe.wait_ge(S["scaled"], 1)
            for n in range(6):
                j, half = n // 2, n % 2
                ps = psY if half == 0 else psG
                if n >= 2:
                    pe.wait_ge(S["mixed"], n - 1)
                for b in range(4):
                    last = nc.tensor.transpose(ps[:, b * P:(b + 1) * P], y[:, 4 * half + b, j * P:(j + 1) * P], ident[:, :])
                last.then_inc(S["ytr"], 1)

        @block.scalar
        def _(act):
            link = linked(act, S["actv"])
            act.wait_ge(S["pool"], 2)
            act.wait_ge(S["small_in"], 64)
            act.wait_ge(S["vec"], 2)
            link(nc.scalar.activation(sp_b[:, :, :], sp_b[:, :, :], ACT.Exp, scale=-1.0))
            link(nc.scalar.activation(arow[:, :], arow[:, :], ACT.Exp))
            link(nc.scalar.activation(acs[:, :, :], sp_b[:, :, :], ACT.Ln, bias=one[:, 0:1]))
            nc.scalar.activation(z[:, :, :], z[:, :, :], ACT.Silu)
            for n, c in enumerate(order):
                act.wait_ge(S["tr"], n + 1)
                if n >= 2:
                    act.wait_ge(S["st"], n - 1)
                nc.scalar.copy(xs[:, c, :], psY[:, 0:SSD_W])
                nc.scalar.copy(btok[:, n % 2, :], psG[:, 0:2 * P]).then_inc(S["ev"], 1)
                if n == 0:
                    act.wait_ge(S["acs_ready"], 1)
                    nc.scalar.activation(eacs[:, :, :], acs[:, :, :], ACT.Exp)
                    nc.scalar.activation(wdec[:, :, :], wdec[:, :, :], ACT.Exp)
                    nc.scalar.activation(dec[:, :, :], dec[:, :, :], ACT.Exp).then_inc(S["exps"], 1)
                if n >= 1:
                    act.wait_ge(S["st"], n)
                    nc.scalar.copy(st[:, order[n - 1], :, :], psI[:, :, 0:SSD_W]).then_inc(S["st_ev"], 1)
            act.wait_ge(S["st"], NC)
            nc.scalar.copy(st[:, order[NC - 1], :, :], psI[:, :, 0:SSD_W]).then_inc(S["st_ev"], 1)
            for c in range(NT):
                act.wait_ge(S["A"], c + 1)
                if c == 1:
                    act.wait_ge(S["scan"], 1)
                if c >= 2:
                    act.wait_ge(S["intra"], c - 1)
                for d in range(2):
                    for h in range(SSD_H):
                        last = nc.scalar.activation(decay[c % 2][:, d, h, :], psA[d][:, h // 3, (h % 3) * P:(h % 3 + 1) * P], ACT.Exp,
                                                    bias=nacs[:, c, d * SSD_H + h:d * SSD_H + h + 1])
                    last.then_inc(S["E"], 1)
                if c >= 1:
                    group_squares(act, c - 1)
            group_squares(act, NT - 1)
            act.wait_ge(S["ssq"], NT)
            nc.scalar.activation(ssq[:, :, :], ssq[:, :, :], ACT.Sqrt, bias=eps[:, 0:1], scale=1.0 / GW).then_inc(S["std"], 1)
            for n in range(6):
                act.wait_ge(S["ytr"], n + 1)
                j, half = n // 2, n % 2
                nc.scalar.activation(mixT[:, j, half * 512:(half + 1) * 512], (psY if half == 0 else psG)[:, :], ACT.Copy,
                                     scale=ncol[:, j:j + 1]).then_inc(S["mixed"], 1)

        @block.vector
        def _(dve):
            link = linked(dve, S["vec"])
            dve.wait_ge(S["small_in"], 64)
            b = bass.AP(brow[:, :].tensor, brow[:, :].offset, [brow[:, :].ap[0], [0, NC], [1, H2]])
            link(nc.vector.tensor_tensor(sp_a[:, :, :], dt[:, :, :], b, ALU.add))
            link(nc.vector.scalar_tensor_tensor(sp_b[:, :, :], sp_a[:, :, :], -1.0, sp_a[:, :, :], ALU.mult, ALU.max))
            dve.wait_ge(S["actv"], 3)
            link(nc.vector.tensor_scalar(nacs[:, :, :], sp_b[:, :, :], 1.0, None, ALU.add))
            link(nc.vector.tensor_scalar(eacs[:, :, :], nacs[:, :, :], -1.0, None, ALU.add))
            link(nc.vector.tensor_tensor(sp_b[:, :, :], sp_b[:, :, :], eacs[:, :, :], ALU.subtract))
            link(nc.vector.reciprocal(nacs[:, :, :], nacs[:, :, :]))
            link(nc.vector.tensor_tensor(sp_b[:, :, :], sp_b[:, :, :], nacs[:, :, :], ALU.mult))
            link(nc.vector.tensor_tensor(sp_b[:, :, :], sp_b[:, :, :], acs[:, :, :], ALU.add))
            link(nc.vector.scalar_tensor_tensor(dt[:, :, :], sp_a[:, :, :], 0.0, sp_b[:, :, :], ALU.max, ALU.add))
            a = bass.AP(arow[:, :].tensor, arow[:, :].offset, [arow[:, :].ap[0], [0, NC], [1, H2]])
            nc.vector.scalar_tensor_tensor(dta[:, :, :], dt[:, :, :], -1.0, a, ALU.mult, ALU.mult).then_inc(S["dta_ready"], 1)
            dve.wait_ge(S["cum"], 1)
            for d in range(2):
                hs = slice(d * SSD_H, (d + 1) * SSD_H)
                link(nc.vector.tensor_copy(acs[:, :, hs], psA[0][:, d, 0:NC * SSD_H].rearrange("p (c h) -> p c h", h=SSD_H)))
            link(nc.vector.tensor_copy(dec[:, :, :].rearrange("p c h -> p (c h)"), psA[1][:, 0, 0:NC * H2]))
            link(nc.vector.tensor_scalar(nacs[:, :, :], acs[:, :, :], -1.0, None, ALU.mult))
            nc.vector.tensor_tensor(wdec[:, :, :], dec[:, :, :], nacs[:, :, :], ALU.add).then_inc(S["acs_ready"], 1)
            dve.wait_ge(S["exps"], 1)
            link(nc.vector.tensor_tensor(wdec[:, :, :], wdec[:, :, :], dt[:, :, :], ALU.mult))
            link(nc.vector.memset(run[:, :, :], 0.0))

            def scan(n, d):
                c = order[n] if d == 0 else NC - 1 - n
                if d == 0:
                    dve.wait_ge(S["st_ev"], n + 1)
                if n >= NTC:
                    nc.vector.tensor_copy(start[:, c, :, d, :], run[:, d, :].rearrange("p (g w) -> p g w", g=NGRP))
                if n < NC - 1:
                    link(nc.vector.tensor_tensor(by_head(run[:, d, :]), by_head(run[:, d, :]),
                                                 head_cols(dec[:, c, d * SSD_H:(d + 1) * SSD_H]), ALU.mult))
                    link(nc.vector.tensor_tensor(run[:, d, :], run[:, d, :], st[:, c, d, :], ALU.add))

            for n, c in enumerate(order):
                dve.wait_ge(S["ev"], n + 1)
                if n >= 2:
                    dve.wait_ge(S["st"], n - 1)
                for d in range(2):
                    last = nc.vector.tensor_tensor(by_head(xdec[:, n % 2, d, :]), by_head(xs[:, c, :]),
                                                   head_cols(wdec[:, c, d * SSD_H:(d + 1) * SSD_H]), ALU.mult)
                last.then_inc(S["xdec"], 1)
                if n >= 2:
                    scan(n - 2, 0)
            for n in (NC - 2, NC - 1):
                scan(n, 0)
            for n in range(NC):
                scan(n, 1)
            link(nc.vector.memset(t1[:, :], 0.0))
            dve.sem_inc(S["scan"], 1)
            for c in range(NT):
                if c >= 2:
                    dve.wait_ge(S["intra"], c - 1)
                for d in range(2):
                    nc.vector.tensor_tensor(by_head(xdt[c % 2][:, d, :]), by_head(xs[:, c, :]),
                                            head_cols(dt[:, c, d * SSD_H:(d + 1) * SSD_H]), ALU.mult)
                dve.wait_ge(S["G"], c + 1)
                for d in range(2):
                    dve.wait_ge(S["E"], 2 * c + d + 1)
                    for g in range(NGRP):
                        part = decay[c % 2][:, d, 3 * g:3 * g + 3, :]
                        nc.vector.tensor_tensor(part, part, g_bcast(g),
                                                ALU.mult).then_inc(S["W"], 1)
                dve.wait_ge(S["inter"], c + 1)
                for d, t in ((0, t1[:, :]), (1, t2)):
                    src = psI[:, :, d * GW:(d + 1) * GW].rearrange("p g (h e) -> p g h e", e=HD)
                    e = eacs[:, c, d * SSD_H:(d + 1) * SSD_H]
                    e = bass.AP(e.tensor, e.offset, [e.ap[0], [3, NGRP], [1, 3], [0, HD]])
                    link(nc.vector.tensor_tensor(t.rearrange("p (g h e) -> p g h e", g=NGRP, e=HD), src, e, ALU.mult))
                dve.sem_inc(S["i_used"], 1)
                link(nc.vector.tensor_tensor(t1[:, :], t1[:, :], t2, ALU.add))
                link(nc.vector.tensor_tensor(by_head(t2), by_head(xs[:, c, :]), head_cols(drow[:, :]), ALU.mult))
                link(nc.vector.tensor_tensor(t1[:, :], t1[:, :], t2, ALU.add))
                dve.wait_ge(S["intra"], c + 1)
                link(nc.vector.tensor_tensor(t1[:, :], t1[:, :], psY[:, 0:SSD_W], ALU.add))
                dve.sem_inc(S["y_used"], 1)
                link(nc.vector.tensor_tensor(y[:, c, :], t1[:, :], z[:, c, :], ALU.mult))
                dve.sem_inc(S["gated"], 1)
            dve.wait_ge(S["std"], 1)
            link(nc.vector.reciprocal(ssq[:, :, :], ssq[:, :, :]))
            for c in range(NT):
                for g in range(NGRP):
                    last = nc.vector.tensor_scalar(y[:, c, g * GW:(g + 1) * GW], y[:, c, g * GW:(g + 1) * GW], ssq[:, c, g:g + 1], None,
                                                   ALU.mult)
            last.then_inc(S["scaled"], 1)


HY_EMB, HY_HID = 33, 64
HF = T // 2
NF = HF // P
TWO_PI_HI = 6.28125
TWO_PI_LO = 2 * np.pi - 6.28125
PI_BELOW = float(np.nextafter(np.float32(np.pi), np.float32(0)))
ROUND = 1.5 * 2.0 ** 23


def phase_hyena(nc, kit, keep, io):
    scope = ExitStack()
    with scope:
        hyT, mixT = keep["hyT"], keep["mixT"]
        cos = kit.sb(scope, "dft_cos", [P, NT, HF])
        sin = kit.sb(scope, "dft_sin", [P, NT, HF])
        cos_odd_t = kit.sb(scope, "dft_cos_odd_t", [P, NF, HF])
        sin_odd_t = kit.sb(scope, "dft_sin_odd_t", [P, NF, HF])
        X = kit.sb(scope, "hy_x", [P, NT, 3, HY_W])
        Z = kit.sb(scope, "hy_z", [P, NT, 2, HY_W])
        ZP = Z[:, :, :, :].rearrange("p (f par) j c -> p f par j c", par=2)
        decay = kit.sb(scope, "hy_decay", [P, NT, HY_W])
        w1 = kit.sb(scope, "hy_w1", [HY_EMB, HY_HID])
        w2 = kit.sb(scope, "hy_w2", [HY_HID, HY_HID])
        w3 = kit.sb(scope, "hy_w3", [HY_HID, 2 * HY_W])
        zt = kit.sb(scope, "hy_pos", [HY_EMB, T])
        bf = kit.sb(scope, "hy_bias_freq", [HY_HID, 2, 2])
        hid = Z[0:HY_HID, 2:4, :, :].rearrange("p a b c -> p (a b c)")
        turns = Z[0:HY_HID, 0:2, :, :].rearrange("p a b c -> p (a b c)")
        drow = kit.sb(scope, "hy_d_row", [1, HY_W])
        alt_row = kit.sb(scope, "alt_row", [1, HF])
        alt_col = kit.sb(scope, "alt_col", [P, 1])
        wcol = kit.sb(scope, "inv_scale", [P, NF])
        ident = kit.sb(scope, "ident_d", [P, P])
        ones = kit.sb(scope, "ones_d", [P, P])
        absd = kit.sb(scope, "hy_abs", [P, 2, 2, HY_W])
        inv = kit.sb(scope, "hy_inv", [P, HY_W])
        F = kit.sb(scope, "hy_spectra", [P, 2, 2, 4, HY_W])
        tmp = kit.sb(scope, "hy_tmp", [P, 4, 2, HY_W])
        mid = kit.sb(scope, "hy_mid", [1, 4, HY_W])
        zmid = absd[0:1, :, :, :].rearrange("p a b c -> p (a b) c")
        ps = [kit.ps(scope, f"hyps{i}", [P, 512]) for i in range(8)]
        S = {n: kit.sem("h_" + n) for n in ("small_in", "ident", "ones", "vec", "u_ready", "utr", "u_tok", "h1", "h2",
                                            "red", "sined", "h3", "h3_read", "abs", "abs_used", "x_ready", "mid", "mid_out", "zmid", "tables_in", "fwd",
                                            "spec", "z", "inv", "wrote")}
        block = scope.enter_context(nc.Block())
        small = ((w1, "hy_f_w1"), (w2, "hy_f_w2"), (w3, "hy_f_w3"), (zt, "hy_pos"), (bf, "hy_bias_freq"), (decay, "hy_decay"), (drow, "hy_d"),
                 (alt_row, "alt_row"), (alt_col, "alt_col"), (wcol, "inv_scale"))

        @block.sync
        def _(sp):
            for dst, src in small:
                sp.dma_start(dst[:], io[src]).then_inc(S["small_in"], 16)
            for dst, src in ((cos, "dft_cos"), (sin, "dft_sin"), (cos_odd_t, "dft_cos_odd_t"), (sin_odd_t, "dft_sin_odd_t")):
                sp.dma_start(dst[:, :, :], io[src].rearrange("(k p) n -> p k n", p=P)).then_inc(S["tables_in"], 16)

        @block.gpsimd
        def _(pool):
            identity(nc, pool, ident, S["ident"])
            nc.gpsimd.memset(ones[:, :], 1.0).then_inc(S["ones"], 1)

        @block.tensor
        def _(pe):
            pe.wait_ge(S["ident"], 2)
            for n in range(4):
                c, half = n // 2, n % 2
                pe.wait_ge(S["u_ready"], c + 1)
                for b in range(4):
                    last = nc.tensor.transpose(ps[4 + n][:, b * P:(b + 1) * P], hyT[:, 4 + c, 2 * b * P + half:2 * (b + 1) * P:2], ident[:, :])
                last.then_inc(S["utr"], 1)
            pe.wait_ge(S["small_in"], 16 * len(small))
            for i in range(2):
                last = nc.tensor.matmul(ps[i][0:HY_HID, :], w1[:, :], zt[:, i * 512:(i + 1) * 512], start=True, stop=True)
            last.then_inc(S["h1"], 1)
            pe.wait_ge(S["sined"], 1)
            for i in range(2):
                last = nc.tensor.matmul(ps[2 + i][0:HY_HID, :], w2[:, :], hid[:, i * 512:(i + 1) * 512], start=True, stop=True)
            last.then_inc(S["h2"], 1)
            pe.wait_ge(S["sined"], 2)
            pe.wait_ge(S["ones"], 1)
            for k in range(NT + 1):
                if k < NT:
                    if k >= 2:
                        pe.wait_ge(S["h3_read"], k - 1)
                    nc.tensor.matmul(ps[k % 2][:, :], hid[:, k * P:(k + 1) * P], w3[:, :], start=True, stop=True).then_inc(S["h3"], 1)
                if k >= 1:
                    pe.wait_ge(S["abs"], k)
                    nc.tensor.matmul(ps[2][:, :], ones[:, :], absd[:, (k - 1) % 2, :, :].rearrange("p a b -> p (a b)"), start=(k == 1),
                                     stop=(k == NT)).then_inc(S["abs_used"], 1)
            pe.wait_ge(S["x_ready"], 1)
            pe.wait_ge(S["u_tok"], 4)
            for b, (k0, lo) in enumerate(((0, 0), (NF, 1))):
                for k in range(NF):
                    last = nc.tensor.matmul(ps[2 + b][0:1, :], alt_col[:, :], X[:, k0 + k, lo:lo + 2, :].rearrange("p a b -> p (a b)"),
                                            start=(k == 0), stop=(k == NF - 1))
            last.then_inc(S["mid"], 1)
            pe.wait_ge(S["tables_in"], 64)
            for f in range(NF):
                bank = 4 * ((f + 1) % 2)
                if f == 1:
                    pe.wait_ge(S["mid_out"], 1)
                if f >= 2:
                    pe.wait_ge(S["spec"], f - 1)
                for par in range(2):
                    for j, (tab, lo) in enumerate(((cos, 0), (sin, 1))):
                        for k in range(NF):
                            last = nc.tensor.matmul(ps[bank + 2 * par + j][:, :], tab[:, NF * par + k, f * P:(f + 1) * P],
                                                    X[:, NF * par + k, lo:lo + 2, :].rearrange("p a b -> p (a b)"),
                                                    start=(k == 0), stop=(k == NF - 1))
                last.then_inc(S["fwd"], 1)
            pe.wait_ge(S["spec"], NF - 1)
            pe.wait_ge(S["zmid"], 1)
            outs = [(c, par) for c in range(2) for par in range(2)]
            for q, (c, par) in enumerate(outs):
                nc.tensor.matmul(ps[4 + q][:, :], zmid[:, par, c * P:(c + 1) * P], alt_row[:, :], start=True, stop=False)
            for f in range(NF):
                pe.wait_ge(S["z"], f + 1)
                for q, (c, par) in enumerate(outs):
                    tabs = (cos, sin) if par == 0 else (cos_odd_t, sin_odd_t)
                    for j in range(2):
                        last = nc.tensor.matmul(ps[4 + q][:, :], ZP[:, f, par, j, c * P:(c + 1) * P], tabs[j][:, f, :], start=False,
                                                stop=(f == NF - 1 and j == 1))
                    if f == NF - 1:
                        last.then_inc(S["inv"], 1)

        @block.scalar
        def _(act):
            for n in range(4):
                c, half = n // 2, n % 2
                act.wait_ge(S["utr"], n + 1)
                nc.scalar.copy(X[:, 4 * half:4 * half + 4, 1, c * P:(c + 1) * P],
                               ps[4 + n][:, :].rearrange("p (b c) -> p b c", b=4)).then_inc(S["u_tok"], 1)
            for i in range(2):
                act.wait_ge(S["red"], i + 1)
                nc.scalar.activation(hid[:, :], turns[:, :], ACT.Sin).then_inc(S["sined"], 1)
            for k in range(NT):
                act.wait_ge(S["h3_read"], k + 1)
                if k >= 2:
                    act.wait_ge(S["abs_used"], k - 1)
                nc.scalar.activation(absd[:, k % 2, :, :], X[:, k, 0:3:2, :], ACT.Abs).then_inc(S["abs"], 1)
            act.wait_ge(S["mid"], 1)
            nc.scalar.copy(mid[:, 0:2, :].rearrange("p a b -> p (a b)"), ps[2][0:1, :])
            nc.scalar.copy(mid[:, 2:4, :].rearrange("p a b -> p (a b)"), ps[3][0:1, :]).then_inc(S["mid_out"], 1)
            for f in range(NF):
                act.wait_ge(S["fwd"], f + 1)
                if f >= 2:
                    act.wait_ge(S["z"], f - 1)
                for par in range(2):
                    C, N = (ps[4 * ((f + 1) % 2) + 2 * par + j] for j in range(2))
                    to, w = F[:, f % 2, par, :, :], wcol[:, f:f + 1]
                    nc.scalar.copy(to[:, 0, :], C[:, 0:HY_W])
                    nc.scalar.activation(to[:, 1, :], C[:, HY_W:], ACT.Copy, scale=w)
                    nc.scalar.activation(to[:, 2, :], N[:, 0:HY_W], ACT.Copy, scale=w)
                    last = nc.scalar.copy(to[:, 3, :], N[:, HY_W:])
                last.then_inc(S["spec"], 1)

        @block.vector
        def _(dve):
            link = linked(dve, S["vec"])
            for c in range(2):
                nc.vector.tensor_tensor(hyT[:, 4 + c, :], hyT[:, 4 + c, :], hyT[:, 2 + c, :], ALU.mult).then_inc(S["u_ready"], 1)
            dve.wait_ge(S["small_in"], 16 * len(small))
            for i, done in enumerate(("h1", "h2")):
                dve.wait_ge(S[done], 1)
                for j in range(2):
                    o = slice(j * 512, (j + 1) * 512)
                    link(nc.vector.tensor_scalar(turns[:, o], ps[2 * i + j][0:HY_HID, :], bf[:, i, 0:1], bf[:, i, 1:2], ALU.add, ALU.mult))
                link(nc.vector.tensor_scalar(hid[:, :], turns[:, :], 1 / (2 * np.pi), ROUND, ALU.mult, ALU.add))
                link(nc.vector.tensor_scalar(hid[:, :], hid[:, :], -ROUND, None, ALU.add))
                link(nc.vector.scalar_tensor_tensor(turns[:, :], hid[:, :], -TWO_PI_HI, turns[:, :], ALU.mult, ALU.add))
                link(nc.vector.scalar_tensor_tensor(turns[:, :], hid[:, :], -TWO_PI_LO, turns[:, :], ALU.mult, ALU.add))
                link(nc.vector.tensor_scalar(turns[:, :], turns[:, :], PI_BELOW, -PI_BELOW, ALU.min, ALU.max))
                dve.sem_inc(S["red"], 1)
            for k in range(NT):
                dve.wait_ge(S["h3"], k + 1)
                nc.vector.tensor_tensor(X[:, k, 0, :], ps[k % 2][:, 0:HY_W], decay[:, k, :], ALU.mult)
                nc.vector.tensor_tensor(X[:, k, 2, :], ps[k % 2][:, HY_W:], decay[:, k, :], ALU.mult).then_inc(S["h3_read"], 1)
            dve.wait_ge(S["abs_used"], NT)
            link(nc.vector.tensor_copy(inv[:, :], ps[2][:, 0:HY_W]))
            link(nc.vector.tensor_tensor(inv[:, :], inv[:, :], ps[2][:, HY_W:], ALU.add))
            link(nc.vector.reciprocal(inv[:, :], inv[:, :]))
            ib = bass.AP(inv[:, :].tensor, inv[:, :].offset, [inv[:, :].ap[0], [0, NT], [1, HY_W]])
            link(nc.vector.tensor_tensor(X[:, :, 0, :], X[:, :, 0, :], ib, ALU.mult))
            link(nc.vector.tensor_tensor(X[:, :, 2, :], X[:, :, 2, :], ib, ALU.mult))
            link(nc.vector.memset(X[0:1, 0, 2, :], 0.0))
            link(nc.vector.tensor_tensor(X[0:1, 0, 0, :], X[0:1, 0, 0, :], drow[:, :], ALU.add))
            link(nc.vector.tensor_tensor(X[:, :, 0, :], X[:, :, 0, :], X[:, :, 2, :], ALU.add))
            link(nc.vector.scalar_tensor_tensor(X[:, :, 2, :], X[:, :, 2, :], -2.0, X[:, :, 0, :], ALU.mult, ALU.add))
            dve.sem_inc(S["x_ready"], 1)
            dve.wait_ge(S["mid_out"], 1)
            kr, ur, us, ks = (mid[:, j, :] for j in range(4))
            for j, (a, b) in enumerate(((ur, kr), (ur, ks), (us, ks), (us, kr))):
                last = nc.vector.scalar_tensor_tensor(zmid[:, j, :], a, 1.0 / T, b, ALU.mult, ALU.mult)
            link(last)
            nc.vector.tensor_tensor(zmid[:, 0, :], zmid[:, 0, :], zmid[:, 2, :], ALU.subtract)
            nc.vector.tensor_tensor(zmid[:, 1, :], zmid[:, 1, :], zmid[:, 3, :], ALU.add).then_inc(S["zmid"], 1)
            for f in range(NF):
                dve.wait_ge(S["spec"], f + 1)
                for par in range(2):
                    for e in range(2):
                        o = e ^ par
                        K, U, A, B = (F[:, f % 2, e if j in (1, 2) else o, j, :] for j in range(4))
                        for j, (a, b) in enumerate(((U, K), (U, B), (A, B), (A, K))):
                            last = nc.vector.tensor_tensor(tmp[:, j, e, :], a, b, ALU.mult)
                    link(last)
                    nc.vector.tensor_tensor(tmp[:, 0, :, :], tmp[:, 0, :, :], tmp[:, 2, :, :], ALU.subtract)
                    link(nc.vector.tensor_tensor(tmp[:, 1, :, :], tmp[:, 1, :, :], tmp[:, 3, :, :], ALU.add))
                    link(nc.vector.tensor_tensor(ZP[:, f, par, :, :], tmp[:, 0:2, 0, :], tmp[:, 0:2, 1, :], ALU.add))
                dve.sem_inc(S["z"], 1)
            for q in range(4):
                c, par = q // 2, q % 2
                dve.wait_ge(S["inv"], q + 1)
                last = nc.vector.tensor_tensor(mixT[:, 6 + c, par:T:2], ps[4 + q][:, :], hyT[:, c, par:T:2], ALU.mult)
            last.then_inc(S["wrote"], 1)
            dve.wait_ge(S["wrote"], 1)


def hyena_constants():
    f32 = np.float32
    t = np.linspace(0.0, 1.0, T, dtype=f32)[:, None]
    w = (f32(2.0 * np.pi) * np.arange(T, dtype=f32)[:, None] / f32(T)).astype(f32)
    bands = (HY_EMB - 1) // 2
    f = np.linspace(1e-4, bands - 1, bands, dtype=f32)[None, :]
    pos = np.concatenate([t, np.cos(f * w), -np.sin(f * w)], axis=1).astype(f32)
    deltas = np.abs(np.linspace(np.log(1e-2) / 1.5, np.log(1e-2) / 0.3, HY_W, dtype=f32))
    decay = np.exp(-t * deltas).astype(f32)
    order = np.concatenate([np.arange(0, T, 2), np.arange(1, T, 2)])
    angle = np.outer(order, np.arange(HF)) % (2 * T) * (np.pi / T)
    cos, sin = np.cos(angle).astype(f32), np.sin(angle).astype(f32)
    alt = (1.0 - 2.0 * (np.arange(HF) % 2)).astype(f32)
    scale = np.full(HF, 2.0 / T)
    scale[0] = 1.0 / T
    return {
        "hy_pos": np.ascontiguousarray(pos[order].T),
        "hy_decay": np.ascontiguousarray(decay[order].reshape(NT, P, HY_W).transpose(1, 0, 2)),
        "dft_cos": cos,
        "dft_sin": sin,
        "dft_cos_odd_t": np.ascontiguousarray(cos[HF:].T),
        "dft_sin_odd_t": np.ascontiguousarray(sin[HF:].T),
        "alt_row": alt[None, :],
        "alt_col": np.ascontiguousarray(alt[:P, None]),
        "inv_scale": np.ascontiguousarray(scale.astype(f32).reshape(NF, P).T),
    }


HALF = P // 2
NUNIT = (T * TOPK + NE * (HALF - 1)) // HALF
NBLK = (T * TOPK + NE * (P - 1)) // P
NROW = NUNIT * HALF
ROW_LIST = NE * T


def row_of(ap, n, at=0):
    return bass.AP(ap.tensor, ap.offset + at, [[0, P], [1, n]])


QUARTERS = tuple((half, what) for half in range(2) for what in range(2))


def gate_up_quarter(io, e, q):
    half, what = QUARTERS[q]
    at = what * DE + half * 512
    return io["w_gate_up"][bass.ds(e, 1), :, at:at + 512].rearrange("a (k p) n -> p (a k) n", p=P)


def first_weights(kit, scope):
    return {"gate_up": kit.sb(scope, "w_gate_up0", [P, 4, KD, 512], side="right"),
            "in": [kit.sem(f"f_gate_up_in0{q}") for q in range(4)]}


def load_first_weights(sp, weights, io):
    for q in range(4):
        sp.dma_start(weights["gate_up"][:, q, :, :], gate_up_quarter(io, 0, q)).then_inc(weights["in"][q], 16)


def phase_mix(nc, kit, keep, io, dram, weights):
    scope = ExitStack()
    with scope:
        mixT, modT, dest, gate, table = keep["mixT"], keep["modT"], keep["dest"], keep["gate"], keep["table"]
        wout = kit.sb(scope, "w_out", [P, KD, D])
        wr = kit.sb(scope, "w_router", [P, KD, NE])
        brt = kit.sb(scope, "b_router_row", [P, NE])
        gains = kit.sb(scope, "gains_col", [P, 3, KD])
        vcol = kit.sb(scope, "vectors_col", [P, 4, KD])
        vrow = kit.sb(scope, "vectors_rows", [4 * KD, P])
        rows = kit.sb(scope, "vectors_row", [P, 3, D])
        xin = kit.sb(scope, "x_tile", [P, 2, D])
        x1 = kit.sb(scope, "x1_tile", [P, 2, D])
        h2 = kit.sb(scope, "h2_tile", [P, 2, D])
        sq = kit.sb(scope, "mix_squares", [P, 2, D])
        h2T = kit.sb(scope, "h2_t", [P, KD, P])
        st = kit.sb(scope, "mix_stat", [P, NT, 4])
        eps = kit.sb(scope, "eps_e", [P, 1])
        ident = kit.sb(scope, "ident_e", [P, P])
        ones = kit.sb(scope, "ones_e", [P, P])
        before = kit.sb(scope, "tri_strict", [P, P])
        lanes = kit.sb(scope, "expert_number", [P, NE])
        logit = kit.sb(scope, "logits", [P, NE])
        top = kit.sb(scope, "top_logits", [P, NT, 8])
        topi = kit.sb(scope, "top_experts", [P, NT, 8], U32)
        topf = kit.sb(scope, "top_experts_f", [P, NT, TOPK])
        shifted = kit.sb(scope, "top_shifted", [P, NT, TOPK])
        gsum = kit.sb(scope, "gate_sum", [P, NT])
        hot = kit.sb(scope, "one_hot", [P, NT, TOPK, NE])
        mask = kit.sb(scope, "chosen", [P, NT, NE])
        place = kit.sb(scope, "place", [P, NT, NE])
        chosen_place = kit.sb(scope, "chosen_place", [P, NT, TOPK])
        in_list = kit.sb(scope, "place_in_lists", [P, NT * TOPK], I32)
        picked = kit.sb(scope, "picked", [P, 2, TOPK, NE])
        count = kit.sb(scope, "count_so_far", [P, NT + 1, NE])
        amount = kit.sb(scope, "units_and_blocks", [P, 2, NE])
        cum = kit.sb(scope, "amount_before", [P, 2, 2, NE])
        destf = kit.sb(scope, "dest_f", [P, NT, TOPK])
        tokens = kit.sb(scope, "token_number", [P, NT], I32)
        zero = kit.sb(scope, "zero_rows", [P, ROW_LIST // P], I32)
        psO = [kit.ps(scope, f"psO{i}", [P, D]) for i in range(2)]
        psH = kit.ps(scope, "psH", [P, D])
        psL = kit.ps(scope, "psL", [P, 512])
        psR = kit.ps(scope, "psR", [P, 512])
        S = {n: kit.sem("e_" + n) for n in ("small_in", "pool", "vec", "vcol", "vturn", "vrow", "vrow_out", "rows_in", "x_in0", "x_in1",
                                            "proj", "std1", "x1", "std2", "h2", "x1_out0", "x1_out1", "h2_out0", "h2_out1", "h2turn", "h2T",
                                            "logits", "logits_read", "shifted", "exped", "mask", "ranks", "in_list", "dest", "zeroed", "scattered",
                                            "table")}
        w_in = [kit.sem(f"e_w_in{half}") for half in range(2)]
        block = scope.enter_context(nc.Block())

        @block.sync
        def _(sp):
            sp.dma_start(gains[:, :, :], io["gains_col"]).then_inc(S["small_in"], 16)
            sp.dma_start(brt[:, :], row_of(io["b_router"], NE)).then_inc(S["small_in"], 16)
            sp.dma_start(wr[:, :, :], io["w_router"].rearrange("(k p) n -> p k n", p=P)).then_inc(S["small_in"], 16)
            for half in range(2):
                c = slice(half * 512, (half + 1) * 512)
                sp.dma_start(wout[:, :, c], io["w_out"].rearrange("(k p) n -> p k n", p=P)[:, :, c]).then_inc(w_in[half], 16)
            sp.wait_ge(S["vrow"], 1)
            sp.dma_start(dram["vectors"].rearrange("(r p) -> r p", p=P), vrow[:, :]).then_inc(S["vrow_out"], 16)
            sp.wait_ge(S["vrow_out"], 16)
            for j in range(3):
                sp.dma_start(rows[:, j, :], row_of(dram["vectors"], D, j * D)).then_inc(S["rows_in"], 16)
            for t in range(2):
                sp.dma_start(xin[:, t, :], io["x"][t * P:(t + 1) * P, :]).then_inc(S[f"x_in{t}"], 16)
            load_first_weights(sp, weights, io)
            for t in range(NT):
                ts = slice(t * P, (t + 1) * P)
                sp.wait_ge(S["x1"], t + 1)
                sp.dma_start(dram["x1"][ts, :], x1[:, t % 2, :]).then_inc(S[f"x1_out{t % 2}"], 16)
                if t + 2 < NT:
                    sp.dma_start(xin[:, t % 2, :], io["x"][(t + 2) * P:(t + 3) * P, :]).then_inc(S[f"x_in{t % 2}"], 16)
                sp.wait_ge(S["h2"], t + 1)
                sp.dma_start(dram["h2"][ts, :], h2[:, t % 2, :]).then_inc(S[f"h2_out{t % 2}"], 16)
            for i in range(2):
                sp.wait_ge(S[f"x1_out{i}"], 16 * NT // 2)
                sp.wait_ge(S[f"h2_out{i}"], 16 * NT // 2)

        @block.gpsimd
        def _(pool):
            link = linked(pool, S["pool"])
            nc.gpsimd.memset(eps[:, :], EPS)
            nc.gpsimd.memset(ident[:, :], 0.0)
            nc.gpsimd.memset(ones[:, :], 1.0)
            nc.gpsimd.memset(zero[:, :], 0)
            nc.gpsimd.iota(lanes[:, :], pattern=[[1, NE]], base=0, channel_multiplier=0, allow_small_or_imprecise_dtypes=True)
            nc.gpsimd.iota(tokens[:, :], pattern=[[P, NT]], base=0, channel_multiplier=1)
            link(nc.gpsimd.memset(before[:, :], 1.0))
            nc.gpsimd.affine_select(out=ident[:, :], in_=ident[:, :], compare_op=ALU.not_equal, fill=1.0, base=0, pattern=[[-1, P]],
                                    channel_multiplier=1)
            link(nc.gpsimd.affine_select(out=before[:, :], in_=before[:, :], compare_op=ALU.is_gt, fill=0.0, base=0, pattern=[[1, P]],
                                         channel_multiplier=-1))
            pool.dma_start(dram["row_token"].rearrange("(p b) o -> p (b o)", p=P), zero[:, :]).then_inc(S["zeroed"], 16)
            pool.wait_ge(S["zeroed"], 16)
            for t in range(NT):
                pool.wait_ge(S["in_list"], t + 1)
                for k in range(TOPK):
                    at = in_list[:, t * TOPK + k:t * TOPK + k + 1]
                    pool.indirect_dma_start(out=dram["row_token"], out_offset=bass.IndirectOffsetOnAxis(ap=at, axis=0),
                                            in_=tokens[:, t:t + 1], in_offset=None).then_inc(S["scattered"], 16)
            pool.wait_ge(S["scattered"], 16 * NT * TOPK)

        @block.tensor
        def _(pe):
            pe.wait_ge(S["pool"], 2)
            pe.wait_ge(S["vcol"], 1)
            nc.tensor.transpose(psR[0:4 * KD, 0:P], vcol[:, :, :].rearrange("p a k -> p (a k)"), ident[:, :]).then_inc(S["vturn"], 1)
            def project(t):
                if t >= 2:
                    pe.wait_ge(S["x1"], t - 1)
                for n in range(2):
                    pe.wait_ge(w_in[n], 16)
                    for k in range(KD):
                        last = nc.tensor.matmul(psO[t % 2][:, n * 512:(n + 1) * 512], mixT[:, k, t * P:(t + 1) * P],
                                                wout[:, k, n * 512:(n + 1) * 512], start=(k == 0), stop=(k == KD - 1))
                last.then_inc(S["proj"], 1)

            def route(t):
                pe.wait_ge(S["h2"], t + 1)
                if t >= 1:
                    pe.wait_ge(S["h2T"], t)
                for k in range(KD):
                    last = nc.tensor.transpose(psH[:, k * P:(k + 1) * P], h2[:, t % 2, k * P:(k + 1) * P], ident[:, :])
                last.then_inc(S["h2turn"], 1)
                pe.wait_ge(S["h2T"], t + 1)
                pe.wait_ge(S["small_in"], 48)
                if t >= 1:
                    pe.wait_ge(S["logits_read"], t)
                for k in range(KD):
                    last = nc.tensor.matmul(psL[:, 0:NE], h2T[:, k, :], wr[:, k, :], start=(k == 0), stop=(k == KD - 1))
                last.then_inc(S["logits"], 1)

            def rank(t):
                pe.wait_ge(S["mask"], t + 1)
                nc.tensor.matmul(psR[:, 2 * t * NE:(2 * t + 1) * NE], before[:, :], mask[:, t, :], start=True, stop=True)
                nc.tensor.matmul(psR[:, (2 * t + 1) * NE:(2 * t + 2) * NE], ones[:, :], mask[:, t, :], start=True, stop=True
                                 ).then_inc(S["ranks"], 1)

            for t in range(NT + 2):
                if t < NT:
                    project(t)
                if t >= 2:
                    rank(t - 2)
                if 1 <= t <= NT:
                    route(t - 1)

        @block.scalar
        def _(act):
            act.wait_ge(S["pool"], 2)
            act.wait_ge(S["vturn"], 1)
            nc.scalar.copy(vrow[:, :], psR[0:4 * KD, 0:P]).then_inc(S["vrow"], 1)
            sqn = kit.sem("e_sq")
            n = 0
            for t in range(NT):
                for src, done, out, j in ((psO[t % 2][:, :], "proj", "std1", 0), (x1[:, t % 2, :], "x1", "std2", 1)):
                    act.wait_ge(S[done], t + 1)
                    nc.scalar.activation(sq[:, j, :], src, ACT.Square, accum_out=st[:, t, 2 * j:2 * j + 1]).then_inc(sqn, 1)
                    n += 1
                    act.wait_ge(sqn, n)
                    nc.scalar.activation(st[:, t, 2 * j + 1:2 * j + 2], st[:, t, 2 * j:2 * j + 1], ACT.Sqrt, bias=eps[:, 0:1],
                                         scale=1.0 / D).then_inc(S[out], 1)
                act.wait_ge(S["h2turn"], t + 1)
                if t >= 1:
                    act.wait_ge(S["logits"], t)
                nc.scalar.copy(h2T[:, :, :].rearrange("p k t -> p (k t)"), psH[:, :]).then_inc(S["h2T"], 1)
            act.wait_ge(S["shifted"], 1)
            nc.scalar.activation(shifted[:, :, :], shifted[:, :, :], ACT.Exp).then_inc(S["exped"], 1)

        @block.vector
        def _(dve):
            link = linked(dve, S["vec"])
            dve.wait_ge(S["small_in"], 48)
            nc.vector.tensor_tensor(vcol[:, 0, :], modT[:, 2 * KD:3 * KD, 0], gains[:, 0, :], ALU.mult)
            link(nc.vector.tensor_scalar(vcol[:, 1, :], modT[:, 4 * KD:5 * KD, 0], 1.0, None, ALU.add))
            nc.vector.tensor_tensor(vcol[:, 1, :], vcol[:, 1, :], gains[:, 1, :], ALU.mult)
            nc.vector.tensor_copy(vcol[:, 2, :], modT[:, 3 * KD:4 * KD, 0])
            nc.vector.tensor_tensor(vcol[:, 3, :], modT[:, 5 * KD:6 * KD, 0], gains[:, 2, :], ALU.mult).then_inc(S["vcol"], 1)
            link(nc.vector.memset(count[:, 0, :], 0.0))

            def place_tile(t):
                dve.wait_ge(S["ranks"], t + 1)
                link(nc.vector.tensor_tensor(place[:, t, :], psR[:, 2 * t * NE:(2 * t + 1) * NE], count[:, t, :], ALU.add))
                link(nc.vector.tensor_tensor(count[:, t + 1, :], psR[:, (2 * t + 1) * NE:(2 * t + 2) * NE], count[:, t, :], ALU.add))
                pl = place[:, t, :]
                link(nc.vector.tensor_tensor(picked[:, t % 2, :, :], hot[:, t, :, :],
                                             bass.AP(pl.tensor, pl.offset, [pl.ap[0], [0, TOPK], [1, NE]]), ALU.mult))
                link(nc.vector.tensor_reduce(chosen_place[:, t, :], picked[:, t % 2, :, :], AXX, ALU.add))
                nc.vector.scalar_tensor_tensor(in_list[:, t * TOPK:(t + 1) * TOPK], topf[:, t, :], float(T), chosen_place[:, t, :],
                                               ALU.mult, ALU.add).then_inc(S["in_list"], 1)

            dve.wait_ge(S["rows_in"], 48)
            for t in range(NT):
                s = t % 2
                dve.wait_ge(S["std1"], t + 1)
                link(nc.vector.reciprocal(st[:, t, 1:2], st[:, t, 1:2]))
                if t >= 2:
                    dve.wait_ge(S[f"x1_out{s}"], 16 * (t // 2))
                link(nc.vector.scalar_tensor_tensor(x1[:, s, :], psO[s][:, :], st[:, t, 1:2], rows[:, 0, :], ALU.mult, ALU.mult))
                dve.wait_ge(S[f"x_in{s}"], 16 * (t // 2 + 1))
                nc.vector.tensor_tensor(x1[:, s, :], x1[:, s, :], xin[:, s, :], ALU.add).then_inc(S["x1"], 1)
                dve.wait_ge(S["std2"], t + 1)
                link(nc.vector.reciprocal(st[:, t, 3:4], st[:, t, 3:4]))
                if t >= 2:
                    dve.wait_ge(S[f"h2_out{s}"], 16 * (t // 2))
                link(nc.vector.scalar_tensor_tensor(h2[:, s, :], x1[:, s, :], st[:, t, 3:4], rows[:, 1, :], ALU.mult, ALU.mult))
                nc.vector.tensor_tensor(h2[:, s, :], h2[:, s, :], rows[:, 2, :], ALU.add).then_inc(S["h2"], 1)
                dve.wait_ge(S["logits"], t + 1)
                link(nc.vector.tensor_tensor(logit[:, :], psL[:, 0:NE], brt[:, :], ALU.add))
                dve.sem_inc(S["logits_read"], 1)
                link(nc.vector.max(top[:, t, :], logit[:, :]))
                link(nc.vector.max_index(topi[:, t, :], top[:, t, :], logit[:, :]))
                link(nc.vector.tensor_copy(topf[:, t, :], topi[:, t, 0:TOPK]))
                tf, ln = topf[:, t, :], lanes[:, :]
                link(nc.vector.tensor_tensor(hot[:, t, :, :], bass.AP(tf.tensor, tf.offset, [tf.ap[0], [1, TOPK], [0, NE]]),
                                             bass.AP(ln.tensor, ln.offset, [ln.ap[0], [0, TOPK], [1, NE]]), ALU.is_equal))
                if t >= 1:
                    place_tile(t - 1)
                nc.vector.tensor_reduce(mask[:, t, :], hot[:, t, :, :].rearrange("p k e -> p e k"), AXX, ALU.add).then_inc(S["mask"], 1)
            place_tile(NT - 1)
            first = top[:, :, 0:1]
            nc.vector.tensor_tensor(shifted[:, :, :], top[:, :, 0:TOPK], bass.AP(first.tensor, first.offset, [first.ap[0], [8, NT], [0, TOPK]]),
                                    ALU.subtract).then_inc(S["shifted"], 1)
            dve.wait_ge(S["exped"], 1)
            link(nc.vector.tensor_reduce(gsum[:, :], shifted[:, :, :], AXX, ALU.add))
            link(nc.vector.reciprocal(gsum[:, :], gsum[:, :]))
            gs = gsum[:, :]
            link(nc.vector.tensor_tensor(gate[:, :].rearrange("p (t k) -> p t k", k=TOPK), shifted[:, :, :],
                                         bass.AP(gs.tensor, gs.offset, [gs.ap[0], [1, NT], [0, TOPK]]), ALU.mult))
            link(nc.vector.tensor_scalar(amount[:, 0, :], count[:, NT, :], 1.0 / HALF, (HALF - 1) / (2.0 * HALF), ALU.mult, ALU.add))
            link(nc.vector.tensor_scalar(amount[:, 0, :], amount[:, 0, :], ROUND, -ROUND, ALU.add, ALU.add))
            link(nc.vector.tensor_scalar(amount[:, 1, :], amount[:, 0, :], 0.5, 0.25, ALU.mult, ALU.add))
            link(nc.vector.tensor_scalar(amount[:, 1, :], amount[:, 1, :], ROUND, -ROUND, ALU.add, ALU.add))
            link(nc.vector.memset(cum[:, :, :, :], 0.0))
            link(nc.vector.tensor_copy(cum[:, 0, :, 1:NE], amount[:, :, 0:NE - 1]))
            cur, step = 0, 1
            while step < NE:
                nc.vector.tensor_copy(cum[:, 1 - cur, :, 0:step], cum[:, cur, :, 0:step])
                link(nc.vector.tensor_tensor(cum[:, 1 - cur, :, step:NE], cum[:, cur, :, step:NE], cum[:, cur, :, 0:NE - step], ALU.add))
                cur, step = 1 - cur, 2 * step
            nc.vector.tensor_copy(table[:, 0:2, :], amount[0:1, :, :])
            nc.vector.tensor_copy(table[:, 2:4, :], cum[0:1, cur, :, :]).then_inc(S["table"], 1)
            c0 = cum[:, cur, 0, :]
            link(nc.vector.tensor_tensor(hot[:, :, :, :].rearrange("p t k e -> p (t k) e"), hot[:, :, :, :].rearrange("p t k e -> p (t k) e"),
                                         bass.AP(c0.tensor, c0.offset, [c0.ap[0], [0, NT * TOPK], [1, NE]]), ALU.mult))
            link(nc.vector.tensor_reduce(destf[:, :, :], hot[:, :, :, :], AXX, ALU.add))
            link(nc.vector.scalar_tensor_tensor(destf[:, :, :], destf[:, :, :], float(HALF), chosen_place[:, :, :], ALU.mult, ALU.add))
            nc.vector.tensor_copy(dest[:, :], destf[:, :, :].rearrange("p t k -> p (t k)")).then_inc(S["dest"], 1)


BPE = T // P
SLOTS = 2


def phase_experts(nc, kit, keep, weights, io, dram):
    scope = ExitStack()
    with scope:
        table = keep["table"]
        gu = [weights["gate_up"], kit.sb(scope, "w_gate_up1", [P, 4, KD, 512])]
        gu_in = [weights["in"], [kit.sem(f"f_gate_up_in1{q}") for q in range(4)]]
        down = kit.sb(scope, "w_down", [P, 2, 4, D])
        bias = [kit.sb(scope, f"gate_up_bias{i}", [P, 2 * DE]) for i in range(SLOTS)]
        down_bias = kit.sb(scope, "down_bias", [P, D])
        xg = kit.sb(scope, "x_rows", [P, D])
        xT = kit.sb(scope, "x_rows_t", [P, KD, P])
        gated = kit.sb(scope, "gated", [P, 2, 512])
        sig = kit.sb(scope, "sig", [P, 2, 512])
        up = kit.sb(scope, "up", [P, 512])
        actT = kit.sb(scope, "act_t", [P, DE // P, P])
        yrow = kit.sb(scope, "y_rows", [P, D])
        blank = kit.sb(scope, "zeros", [HALF, P])
        listed = kit.sb(scope, "listed_tokens", [P, 1], I32)
        idx = kit.sb(scope, "row_index", [P, 1], I32)
        ident = kit.sb(scope, "ident_f", [P, P])
        psT = kit.ps(scope, "psT", [P, 2, 512])
        psG = kit.ps(scope, "ps_gate_up", [P, 4, 512])
        psD = kit.ps(scope, "ps_down", [P, 2, 512])
        S = {n: kit.sem("f_" + n) for n in ("ident", "down_in0", "down_in1", "down_bias_in", "bias_in0", "bias_in1", "index", "rows_in", "x_turned",
                                            "xT", "gate_up", "vec", "gate_ready", "sig", "act", "act_turned", "actT", "down", "y", "y_out",
                                            "blank", "blank_out", "stored", "list_in", "lists", "gathers", "pieces_in")}
        block = scope.enter_context(nc.Block())

        def units_of(eng, e):
            n = eng.value_load(table[0:1, 0, bass.ds(e, 1)], min_val=0, max_val=2 * BPE)
            return n, eng.value_load(table[0:1, 2, bass.ds(e, 1)], min_val=0, max_val=NUNIT)

        def blocks_of(eng, e):
            n = eng.value_load(table[0:1, 1, bass.ds(e, 1)], min_val=0, max_val=BPE)
            return n, eng.value_load(table[0:1, 3, bass.ds(e, 1)], min_val=0, max_val=NBLK)

        def blocks_to(eng, e):
            n, first = blocks_of(eng, e)
            return eng.snap(n + first)

        def units_in_all(eng):
            n, first = units_of(eng, NE - 1)
            return nc.s_assert_within(eng.snap(n + first), 0, NUNIT)

        def each_block(eng, whole, half, rows=False):
            with eng.Fori(0, NE // 2) as i:
                for slot in range(SLOTS):
                    e = eng.snap(i * 2 + slot)
                    units = eng.value_load(table[0:1, 0, bass.ds(e, 1)], min_val=0, max_val=2 * BPE)
                    first = eng.value_load(table[0:1, 3, bass.ds(e, 1)], min_val=0, max_val=NBLK)
                    if rows:
                        first_unit = eng.value_load(table[0:1, 2, bass.ds(e, 1)], min_val=0, max_val=NUNIT)
                    with eng.Fori(0, BPE) as b:
                        with eng.If(b * 2 < units):
                            block = [eng.snap(first + b)]
                            if rows:
                                block.append(nc.s_assert_within(eng.snap(first_unit + b * 2), 0, NUNIT - 1))
                            with eng.If(b * 2 + 1 < units):
                                whole(i, slot, *block)
                            with eng.Else():
                                half(i, slot, *block)

        @block.sync
        def _(sp):
            def load_bias(e, slot):
                sp.dma_start(bias[slot][:, :], io["b_gate_up"][bass.ds(e, 1), :].broadcast_to([P, 2 * DE])).then_inc(S[f"bias_in{slot}"], 16)

            def load_down_bias(e):
                sp.dma_start(down_bias[:, :], io["b_down"][bass.ds(e, 1), :].broadcast_to([P, D])).then_inc(S["down_bias_in"], 16)

            def load_down(e, half):
                w = io["w_down"][bass.ds(e, 1), half * 512:(half + 1) * 512, :].rearrange("a (k p) n -> p (a k) n", p=P)
                sp.dma_start(down[:, half, :, :], w).then_inc(S[f"down_in{half}"], 16)

            def load_gate_up(e, slot, q):
                sp.dma_start(gu[slot][:, q, :, :], gate_up_quarter(io, e, q)).then_inc(gu_in[slot][q], 16)

            load_bias(0, 0)
            sp.wait_ge(S["rows_in"], 16)
            for half in range(2):
                load_down(0, half)
            load_down_bias(0)
            sp.wait_ge(S["rows_in"], 32)
            for q in range(4):
                load_gate_up(1, 1, q)
            load_bias(1, 1)
            with sp.Fori(0, NE // 2 - 1) as i:
                for slot in range(SLOTS):
                    e, later = sp.snap(i * 2 + slot + 1), sp.snap(i * 2 + slot + 2)
                    end = blocks_to(sp, sp.snap(i * 2 + slot))
                    for q in range(4):
                        sp.wait_ge(gu_in[slot][q], i * 16 + 16)
                        sp.sem_inc(S["pieces_in"], 1)
                        sp.wait_ge(S["gate_up"], end * 4 + q + 1)
                        load_gate_up(later, slot, q)
                    for half in range(2):
                        sp.wait_ge(S[f"down_in{half}"], e * 16)
                        sp.sem_inc(S["pieces_in"], 1)
                        sp.wait_ge(S["down"], end * 2 + half + 1)
                        load_down(e, half)
                    sp.wait_ge(S[f"bias_in{slot}"], i * 16 + 16)
                    sp.sem_inc(S["pieces_in"], 1)
                    sp.wait_ge(S["down_bias_in"], e * 16)
                    sp.sem_inc(S["pieces_in"], 1)
                    sp.wait_ge(S["y"], end + 1)
                    load_down_bias(e)
                    load_bias(later, slot)
            end = blocks_to(sp, NE - 2)
            for half in range(2):
                sp.wait_ge(S[f"down_in{half}"], 16 * (NE - 1))
                sp.wait_ge(S["down"], end * 2 + half + 1)
                load_down(NE - 1, half)
            sp.wait_ge(S["down_bias_in"], 16 * (NE - 1))
            sp.wait_ge(S["y"], end + 1)
            load_down_bias(NE - 1)
            sp.wait_ge(S["blank"], 1)
            units = units_in_all(sp)
            z = blank[:, :]
            with sp.Fori(0, NUNIT) as u:
                with sp.If(u >= units):
                    sp.dma_start(dram["y"][bass.ds(u * HALF, HALF), :].rearrange("r (a b) -> r a b", b=P),
                                 bass.AP(z.tensor, z.offset, [z.ap[0], [0, D // P], [1, P]])).then_inc(S["blank_out"], 16)
                with sp.Else():
                    sp.sem_inc(S["blank_out"], 16)
            sp.wait_ge(S["blank_out"], NUNIT * 16)
            for half in range(2):
                sp.wait_ge(S[f"down_in{half}"], 16 * NE)
            sp.wait_ge(S["down_bias_in"], 16 * NE)
            for slot in range(SLOTS):
                sp.wait_ge(S[f"bias_in{slot}"], 16 * (NE // 2))
                for q in range(4):
                    sp.wait_ge(gu_in[slot][q], 16 * (NE // 2))

        @block.gpsimd
        def _(pool):
            nc.gpsimd.memset(blank[:, :], 0.0).then_inc(S["blank"], 1)
            identity(nc, pool, ident, S["ident"])

            def gather(g, at):
                pool.dma_start(listed[:, :], dram["row_token"][bass.ds(at, P), :], allow_slow_non_contiguous=True).then_inc(S["list_in"], 16)
                pool.wait_ge(S["list_in"], g * 16 + 16)
                pool.sem_inc(S["lists"], 1)
                pool.wait_ge(S["x_turned"], g + 1)
                pool.sem_inc(S["lists"], 1)
                nc.gpsimd.tensor_copy(idx[:, :], listed[:, :]).then_inc(S["index"], 1)
                pool.wait_ge(S["index"], g + 1)
                pool.sem_inc(S["gathers"], 1)
                pool.indirect_dma_start(out=xg[:, :], out_offset=None, in_=dram["h2"],
                                        in_offset=bass.IndirectOffsetOnAxis(ap=idx[:, 0:1], axis=0)).then_inc(S["rows_in"], 16)

            with pool.Fori(0, NE) as e:
                units = pool.value_load(table[0:1, 0, bass.ds(e, 1)], min_val=0, max_val=2 * BPE)
                first = pool.value_load(table[0:1, 3, bass.ds(e, 1)], min_val=0, max_val=NBLK)
                with pool.Fori(0, BPE) as b:
                    with pool.If(b * 2 < units):
                        gather(pool.snap(first + b), pool.snap(e * T + b * P))
            gather(blocks_to(pool, NE - 1), 0)

        @block.tensor
        def _(pe):
            pe.sem_inc(S["gate_up"], 4)
            pe.sem_inc(S["down"], 2)
            pe.sem_inc(S["x_turned"], 1)
            pe.wait_ge(S["ident"], 2)

            def turn_rows():
                for k in range(KD):
                    last = nc.tensor.transpose(psT[:, k // 4, (k % 4) * P:(k % 4 + 1) * P], xg[:, k * P:(k + 1) * P], ident[:, :])
                last.then_inc(S["x_turned"], 1)

            def turn_activations(half, g):
                pe.wait_ge(S["act"], g * 2 + half + 1)
                for k in range(4):
                    last = nc.tensor.transpose(psG[:, half, k * P:(k + 1) * P], gated[:, half, k * P:(k + 1) * P], ident[:, :])
                last.then_inc(S["act_turned"], 1)

            def multiply_down(half, n):
                for k in range(4):
                    last = nc.tensor.matmul(psD[:, n, :], actT[:, 4 * half + k, :], down[:, half, k, n * 512:(n + 1) * 512],
                                            start=(half == 0 and k == 0), stop=(half == 1 and k == 3))
                return last

            def one_block(i, slot, g):
                pe.wait_ge(S["xT"], g + 1)
                for q in range(4):
                    pe.wait_ge(gu_in[slot][q], i * 16 + 16)
                    for k in range(KD):
                        last = nc.tensor.matmul(psG[:, q, :], xT[:, k, :], gu[slot][:, q, k, :], start=(k == 0), stop=(k == KD - 1))
                    last.then_inc(S["gate_up"], 1)
                turn_activations(0, g)
                pe.wait_ge(S["rows_in"], g * 16 + 32)
                turn_rows()
                pe.wait_ge(S["actT"], g * 2 + 1)
                pe.wait_ge(S["down_in0"], i * 32 + 16 * (slot + 1))
                pe.wait_ge(S["y"], g + 1)
                multiply_down(0, 0)
                turn_activations(1, g)
                multiply_down(0, 1).then_inc(S["down"], 1)
                pe.wait_ge(S["actT"], g * 2 + 2)
                pe.wait_ge(S["down_in1"], i * 32 + 16 * (slot + 1))
                multiply_down(1, 0)
                multiply_down(1, 1).then_inc(S["down"], 1)

            def half_block(i, slot, g):
                pe.wait_ge(S["xT"], g + 1)
                for what in range(2):
                    for half in range(2):
                        pe.wait_ge(gu_in[slot][2 * half + what], i * 16 + 16)
                    for k in range(KD):
                        for half in range(2):
                            last = nc.tensor.matmul(psG[half * HALF:(half + 1) * HALF, what, :], xT[:, k, 0:HALF],
                                                    gu[slot][:, 2 * half + what, k, :], start=(k == 0), stop=(k == KD - 1))
                    last.then_inc(S["gate_up"], 1 if what == 0 else 3)
                pe.wait_ge(S["rows_in"], g * 16 + 32)
                turn_rows()
                for part in range(2):
                    pe.wait_ge(S["act"], g * 2 + 1 + part)
                    for k in (2 * part, 2 * part + 1):
                        last = nc.tensor.transpose(psG[:, 2 + part, (k % 2) * P:(k % 2 + 1) * P], gated[:, 0, k * P:(k + 1) * P], ident[:, :])
                    last.then_inc(S["act_turned"], 1)
                for half in range(2):
                    pe.wait_ge(S[f"down_in{half}"], i * 32 + 16 * (slot + 1))
                pe.wait_ge(S["y"], g + 1)
                for k in range(4):
                    if k % 2 == 0:
                        pe.wait_ge(S["actT"], g * 2 + 1 + k // 2)
                    for half in range(2):
                        for n in range(2):
                            last = nc.tensor.matmul(psD[n * HALF:(n + 1) * HALF, 0, :], actT[:, k, half * HALF:(half + 1) * HALF],
                                                    down[:, half, k, n * 512:(n + 1) * 512], start=(half == 0 and k == 0),
                                                    stop=(half == 1 and k == 3))
                last.then_inc(S["down"], 2)

            pe.wait_ge(S["rows_in"], 16)
            turn_rows()
            each_block(pe, one_block, half_block)

        @block.scalar
        def _(act):
            act.sem_inc(S["y_out"], 32)

            def move_rows():
                nc.scalar.copy(xT[:, :, :].rearrange("p k t -> p (k t)"), psT[:, :, :].rearrange("p a b -> p (a b)")).then_inc(S["xT"], 1)

            def move_activations(half, g):
                act.wait_ge(S["act_turned"], g * 2 + half + 1)
                nc.scalar.copy(actT[:, 4 * half:4 * half + 4, :].rearrange("p k t -> p (k t)"), psG[:, half, :]).then_inc(S["actT"], 1)

            act.wait_ge(S["x_turned"], 2)
            move_rows()

            def one_block(i, slot, g, unit):
                for half in range(2):
                    act.wait_ge(S["gate_ready"], g * 2 + half + 1)
                    nc.scalar.activation(sig[:, half, :], gated[:, half, :], ACT.Sigmoid, scale=ALPHA).then_inc(S["sig"], 1)
                move_activations(0, g)
                act.wait_ge(S["x_turned"], g + 3)
                move_rows()
                move_activations(1, g)
                act.wait_ge(S["y"], g + 2)
                unit = nc.s_assert_within(unit, 0, NUNIT - 2)
                for rows in range(2):
                    act.dma_start(dram["y"][bass.ds(unit * HALF + rows * HALF, HALF), :],
                                  yrow[rows * HALF:(rows + 1) * HALF, :]).then_inc(S["y_out"], 16)

            def half_block(i, slot, g, unit):
                act.wait_ge(S["gate_ready"], g * 2 + 2)
                nc.scalar.activation(sig[:, 0, :], gated[:, 0, :], ACT.Sigmoid, scale=ALPHA).then_inc(S["sig"], 2)
                act.wait_ge(S["x_turned"], g + 3)
                move_rows()
                for part in range(2):
                    act.wait_ge(S["act_turned"], g * 2 + 1 + part)
                    nc.scalar.copy(actT[:, 2 * part:2 * part + 2, :].rearrange("p k t -> p (k t)"),
                                   psG[:, 2 + part, 0:2 * P]).then_inc(S["actT"], 1)
                act.wait_ge(S["y"], g + 2)
                for n in range(2):
                    act.dma_start(dram["y"][bass.ds(unit * HALF, HALF), n * 512:(n + 1) * 512],
                                  yrow[n * HALF:(n + 1) * HALF, 0:512]).then_inc(S["y_out"], 16)

            each_block(act, one_block, half_block, rows=True)
            act.wait_ge(S["y_out"], blocks_to(act, NE - 1) * 32 + 32)
            act.sem_inc(S["stored"], 1)

        @block.vector
        def _(dve):
            STEPS = 12
            dve.sem_inc(S["y"], 1)

            def counted(g):
                done = [0]

                def link(ins, by=1):
                    done[0] += by
                    ins.then_inc(S["vec"], by)
                    dve.wait_ge(S["vec"], g * STEPS + done[0])
                    assert done[0] <= STEPS

                return link

            def one_block(i, slot, g):
                brow, link = bias[slot], counted(g)
                dve.wait_ge(S[f"bias_in{slot}"], i * 16 + 16)
                for half in range(2):
                    c = half * 512
                    dve.wait_ge(S["gate_up"], g * 4 + 4 + 2 * half + 1)
                    link(nc.vector.tensor_tensor(gated[:, half, :], psG[:, 2 * half, :], brow[:, c:c + 512], ALU.add))
                    link(nc.vector.tensor_scalar(gated[:, half, :], gated[:, half, :], LIMIT, None, ALU.min))
                    dve.sem_inc(S["gate_ready"], 1)
                    dve.wait_ge(S["sig"], g * 2 + half + 1)
                    link(nc.vector.tensor_tensor(gated[:, half, :], gated[:, half, :], sig[:, half, :], ALU.mult))
                    dve.wait_ge(S["gate_up"], g * 4 + 4 + 2 * half + 2)
                    link(nc.vector.tensor_tensor(up[:, :], psG[:, 2 * half + 1, :], brow[:, DE + c:DE + c + 512], ALU.add))
                    link(nc.vector.tensor_scalar(up[:, :], up[:, :], LIMIT, -LIMIT, ALU.min, ALU.max))
                    link(nc.vector.scalar_tensor_tensor(gated[:, half, :], up[:, :], 1.0, gated[:, half, :], ALU.add, ALU.mult))
                    dve.sem_inc(S["act"], 1)
                dve.wait_ge(S["down_bias_in"], i * 32 + 16 * (slot + 1))
                dve.wait_ge(S["down"], g * 2 + 4)
                dve.wait_ge(S["y_out"], g * 32 + 32)
                nc.vector.tensor_tensor(yrow[:, :], psD[:, :, :].rearrange("p a b -> p (a b)"), down_bias[:, :], ALU.add).then_inc(S["y"], 1)

            def half_block(i, slot, g):
                brow, link = bias[slot], counted(g)

                def add_bias(out, ps, row, at):
                    for half in range(2):
                        part = slice(half * HALF, (half + 1) * HALF)
                        c = at + half * 512
                        last = nc.vector.tensor_tensor(out[part, :], ps[part, :], row[part, c:c + 512], ALU.add)
                    return last

                dve.wait_ge(S[f"bias_in{slot}"], i * 16 + 16)
                dve.wait_ge(S["gate_up"], g * 4 + 4 + 1)
                link(add_bias(gated[:, 0, :], psG[:, 0, :], brow, 0))
                link(nc.vector.tensor_scalar(gated[:, 0, :], gated[:, 0, :], LIMIT, None, ALU.min))
                dve.sem_inc(S["gate_ready"], 2)
                dve.wait_ge(S["sig"], g * 2 + 2)
                link(nc.vector.tensor_tensor(gated[:, 0, :], gated[:, 0, :], sig[:, 0, :], ALU.mult))
                dve.wait_ge(S["gate_up"], g * 4 + 4 + 4)
                link(add_bias(up[:, :], psG[:, 1, :], brow, DE))
                link(nc.vector.tensor_scalar(up[:, :], up[:, :], LIMIT, -LIMIT, ALU.min, ALU.max))
                for part in range(2):
                    c = slice(part * 256, (part + 1) * 256)
                    link(nc.vector.scalar_tensor_tensor(gated[:, 0, c], up[:, c], 1.0, gated[:, 0, c], ALU.add, ALU.mult),
                         1 if part == 0 else STEPS - 6)
                    dve.sem_inc(S["act"], 1)
                dve.wait_ge(S["down_bias_in"], i * 32 + 16 * (slot + 1))
                dve.wait_ge(S["down"], g * 2 + 4)
                dve.wait_ge(S["y_out"], g * 32 + 32)
                add_bias(yrow[:, 0:512], psD[:, 0, :], down_bias, 0).then_inc(S["y"], 1)

            each_block(dve, one_block, half_block)


def phase_combine(nc, kit, keep, io, dram, out):
    scope = ExitStack()
    with scope:
        dest, gate = keep["dest"], keep["gate"]
        rows = kit.sb(scope, "g2_row", [P, D])
        yk = kit.sb(scope, "y_of_token", [P, NT, TOPK, D])
        x1 = kit.sb(scope, "x1_again", [P, 2, D])
        f = kit.sb(scope, "ffn_sum", [P, 2, D])
        sq = kit.sb(scope, "ffn_squares", [P, 2, D])
        o = kit.sb(scope, "out_tile", [P, 2, D])
        st = kit.sb(scope, "ffn_stat", [P, NT, 2])
        eps = kit.sb(scope, "eps_g", [P, 1])
        S = {n: kit.sem("g_" + n) for n in ("row_in", "eps", "x_in0", "x_in1", "vec", "summed", "sq", "std", "ready",
                                            "out0", "out1")}
        y_in = [kit.sem(f"g_y_in{t}") for t in range(NT)]
        block = scope.enter_context(nc.Block())

        @block.sync
        def _(sp):
            sp.dma_start(rows[:, :], row_of(dram["vectors"], D, 3 * D)).then_inc(S["row_in"], 16)
            for t in range(NT):
                if t >= 2:
                    sp.wait_ge(S["ready"], t - 1)
                sp.dma_start(x1[:, t % 2, :], dram["x1"][t * P:(t + 1) * P, :]).then_inc(S[f"x_in{t % 2}"], 16)

        @block.gpsimd
        def _(pool):
            nc.gpsimd.memset(eps[:, :], EPS).then_inc(S["eps"], 1)
            for t in range(NT):
                for k in range(TOPK):
                    pool.indirect_dma_start(out=yk[:, t, k, :], out_offset=None, in_=dram["y"],
                                            in_offset=bass.IndirectOffsetOnAxis(ap=dest[:, t * TOPK + k:t * TOPK + k + 1], axis=0)
                                            ).then_inc(y_in[t], 16)

        @block.scalar
        def _(act):
            act.wait_ge(S["eps"], 1)

            def store(t):
                act.wait_ge(S["ready"], t + 1)
                act.dma_start(out[t * P:(t + 1) * P, :], o[:, t % 2, :]).then_inc(S[f"out{t % 2}"], 16)

            for t in range(NT):
                if t >= 1:
                    store(t - 1)
                act.wait_ge(S["summed"], t + 1)
                if t >= 2:
                    act.wait_ge(S["sq"], t - 1)
                nc.scalar.activation(sq[:, t % 2, :], f[:, t % 2, :], ACT.Square, accum_out=st[:, t, 0:1]).then_inc(S["sq"], 1)
                act.wait_ge(S["sq"], t + 1)
                nc.scalar.activation(st[:, t, 1:2], st[:, t, 0:1], ACT.Sqrt, bias=eps[:, 0:1], scale=1.0 / D).then_inc(S["std"], 1)
            store(NT - 1)
            for i in range(2):
                act.wait_ge(S[f"out{i}"], 16 * NT // 2)

        @block.vector
        def _(dve):
            link = linked(dve, S["vec"])
            dve.wait_ge(S["row_in"], 16)

            def weighed_sum(t):
                dve.wait_ge(y_in[t], 16 * TOPK)
                ft = f[:, t % 2, :]
                link(nc.vector.tensor_scalar(ft, yk[:, t, 0, :], gate[:, t * TOPK:t * TOPK + 1], None, ALU.mult))
                for k in range(1, TOPK):
                    link(nc.vector.scalar_tensor_tensor(ft, yk[:, t, k, :], gate[:, t * TOPK + k:t * TOPK + k + 1], ft, ALU.mult, ALU.add))
                dve.sem_inc(S["summed"], 1)

            def norm_and_add(t):
                dve.wait_ge(S["std"], t + 1)
                link(nc.vector.reciprocal(st[:, t, 1:2], st[:, t, 1:2]))
                if t >= 2:
                    dve.wait_ge(S[f"out{t % 2}"], 16 * (t // 2))
                link(nc.vector.scalar_tensor_tensor(o[:, t % 2, :], f[:, t % 2, :], st[:, t, 1:2], rows[:, :], ALU.mult, ALU.mult))
                dve.wait_ge(S[f"x_in{t % 2}"], 16 * (t // 2 + 1))
                nc.vector.tensor_tensor(o[:, t % 2, :], o[:, t % 2, :], x1[:, t % 2, :], ALU.add).then_inc(S["ready"], 1)

            for t in range(NT + 1):
                if t < NT:
                    weighed_sum(t)
                if t >= 1:
                    norm_and_add(t - 1)


def attention_constants():
    q = np.arange(GRID_W)
    lo = np.clip(q - NA_COLS // 2, 0, GRID_W - NA_COLS)
    inside = (q[None, :] >= lo[:, None]) & (q[None, :] < lo[:, None] + NA_COLS)
    m = np.where(inside, 0.0, MASKED).astype(np.float32)
    return {"na_col_mask": np.concatenate([m, m])}


def build_layer(nc, io, out):
    top = ExitStack()
    with top:
        kit = Kit(nc, top)
        dram = {
            "vectors": nc.dram_tensor("vectors_dram", [4 * D], F32, kind="Internal").ap(),
            "x1": nc.dram_tensor("x1_dram", [T, D], F32, kind="Internal").ap(),
            "h2": nc.dram_tensor("h2_dram", [T, D], F32, kind="Internal").ap(),
            "row_token": nc.dram_tensor("row_token_dram", [ROW_LIST, 1], I32, kind="Internal").ap(),
            "y": nc.dram_tensor("y_dram", [NROW, D], F32, kind="Internal").ap(),
        }
        keep = {"dest": kit.sb(top, "dest", [P, NT * TOPK], I32), "gate": kit.sb(top, "gate", [P, NT * TOPK]),
                "table": kit.sb(top, "table", [1, 4, NE], I32)}
        with ExitStack() as fed:
            with ExitStack() as mixed:
                keep["modT"] = kit.sb(mixed, "modT", [P, 6 * KD, 2])
                keep["hT"] = keep["mixT"] = kit.sb(mixed, "hT_mixT", [P, KD, TA])
                with ExitStack() as convolved:
                    keep["hyT"] = kit.sb(convolved, "hyT", [P, NHT, T])
                    with ExitStack() as scanned:
                        keep["xbcT"] = kit.sb(scanned, "xbcT", [P, NXT, TA])
                        keep["z"] = kit.sb(scanned, "z", [P, NT, SSD_W])
                        keep["dt"] = kit.sb(scanned, "dt", [P, NT + NTC, 2 * SSD_H])
                        with ExitStack() as attended:
                            keep["qT"] = kit.sb(attended, "qT", [P, NQT, T])
                            keep["kT"] = kit.sb(attended, "kT", [P, NQT, TA])
                            keep["v"] = kit.sb(attended, "v", [P, NT + NTC, NA_W])
                            phase_project(nc, kit, keep, io)
                            phase_attention(nc, kit, keep, io)
                        phase_ssd(nc, kit, keep, io)
                    kit.recycle()
                    phase_hyena(nc, kit, keep, io)
                weights = first_weights(kit, fed)
                phase_mix(nc, kit, keep, io, dram, weights)
            phase_experts(nc, kit, keep, weights, io, dram)
        phase_combine(nc, kit, keep, io, dram, out)


def lay_out(x, c, ctx, c_ctx, w_mod, b_mod, norm_g, w_in, ssd_conv_w, ssd_conv_b, ssd_a_log, ssd_dt_bias, ssd_d, ssd_norm_g, na_rpb,
            hy_conv_w, hy_conv_b, hy_f_w1, hy_f_b1, hy_f_w2, hy_f_b2, hy_f_w3, hy_freq, hy_d, w_out, w_router, b_router, w_gate_up,
            b_gate_up, w_down, b_down):
    def col(a):
        return a.reshape(-1, P).T

    def cols(a):
        return a.T.reshape(-1, P, a.shape[0]).transpose(1, 0, 2)

    rpb = np.zeros((NA_H, 2 * NA_ROWS + 1, 2 * GRID_W - 1), np.float32)
    rpb[:, 1:2 * NA_ROWS, GRID_W - NA_COLS:GRID_W + NA_COLS - 1] = na_rpb[0].transpose(2, 0, 1)
    skewed = np.stack([rpb[:, 1 - half:1 - half + 2 * NA_ROWS, GRID_W - 1 - qc:2 * GRID_W - 1 - qc]
                       for half in range(2) for qc in range(GRID_W)])
    g = norm_g[0]
    hy_b = np.stack([hy_f_b1[0], hy_f_b2[0]], -1)
    a = {
        "x": x[0], "x_t": x[0].T, "ctx_t": ctx[0].T, "w_mod": w_mod[0], "w_in": w_in[0],
        "c_col": np.stack([col(c[0]), col(c_ctx)], -1), "b_mod_col": col(b_mod[0]), "gain0_col": col(g[0]),
        "gains_col": g[1:].reshape(3, KD, P).transpose(2, 0, 1),
        "ssd_conv_col": cols(np.concatenate([ssd_conv_w[0], ssd_conv_b])),
        "hy_conv_col": cols(np.concatenate([hy_conv_w[0], hy_conv_b])),
        "rpb_skewed": skewed, "dt_bias": ssd_dt_bias[0].reshape(-1), "a_log": ssd_a_log[0].reshape(-1), "ssd_d": ssd_d[0],
        "ssd_norm_col": col(ssd_norm_g[0]),
        "hy_f_w1": hy_f_w1[0], "hy_f_w2": hy_f_w2[0], "hy_f_w3": hy_f_w3[0],
        "hy_bias_freq": np.stack([hy_b, hy_freq[0].T], -1), "hy_d": hy_d,
        "w_out": w_out[0], "w_router": w_router[0], "b_router": b_router[0], "w_gate_up": w_gate_up[0], "b_gate_up": b_gate_up[0],
        "w_down": w_down[0], "b_down": b_down[0],
    }
    return {**a, **hyena_constants(), **attention_constants()}


def kernel(**inputs):
    import concourse.bacc as bacc
    from concourse.bass_utils import run_bass_kernel_spmd

    nc = bacc.Bacc("TRN2", target_bir_lowering=False, num_devices=1)
    arrays, io = {}, {}
    for name, a in lay_out(**{k: np.asarray(v) for k, v in inputs.items()}).items():
        a = np.ascontiguousarray(a)
        arrays[f"in_{name}"] = a
        io[name] = nc.dram_tensor(f"in_{name}", a.shape, mybir.dt.from_np(a.dtype), kind="ExternalInput").ap()
    out = nc.dram_tensor("out_0", (1, T, D), F32, kind="ExternalOutput").ap()
    build_layer(nc, io, out[0])
    r = run_bass_kernel_spmd(nc, [arrays], core_ids=[0])
    return r.results[0]["out_0"]
```
